# Optimizing a Trainium2 kernel written in Bass

```python
import jax
import jax.numpy as jnp
from jax import lax
import numpy as np

D_MODEL = 2048
BATCH = 1
SEQ = 256
DEPTH = 1

GRID_W = 64
CTX_LEN = 256
N_MOD = 6
RMS_EPS = 1e-6
RWKV_HEAD = 64
RWKV_DIM = D_MODEL
RWKV_HEADS = RWKV_DIM // RWKV_HEAD
N_DIR = 2
DECAY_LORA = 96
ICLR_LORA = 96
GATE_LORA = 256
LNX_EPS = 64e-5
GMLP_DIM = D_MODEL // 2
CHUNK = 128
GMLP_GROUPS = 8
GMLP_GROUP_CH = GMLP_DIM // GMLP_GROUPS
LN_EPS = 1e-5
D_FF = 5632

OFF_K = RWKV_DIM
OFF_V = 2 * RWKV_DIM
OFF_DEC = 3 * RWKV_DIM
OFF_ICLR = OFF_DEC + N_DIR * DECAY_LORA
OFF_GATE = OFF_ICLR + N_DIR * ICLR_LORA
RWKV_COLS = OFF_GATE + GATE_LORA
OFF_GATES = RWKV_COLS + 2 * GMLP_DIM
IN_COLS = OFF_GATES + 2 * D_MODEL

kernel_name = "hybrid_rwkv7_chunkmlp_convffn_dit_layer"

def rmsnorm(x, g):
    xf = x.astype(jnp.float32)
    y = xf * lax.rsqrt(jnp.mean(xf * xf, axis=-1, keepdims=True) + RMS_EPS)
    return (y * g.astype(jnp.float32)).astype(x.dtype)

def dwconv1d(x, w):
    return lax.conv_general_dilated(x, w[:, None, :], window_strides=(1,), padding=((1, 1),),
                                    dimension_numbers=('NWC', 'WIO', 'NWC'),
                                    feature_group_count=x.shape[-1])

def dwconv2d_grid(x, w):
    B, T, C = x.shape
    rows = T // GRID_W
    y = lax.conv_general_dilated(x.reshape(B, rows, GRID_W, C), w[:, :, None, :],
                                 window_strides=(1, 1), padding=((1, 1), (1, 1)),
                                 dimension_numbers=('NHWC', 'HWIO', 'NHWC'),
                                 feature_group_count=C)
    return y.reshape(B, T, C)

def rwkv_terms(slab, w0, w_decay_up, a0, w_iclr_up, w_gate_up, k_k, k_a):
    f32 = jnp.float32
    B, T, _ = slab.shape
    r, k, v, dec, iclr, gate = jnp.split(slab, [OFF_K, OFF_V, OFF_DEC, OFF_ICLR, OFF_GATE], axis=-1)
    dec = dec.reshape(B, T, N_DIR, DECAY_LORA)
    iclr = iclr.reshape(B, T, N_DIR, ICLR_LORA)
    w_pre = (w0 + jnp.einsum('btdr,drc->btdc', jnp.tanh(dec), w_decay_up)).astype(f32)
    decay = jnp.exp(-jnp.exp(-jax.nn.softplus(-w_pre) - 0.5))
    a = jax.nn.sigmoid((a0 + jnp.einsum('btdr,drc->btdc', iclr, w_iclr_up)).astype(f32))
    g = jax.nn.sigmoid(gate) @ w_gate_up
    kk = (k * k_k).astype(f32).reshape(B, T, RWKV_HEADS, RWKV_HEAD)
    kk = kk * lax.rsqrt(jnp.maximum(jnp.sum(kk * kk, axis=-1, keepdims=True), 1e-24))
    k_dir = k.astype(f32)[:, :, None, :] * (1.0 + (a - 1.0) * k_a.astype(f32))
    heads = lambda z: z.reshape(*z.shape[:-1], RWKV_HEADS, RWKV_HEAD)
    a_h = heads(a)
    return (heads(r.astype(f32)), heads(k_dir), heads(v.astype(f32)), kk, heads(decay),
            kk[:, :, None] * a_h, g)

def wkv_scan(s0, r, w, k, v, kk, b, reverse):
    tm = lambda z: jnp.moveaxis(z, 1, 0)

    def step(S, inp):
        r_t, w_t, k_t, v_t, kk_t, b_t = inp
        sa = jnp.einsum('bhij,bhj->bhi', S, kk_t)
        S = S * w_t[:, :, None, :] - sa[..., None] * b_t[:, :, None, :] + v_t[..., None] * k_t[:, :, None, :]
        return S, jnp.einsum('bhij,bhj->bhi', S, r_t)

    s_final, ys = lax.scan(step, s0, (tm(r), tm(w), tm(k), tm(v), tm(kk), tm(b)), reverse=reverse)
    return s_final, jnp.moveaxis(ys, 0, 1)

def dir_inputs(terms, d):
    r, k_dir, v, kk, decay, b, _ = terms
    return r, decay[:, :, d], k_dir[:, :, d], v, kk, b[:, :, d]

def rwkv_readout(y, terms, r_k, lnx_g, lnx_b, dtype):
    r, k_dir, v, _, _, _, g = terms
    B, T = y.shape[:2]
    mu = jnp.mean(y, axis=-1, keepdims=True)
    var = jnp.mean(jnp.square(y - mu), axis=-1, keepdims=True)
    yn = ((y - mu) * lax.rsqrt(var + LNX_EPS)).reshape(B, T, RWKV_DIM) * lnx_g + lnx_b
    bonus = jnp.sum(r[:, :, None] * k_dir * r_k, axis=(2, 4))[..., None] * v
    return ((yn + bonus.reshape(B, T, RWKV_DIM)) * g).astype(dtype)

def rwkv_mixer(slab_x, slab_c, w0, w_decay_up, a0, w_iclr_up, w_gate_up, k_k, k_a, r_k,
               lnx_g, lnx_b, need_ctx):
    tx = rwkv_terms(slab_x, w0, w_decay_up, a0, w_iclr_up, w_gate_up, k_k, k_a)
    tc = rwkv_terms(slab_c, w0, w_decay_up, a0, w_iclr_up, w_gate_up, k_k, k_a)
    B = slab_x.shape[0]
    ys_x, ys_c = [], []
    for d in range(N_DIR):
        s0 = jnp.zeros((B, RWKV_HEADS, RWKV_HEAD, RWKV_HEAD), jnp.float32)
        s_ctx, yc = wkv_scan(s0, *dir_inputs(tc, d), reverse=(d == 1))
        _, yx = wkv_scan(s_ctx, *dir_inputs(tx, d), reverse=(d == 1))
        ys_x.append(yx)
        ys_c.append(yc)
    out_x = rwkv_readout(ys_x[0] + ys_x[1], tx, r_k, lnx_g, lnx_b, slab_x.dtype)
    out_c = rwkv_readout(ys_c[0] + ys_c[1], tc, r_k, lnx_g, lnx_b, slab_c.dtype) if need_ctx else None
    return out_x, out_c

def chunk_mlp(uv, ln_v_g, ln_v_b, w_spatial, b_spatial):
    z = jax.nn.gelu(uv, approximate=False)
    u, v = jnp.split(z, 2, axis=-1)
    B, T, _ = v.shape
    vf = v.astype(jnp.float32)
    mu = jnp.mean(vf, axis=-1, keepdims=True)
    var = jnp.mean(jnp.square(vf - mu), axis=-1, keepdims=True)
    v = ((vf - mu) * lax.rsqrt(var + LN_EPS) * ln_v_g + ln_v_b).astype(u.dtype)
    v = v.reshape(B, T // CHUNK, CHUNK, GMLP_GROUPS, GMLP_GROUP_CH)
    s = jnp.einsum('gpq,bnqgc->bnpgc', w_spatial, v) + b_spatial.T[None, None, :, :, None]
    return u * s.reshape(B, T, GMLP_DIM)

def merge_branches(p, y_rwkv, ln_v_g, ln_v_b, w_spatial, b_spatial, w_proj_a, w_proj_b, w_out):
    y_gmlp = chunk_mlp(p[..., RWKV_COLS:OFF_GATES], ln_v_g, ln_v_b, w_spatial, b_spatial)
    gate_a, gate_b = jnp.split(p[..., OFF_GATES:], 2, axis=-1)
    m = jax.nn.sigmoid(gate_a) * (y_rwkv @ w_proj_a) + jax.nn.sigmoid(gate_b) * (y_gmlp @ w_proj_b)
    return m @ w_out

def conv_glu_ffn(h, w_up, conv_w, w_down, grid):
    up = h @ w_up
    up = dwconv2d_grid(up, conv_w) if grid else dwconv1d(up, conv_w[1])
    a, b = jnp.split(up, 2, axis=-1)
    return (jax.nn.silu(a) * b) @ w_down

def trunk_layer(x, ctx, c, c_ctx, w_mod, b_mod, g_pre1, g_post1, g_pre2, g_post2, w_in, conv_rwkv,
                w0, w_decay_up, a0, w_iclr_up, w_gate_up, k_k, k_a, r_k, lnx_g, lnx_b,
                ln_v_g, ln_v_b, w_spatial, b_spatial, w_proj_a, w_proj_b, w_out,
                w_up, conv_ffn, w_down, need_ctx):
    mod = jax.nn.silu(c) @ w_mod + b_mod
    mod_c = jax.nn.silu(c_ctx) @ w_mod + b_mod
    sh1, sc1, gt1, sh2, sc2, gt2 = jnp.split(mod[:, None, :], N_MOD, axis=-1)
    csh1, csc1, cgt1, csh2, csc2, cgt2 = jnp.split(mod_c, N_MOD, axis=-1)

    h = rmsnorm(x, g_pre1) * (1.0 + sc1) + sh1
    hc = rmsnorm(ctx, g_pre1) * (1.0 + csc1) + csh1
    p = h @ w_in
    pc = hc @ (w_in if need_ctx else w_in[:, :RWKV_COLS])
    y_rwkv, yc_rwkv = rwkv_mixer(dwconv1d(p[..., :RWKV_COLS], conv_rwkv),
                                 dwconv1d(pc[..., :RWKV_COLS], conv_rwkv),
                                 w0, w_decay_up, a0, w_iclr_up, w_gate_up, k_k, k_a, r_k,
                                 lnx_g, lnx_b, need_ctx)
    mix = merge_branches(p, y_rwkv, ln_v_g, ln_v_b, w_spatial, b_spatial, w_proj_a, w_proj_b, w_out)
    x = x + gt1 * rmsnorm(mix, g_post1)

    h2 = rmsnorm(x, g_pre2) * (1.0 + sc2) + sh2
    x = x + gt2 * rmsnorm(conv_glu_ffn(h2, w_up, conv_ffn, w_down, grid=True), g_post2)

    if need_ctx:
        mix_c = merge_branches(pc, yc_rwkv, ln_v_g, ln_v_b, w_spatial, b_spatial, w_proj_a, w_proj_b, w_out)
        ctx = ctx + cgt1 * rmsnorm(mix_c, g_post1)
        h2c = rmsnorm(ctx, g_pre2) * (1.0 + csc2) + csh2
        ctx = ctx + cgt2 * rmsnorm(conv_glu_ffn(h2c, w_up, conv_ffn, w_down, grid=False), g_post2)
    return x, ctx

def setup_inputs(seed: int = 0) -> dict:
    key = jax.random.key(seed)
    ks = iter(jax.random.split(key, 40))
    L = DEPTH
    f32 = jnp.float32

    def nrm(shape, scale):
        return jax.random.normal(next(ks), shape, f32) * scale

    def gain(shape):
        return 1.0 + nrm(shape, 0.05)

    conv_base = jnp.array([0.3, 1.0, 0.3], f32)[None, :, None]
    ffn_base = jnp.zeros((3, 3), f32).at[1, 1].set(1.0)[None, :, :, None]
    return {
        "x": nrm((BATCH, SEQ, D_MODEL), 1.0),
        "c": nrm((BATCH, D_MODEL), 1.0),
        "ctx": nrm((BATCH, CTX_LEN, D_MODEL), 1.0),
        "c_ctx": nrm((D_MODEL,), 1.0),
        "w_mod": nrm((L, D_MODEL, N_MOD * D_MODEL), 0.5 * D_MODEL ** -0.5),
        "b_mod": nrm((L, N_MOD * D_MODEL), 0.01),
        "g_pre1": gain((L, D_MODEL)),
        "g_post1": gain((L, D_MODEL)),
        "g_pre2": gain((L, D_MODEL)),
        "g_post2": gain((L, D_MODEL)),
        "w_in": nrm((L, D_MODEL, IN_COLS), D_MODEL ** -0.5),
        "conv_rwkv": conv_base + nrm((L, 3, RWKV_COLS), 0.05),
        "w0": jax.random.uniform(next(ks), (L, N_DIR, RWKV_DIM), f32, -6.0, -1.0),
        "w_decay_up": nrm((L, N_DIR, DECAY_LORA, RWKV_DIM), 0.5 * DECAY_LORA ** -0.5),
        "a0": nrm((L, N_DIR, RWKV_DIM), 0.5),
        "w_iclr_up": nrm((L, N_DIR, ICLR_LORA, RWKV_DIM), 0.5 * ICLR_LORA ** -0.5),
        "w_gate_up": nrm((L, GATE_LORA, RWKV_DIM), GATE_LORA ** -0.5),
        "k_k": 0.85 + nrm((L, RWKV_DIM), 0.05),
        "k_a": gain((L, RWKV_DIM)),
        "r_k": nrm((L, RWKV_HEADS, RWKV_HEAD), 0.1),
        "lnx_g": gain((L, RWKV_DIM)),
        "lnx_b": nrm((L, RWKV_DIM), 0.01),
        "ln_v_g": gain((L, GMLP_DIM)),
        "ln_v_b": nrm((L, GMLP_DIM), 0.01),
        "w_spatial": nrm((L, GMLP_GROUPS, CHUNK, CHUNK), CHUNK ** -0.5),
        "b_spatial": gain((L, GMLP_GROUPS, CHUNK)),
        "w_proj_a": nrm((L, RWKV_DIM, D_MODEL), RWKV_DIM ** -0.5),
        "w_proj_b": nrm((L, GMLP_DIM, D_MODEL), GMLP_DIM ** -0.5),
        "w_out": nrm((L, D_MODEL, D_MODEL), D_MODEL ** -0.5),
        "w_up": nrm((L, D_MODEL, 2 * D_FF), D_MODEL ** -0.5),
        "conv_ffn": ffn_base + nrm((L, 3, 3, 2 * D_FF), 0.2),
        "w_down": nrm((L, D_FF, D_MODEL), D_FF ** -0.5),
    }

def reference(x, c, ctx, c_ctx, w_mod, b_mod, g_pre1, g_post1, g_pre2, g_post2, w_in, conv_rwkv,
              w0, w_decay_up, a0, w_iclr_up, w_gate_up, k_k, k_a, r_k, lnx_g, lnx_b,
              ln_v_g, ln_v_b, w_spatial, b_spatial, w_proj_a, w_proj_b, w_out,
              w_up, conv_ffn, w_down):
    for l in range(DEPTH):
        x, ctx = trunk_layer(x, ctx, c, c_ctx, w_mod[l], b_mod[l], g_pre1[l], g_post1[l], g_pre2[l],
                             g_post2[l], w_in[l], conv_rwkv[l], w0[l], w_decay_up[l], a0[l],
                             w_iclr_up[l], w_gate_up[l], k_k[l], k_a[l], r_k[l], lnx_g[l], lnx_b[l],
                             ln_v_g[l], ln_v_b[l], w_spatial[l], b_spatial[l], w_proj_a[l],
                             w_proj_b[l], w_out[l], w_up[l], conv_ffn[l], w_down[l],
                             need_ctx=(l < DEPTH - 1))
    return x


_drawn_inputs = setup_inputs


def setup_inputs(seed=0):
    import zlib

    import numpy as np

    out = dict(_drawn_inputs(seed))
    spreads = {}
    factors = {'b_mod': 3.488,
     'g_post1': 3.489,
     'g_pre2': 2.855,
     'g_post2': 3.787,
     'w_decay_up': 8.0,
     'k_k': 12.096,
     'k_a': 3.136,
     'lnx_g': 8.0,
     'lnx_b': 64.0,
     'ln_v_g': 7.285,
     'ln_v_b': 64.0,
     'b_spatial': 7.493}
    for name, (base, spread) in spreads.items():
        noise = np.random.default_rng([zlib.crc32(name.encode()), seed]).standard_normal(out[name].shape)
        drawn = base * np.exp(spread * noise) if base else spread * noise
        out[name] = jnp.asarray(drawn.astype(out[name].dtype))
    for name, factor in factors.items():
        out[name] = (out[name] * factor).astype(out[name].dtype)
    return out
```

```python
from contextlib import ExitStack

import numpy as np
import concourse.bass as bass
from concourse import mybir

F32 = mybir.dt.float32
ALU = mybir.AluOpType
ACT = mybir.ActivationFunctionType

P = 128
D = 2048
KT = D // P
T = 256
TT = 512
HEAD = 64
C = 64
NCH = TT // C
PAIRS = D // P
LORA = 96
G = 1024
GG = G // P
FF = 5632
FT = FF // P
GRID = 64
ROWS = T // GRID
NMOD = 6 * KT
REG = KT * P
LEVELS = 6
DECAY_C = float(np.exp(-0.5))
NCONST = 13
RMS_EPS = 1e-6
LNX_EPS = 64e-5
LN_EPS = 1e-5
KK_MIN = 1e-24
LN_SHIFT = 20

PK, PR, PV, PW0, PA0, PKK, PKA, PRK, PLG, PLB, PNW0, PNA0, POKA = 0, 3, 6, 9, 11, 13, 14, 15, 16, 17, 18, 20, 22
NPAR = 18
NPARX = 24
PAIR_STEPS = 68

PHASES = [("mod", (8, 8, 8, 8)), ("lora", (2, 2, 1, 1)), ("pair", (PAIRS, PAIRS, PAIRS, 4 * PAIRS)),
          ("gv", (2, 2, 2, 2)), ("gu", (2, 2, 2, 2)), ("merge", (KT,) * 4), ("out", (4,) * 4),
          ("up", (FT // 2,) * 4), ("down", (KT,) * 4)]


def loads_before(phase):
    total = [0, 0, 0, 0]
    for name, n in PHASES:
        if name == phase:
            return total
        total = [a + b for a, b in zip(total, n)]
    raise ValueError(phase)


def layer_kernel(nc, io):
    ctx = ExitStack()
    with ctx:
        def sb(name, *shape):
            return ctx.enter_context(nc.sbuf_tensor(name, list(shape), F32))

        def bank(name):
            return ctx.enter_context(nc.psum_tensor(name, [P, 512], F32))

        def sem(name):
            return ctx.enter_context(nc.semaphore(name))

        ring = sb("ring", P, 4, REG)
        hT = sb("hT", P, KT, TT)
        arena = sb("arena", P, 27000)
        yr = sb("yr", P, KT, T)
        ident = sb("ident", P, P)
        ones = sb("ones", P, P)
        blk = sb("blk", P, P)
        score_mask = sb("score_mask", P, 2, P)
        off_mask = sb("off_mask", P, 2, LEVELS, C)
        eye2 = sb("eye2", P, C)
        scan_mask = sb("scan_mask", P, TT)
        modT = sb("modT", P, NMOD, 2)
        bmod = sb("bmod", P, NMOD)
        gains = sb("gains", P, 4, KT)
        scal = sb("scal", P, 8)
        cvec = sb("cvec", P, KT, 2)
        csil = sb("csil", P, KT, 2)
        params = sb("params", P, PAIRS, NPAR)
        paramx = sb("paramx", P, PAIRS, NPARX)
        par_a = sb("par_a", P, NPARX)
        par_v = sb("par_v", P, NPARX)
        conv_lora = sb("conv_lora", P, 6, 3)
        rstd = sb("rstd", P, TT)
        gcol = sb("gcol", P, KT, 2)

        used = [0]

        def view(*shape):
            n = int(np.prod(shape))
            v = arena[:, used[0]:used[0] + n]
            used[0] += n
            assert used[0] <= 27000, used
            if len(shape) == 1:
                return v
            names = "abcd"[:len(shape)]
            return v.rearrange("p (" + " ".join(names) + ") -> p " + " ".join(names),
                               **{k: s for k, s in zip(names, shape)})

        lora_act = view(6, TT)
        lora_w = view(6, P)
        kx, rx, vx, kkx = view(TT), view(TT), view(TT), view(TT)
        tmp = view(TT)
        tmp2 = view(TT)
        ew = [view(TT) for _ in range(2)]
        ea = [view(TT) for _ in range(2)]
        cumP = [view(TT) for _ in range(2)]
        cumG = [view(TT) for _ in range(2)]
        eInEx = [view(2, TT) for _ in range(2)]
        eIn = [eInEx[d][:, 0] for d in range(2)]
        eEx = [eInEx[d][:, 1] for d in range(2)]
        eNeg = [view(TT) for _ in range(2)]
        wc = [view(NCH) for _ in range(2)]
        kdir = [view(TT) for _ in range(2)]
        X = view(NCH, 2, C)
        KR = [view(NCH, 2, C) for _ in range(2)]
        SC = [[view(NCH, 2, C) for _ in range(2)] for _ in range(2)]
        NL = [v.rearrange("p (c t) -> p c t", t=C) for v in cumG]
        ZU = [v.rearrange("p (c t) -> p c t", t=C) for v in cumP]
        ZL = [v.rearrange("p (c t) -> p c t", t=C) for v in eNeg]
        TU = [v.rearrange("p (c t) -> p c t", t=C) for v in ew]
        XT = [v.rearrange("p a (c t) -> p (a c) t", t=P) for v in eInEx]
        VU = [view(NCH, 2, C) for _ in range(2)]
        gT = view(T)
        yd = [view(T) for _ in range(2)]
        rhs_sb = [view(C) for _ in range(2)]
        ST = [[view(HEAD) for _ in range(2)] for _ in range(2)]
        STw = [view(HEAD) for _ in range(2)]
        ra, rb, rc = view(T), view(T), view(T)
        x_sq = arena[:, 8192:8192 + KT * TT].rearrange("p (a b) -> p a b", a=KT)
        used[0] = 0
        yg = view(GG, T)
        vg = view(2, G)
        vrow = view(2, G)
        bsp = view(GG, P)
        wsp = view(GG, P)
        bn = view(2, 2, 6)
        mv = view(2, 2)
        vrs = view(2)
        ug = [view(T) for _ in range(2)]
        vcur = [view(2, P) for _ in range(2)]
        ssp = [view(T) for _ in range(2)]
        sga, sgb = view(T), view(T)
        mta, mtb = view(T), view(T)
        used[0] = 0
        xT = view(KT, T)
        mixT = view(KT, T)
        sq = view(KT, T)
        used[0] = 2 * KT * T
        ffT = view(FT, T)
        convw = view(4, 9)
        cv = [view(T) for _ in range(4)]
        sil = [view(T) for _ in range(2)]
        mT = arena[:, 22000:22000 + KT * T].rearrange("p (a b) -> p a b", a=KT)
        h2T = hT[:, :, T:TT]

        PB = [bank("PB0"), bank("PB1")]
        CH = [bank("CH0"), bank("CH1")]
        Q = [bank(f"Q{n}") for n in range(4)]

        loaded = [sem(f"region{r}_loaded") for r in range(4)]
        used = [sem(f"region{r}_used") for r in range(4)]
        consts_ld = sem("consts_loaded")
        x_ld = sem("x_loaded")
        seen = sem("waits_seen")
        act_step = sem("scalar_steps")
        dve_step = sem("vector_steps")
        phase_v = sem("vector_phase_done")
        cexp_rdy = sem("exp_c_ready")
        csil_rdy = sem("silu_c_ready")
        par_rdy = sem("parameters_ready")
        mod_sbd = sem("mod_tile_evacuated")
        sq_rdy = sem("squares_ready")
        ssq_ps = sem("square_sums_done")
        rstd_rdy = sem("rstd_ready")
        h_rdy = sem("h_ready")
        lo_mid = sem("lora_centre_tap_done")
        lo_cv = sem("lora_conv_done")
        lo_act = sem("lora_act_ready")
        lw_ld = sem("lora_up_loaded")
        pair_done = sem("pair_done")
        proj_ps = sem("projection_done")
        pb_free = [sem("proj_bank0_free"), sem("proj_bank1_free")]
        cv_mid = sem("conv_centre_tap_done")
        kk0_rdy = sem("kk_raw_ready")
        kksq_rdy = sem("kk_squares_ready")
        kkm_rdy = sem("kk_sum_clamped")
        kkr_rdy = sem("kk_rsqrt_ready")
        cum_rdy = sem("decay_sums_ready")
        exp_rdy = sem("decay_exps_ready")
        x_rdy = sem("khat_beta_ready")
        sc_ps = sem("scores_done")
        sc_sb = sem("scores_masked")
        nl_ps = sem("l_rows_done")
        nl_sb = sem("l_rows_masked")
        xt_ps = sem("token_major_done")
        xt_sb = sem("token_major_copied")
        vt_ps = sem("v_token_major_done")
        vt_sb = sem("v_token_major_copied")
        vt_all = sem("v_token_major_both")
        vt_low = sem("v_token_major_lower")
        z_rdy = [sem(f"inverse_ready{d}") for d in range(2)]
        tu_ps = [sem(f"inverse_t_done{d}") for d in range(2)]
        tu_sb = [sem(f"inverse_t_masked{d}") for d in range(2)]
        zz_ps = [sem(f"inverse_z_done{d}") for d in range(2)]
        rhs_ps = [sem(f"rhs_done{d}") for d in range(2)]
        rhs_cp = [sem(f"rhs_copied{d}") for d in range(2)]
        u_ps = [sem(f"u_done{d}") for d in range(2)]
        u_sb = [[sem(f"u_copied{d}{h}") for h in range(2)] for d in range(2)]
        st_ps = [sem(f"state_done{d}") for d in range(2)]
        st_sb = [sem(f"state_updated{d}") for d in range(2)]
        y_ps = [sem(f"y_done{d}") for d in range(2)]
        y_sb = [sem(f"y_copied{d}") for d in range(2)]
        ysum_rdy = sem("y_sum_ready")
        mean_ps = sem("mean_done")
        dev_rdy = sem("deviation_ready")
        dev2_rdy = sem("deviation_squares_ready")
        var_ps = sem("variance_done")
        rs_rdy = sem("readout_rstd_ready")
        bon_rdy = sem("bonus_product_ready")
        bon_ps = sem("bonus_done")
        late_ld = sem("late_constants_loaded")
        gv_act = sem("gmlp_v_gelu_done")
        gv_st = sem("gmlp_v_stats")
        gv_rs = sem("gmlp_v_rstd")
        vc_rdy = sem("gmlp_v_normed")
        gs_ps = sem("gmlp_spatial_done")
        gu_act = sem("gmlp_u_gelu_done")
        yg_rdy = sem("gmlp_out_ready")
        me_act = sem("merge_gates_ready")
        m_rdy = sem("merged_ready")
        o_sb = sem("w_out_copied")
        xr_ld = sem("x_reloaded")
        up_mid = sem("up_centre_tap_done")
        up_cv = sem("up_conv_done")
        up_act = sem("silu_done")
        ff_rdy = sem("ff_ready")
        dn_sb = sem("down_copied")
        cw_ld = sem("conv_ffn_loaded")
        x1_rdy = sem("x_after_mixer_ready")
        out_rdy = sem("output_ready")
        stored = sem("output_stored")

        def product_count(r, phase, k, i, per):
            return i * per + (loads_before(phase)[r] + k + 2)

        def item_count(i, n):
            return i * 5 + (n // 2 + 2)

        def proj_count(i, n):
            return i * 6 + (n - 1)

        def seg(v):
            return v.rearrange("p (s t) -> p s t", s=2)

        def chunks(v):
            return v.rearrange("p (c t) -> p c t", t=C)

        class Steps:

            def __init__(self, eng, s):
                self.eng, self.sem, self.base, self.n, self.seen = eng, s, 0, 0, 0
                self.fixed = 0

            def tick(self, ins):
                ins.then_inc(self.sem, 1)
                self.n += 1
                return self.n

            def need(self, n):
                if n > self.seen:
                    self.eng.wait_ge(self.sem, self.base + n)
                    self.seen = n

            def enter(self, i, per):
                self.fixed += self.n
                self.base = i * per + self.fixed
                self.n = self.seen = 0
                self.per = per

            def leave(self, passes):
                assert self.n == self.per, (self.n, self.per)
                self.fixed += self.per * passes
                self.base = self.fixed
                self.n = self.seen = 0

        four = [PB[0], PB[1], CH[0], CH[1]]

        def chunk_at(d, s):
            return (s + 4) % NCH if d == 0 else NCH - 1 - s

        def wide(v, n):
            return v[:, None, :].to_broadcast([P, n, v.shape[-1]])

        def deep(v, n):
            return v[:, :, None].to_broadcast([P, v.shape[-1], n])

        block = ctx.enter_context(nc.Block())

        @block.sync
        def _(sp):
            def load(r, phase, k, i, per, src):
                sp.wait_ge(used[r], i * per + (loads_before(phase)[r] + k + 1))
                n = src.shape[-1] if len(src.shape) == 2 else None
                p = src.shape[0]
                sp.dma_start(ring[0:p, r, 0:n], src).then_inc(loaded[r], 16)

            sp.dma_start(cvec[:], io["cvec"]).then_inc(consts_ld, 16)
            for t, name in ((ident, "ident"), (ones, "ones"), (blk, "blk"), (score_mask, "score_mask"),
                            (off_mask, "off_mask"), (eye2, "eye2"), (scan_mask, "scan_mask"), (bmod, "bmod"),
                            (gains, "gains"), (params, "params"), (conv_lora, "conv_lora"), (scal, "scal")):
                sp.dma_start(t[:], io[name]).then_inc(consts_ld, 16)
            sp.dma_start(hT[:], io["xT_all"]).then_inc(x_ld, 16)
            with sp.Fori(0, 8) as i:
                for r in range(4):
                    load(r, "mod", 0, i, 1, io["w_mod"][bass.ds(i * 4 + r, 1)].rearrange("a p n -> (a p) n"))
            for n in range(6):
                w = io["w_lora"][n] if n < 4 else io["w_gate"][n - 4]
                load(n % 4, "lora", n // 4, 0, 0, w[:, :])
            with sp.Fori(0, PAIRS) as i:
                for r in range(3):
                    load(r, "pair", 0, i, 1, io["w_rkv"][bass.ds(i * 3 + r, 1)].rearrange("a p n -> (a p) n"))
                sp.wait_ge(proj_ps, i * 6 + 1)
                sp.dma_start(lora_w[:], io["w_up_lora"][bass.ds(i, 1)].rearrange("a p m n -> (a p) m n")).then_inc(lw_ld, 16)
                for k in range(4):
                    load(3, "pair", k, i, 4,
                         io["w_mod"][bass.ds(i * 4 + 32 + k, 1)].rearrange("a p n -> (a p) n"))
            for h in range(2):
                for r in range(4):
                    load(r, "gv", h, 0, 0, io["w_v"][h * 4 + r])
            sp.wait_ge(pair_done, PAIRS + 1)
            sp.dma_start(vrow[:], io["lnv"].partition_broadcast(P)).then_inc(late_ld, 16)
            sp.dma_start(bsp[:], io["b_spatial"].partition_broadcast(P)).then_inc(late_ld, 16)
            sp.dma_start(wsp[:], io["w_spatial"]).then_inc(late_ld, 16)
            with sp.Fori(0, 2) as i:
                for r in range(4):
                    load(r, "gu", 0, i, 1, io["w_u"][bass.ds(i * 4 + r, 1)].rearrange("a p n -> (a p) n"))
            with sp.Fori(0, KT) as i:
                load(0, "merge", 0, i, 1, io["w_ga"][bass.ds(i, 1)].rearrange("a p n -> (a p) n"))
                load(1, "merge", 0, i, 1, io["w_gb"][bass.ds(i, 1)].rearrange("a p n -> (a p) n"))
                load(2, "merge", 0, i, 1, io["w_pa"][bass.ds(i, 1)].rearrange("a p n -> (a p) n"))
                load(3, "merge", 0, i, 1, io["w_pb"][bass.ds(i, 1)].rearrange("a p n -> (a p) n"))
            sp.wait_ge(m_rdy, KT + 1)
            sp.dma_start(xT[:], io["xT_all"][:, :, 0:T]).then_inc(xr_ld, 16)
            with sp.Fori(0, 4) as i:
                for r in range(4):
                    load(r, "out", 0, i, 1, io["w_out"][bass.ds(i * 4 + r, 1)].rearrange("a p n -> (a p) n"))
            with sp.Fori(0, FT // 2) as i:
                sp.wait_ge(up_cv, i * 2 + 2)
                sp.dma_start(convw[:], io["conv_ffn"][bass.ds(i, 1)].rearrange("a p m n -> (a p) m n")).then_inc(cw_ld, 16)
                for r in range(4):
                    load(r, "up", 0, i, 1, io["w_up"][bass.ds(i * 4 + r, 1)].rearrange("a p n -> (a p) n"))
            with sp.Fori(0, KT) as i:
                for r in range(4):
                    load(r, "down", 0, i, 1, io["w_down"][bass.ds(i * 4 + r, 1)].rearrange("a p n -> (a p) n"))
            sp.wait_ge(out_rdy, 1)
            sp.dma_start(io["outT"], mixT[:]).then_inc(stored, 16)
            sp.wait_ge(stored, 16)

        @block.tensor
        def _(pe):
            mm = nc.tensor.matmul

            def region(r, phase, k, i, per):
                pe.wait_ge(loaded[r], i * (16 * per) + 16 * (loads_before(phase)[r] + k + 1))

            def tile(r, kt, m=P):
                return ring[:, r, kt * m:(kt + 1) * m]

            def small():
                pe.sem_inc(seen, 1)

            for r in range(4):
                pe.sem_inc(used[r], 1)
            pe.sem_inc(proj_ps, 1)
            pe.sem_inc(pair_done, 1)

            def mod_tile(r, out):
                for kt in range(KT):
                    last = mm(out, tile(r, kt), csil[:, kt, :], start=(kt == 0), stop=(kt == KT - 1))
                return last

            def sum_squares(src, n, out):
                pe.wait_ge(sq_rdy, n)
                for kt in range(KT):
                    last = mm(out, ones[:, :], src[:, kt, :], start=(kt == 0), stop=(kt == KT - 1))
                last.then_inc(ssq_ps, 1)

            pe.wait_ge(consts_ld, 16 * NCONST)
            sum_squares(x_sq, 1, Q[1][:, :])
            pe.wait_ge(csil_rdy, 1)
            pe.sem_inc(mod_sbd, 1)
            with pe.Fori(0, 8) as i:
                pe.wait_ge(mod_sbd, i + 1)
                for r in range(4):
                    region(r, "mod", 0, i, 1)
                    mod_tile(r, Q[0][:, 2 * r:2 * r + 2]).then_inc(used[r], 1)

            pe.wait_ge(h_rdy, 1)
            for n in range(6):
                r = n % 4
                region(r, "lora", n // 4, 0, 0)
                if n >= 2:
                    pe.wait_ge(lo_cv, n - 1)
                m = LORA if n < 4 else P
                for kt in range(KT):
                    last = mm(PB[n % 2][0:m, :], tile(r, kt, m), hT[:, kt, :], start=(kt == 0), stop=(kt == KT - 1))
                last.then_inc(used[r], 1)
            pe.wait_ge(lo_cv, 6)
            pe.wait_ge(lo_act, 4)
            pe.sem_inc(pb_free[0], 1)
            pe.sem_inc(pb_free[1], 1)

            def pair(i):
                def bank_for(n):
                    pe.wait_ge(pb_free[n % 2], i * 5 + n // 2 + 1)
                    return PB[n % 2]

                for n in range(3):
                    b = bank_for(n)
                    region(n, "pair", 0, i, 1)
                    for kt in range(KT):
                        last = mm(b[:, :], tile(n, kt), hT[:, kt, :], start=(kt == 0), stop=(kt == KT - 1))
                    last.then_inc(used[n], 1)
                pe.wait_ge(lw_ld, i * 16 + 16)
                for d in range(2):
                    b = bank_for(3 + 2 * d)
                    mm(b[:, :], lora_w[0:LORA, d, :], lora_act[0:LORA, d, :], start=True, stop=True).then_inc(proj_ps, 1)
                    b = bank_for(4 + 2 * d)
                    mm(b[:, :], lora_w[0:LORA, 2 + d, :], lora_act[0:LORA, 2 + d, :], start=True, stop=True).then_inc(proj_ps, 1)
                b = bank_for(7)
                pe.wait_ge(kksq_rdy, i + 1)
                mm(b[:, :], blk[:, :], tmp, start=True, stop=True).then_inc(proj_ps, 1)
                b = bank_for(8)
                for k in range(2):
                    last = mm(b[:, 0:T], lora_w[:, 4 + k, :], lora_act[:, 4 + k, 0:T], start=(k == 0), stop=(k == 1))
                last.then_inc(proj_ps, 1)
                b = bank_for(9)
                for k in range(4):
                    region(3, "pair", k, i, 4)
                    mod_tile(3, b[:, 2 * k:2 * k + 2]).then_inc(used[3], 1)
                pe.wait_ge(pb_free[0], item_count(i, 2))
                for ch in range(NCH):
                    for h in range(2):
                        hr = slice(64 * h, 64 * h + 64)
                        last = mm(CH[0][hr, ch * C:(ch + 1) * C], vx[:, ch * C:(ch + 1) * C], ident[:, hr],
                                  start=True, stop=True)
                last.then_inc(vt_ps, 1)
                for d in range(2):
                    pe.wait_ge(x_rdy, i * 2 + d + 1)
                    if d == 1:
                        pe.wait_ge(nl_sb, i * 2 + 1)
                        pe.wait_ge(xt_sb, i * 4 + 2)
                    for s in range(2):
                        for h in range(2):
                            rows = slice(64 * h, 64 * h + 64)
                            for c in range(4):
                                ch = 4 * s + c
                                last = mm(Q[2 * s + h][:, c * P:(c + 1) * P], X[rows, ch], KR[d][rows, ch],
                                          start=True, stop=True)
                        last.then_inc(sc_ps, 1)
                    for s in range(2):
                        pe.wait_ge(sc_sb, i * 4 + 2 * d + s + 1)
                        for c in range(4):
                            ch = 4 * s + c
                            last = nc.tensor.transpose(Q[2 * s + 1][:, c * P:(c + 1) * P], X[:, ch], ident[:, :])
                        last.then_inc(xt_ps, 1)
                    for h in range(2):
                        rows, orow = slice(64 * h, 64 * h + 64), slice(64 - 64 * h, 128 - 64 * h)
                        for ch in range(NCH):
                            last = mm(Q[0][orow, ch * C:(ch + 1) * C], KR[d][rows, ch, 0], X[rows, ch, 1 - h],
                                      start=True, stop=True)
                    last.then_inc(nl_ps, 1)
                pe.wait_ge(xt_sb, i * 4 + 4)
                pe.wait_ge(nl_sb, i * 2 + 2)
                for lv in range(LEVELS - 1):
                    for d in range(2):
                        pe.wait_ge(z_rdy[d], i * LEVELS + lv + 1)
                        small()
                        for h in range(2):
                            hr = slice(64 - 64 * h, 128 - 64 * h)
                            for ch in range(NCH):
                                last = mm(Q[2 * d][hr, ch * C:(ch + 1) * C], NL[d][hr, ch], ZU[d][hr, ch],
                                          start=True, stop=True)
                        last.then_inc(tu_ps[d], 1)
                    for d in range(2):
                        pe.wait_ge(tu_sb[d], i * (LEVELS - 1) + lv + 1)
                        small()
                        for h in range(2):
                            hr = slice(64 - 64 * h, 128 - 64 * h)
                            for ch in range(NCH):
                                last = mm(Q[2 * d + 1][hr, ch * C:(ch + 1) * C], ZL[d][hr, ch], TU[d][hr, ch],
                                          start=True, stop=True)
                        if lv < LEVELS - 2:
                            for h in range(2):
                                hr = slice(64 - 64 * h, 128 - 64 * h)
                                for ch in range(NCH):
                                    last = mm(Q[2 * d][hr, ch * C:(ch + 1) * C], TU[d][hr, ch], ZL[d][hr, ch],
                                              start=True, stop=True)
                        last.then_inc(zz_ps[d], 1)
                pe.wait_ge(vt_all, i + 1)
                for s in range(NCH):
                    for d in range(2):
                        ch = chunk_at(d, s)
                        if s:
                            pe.wait_ge(st_sb[d], i * 7 + s)
                        else:
                            pe.wait_ge(z_rdy[d], i * LEVELS + LEVELS)
                        small()
                        for h in range(2):
                            rows, orow = slice(64 * h, 64 * h + 64), slice(64 - 64 * h, 128 - 64 * h)
                            last = mm(CH[d][orow, 0:C], SC[d][h][rows, ch, 0], VU[d][rows, ch, h],
                                      start=True, stop=(s == 0))
                            if s:
                                last = mm(CH[d][orow, 0:C], KR[d][rows, ch, 0], ST[d][s % 2][rows, :],
                                          start=False, stop=True)
                        last.then_inc(rhs_ps[d], 1)
                    for d in range(2):
                        ch = chunk_at(d, s)
                        pe.wait_ge(rhs_cp[d], i * NCH + s + 1)
                        small()
                        for h in range(2):
                            hr = slice(64 - 64 * h, 128 - 64 * h)
                            last = mm(CH[d][hr, C:2 * C], ZU[d][hr, ch], rhs_sb[d][hr, :], start=True, stop=True)
                        last.then_inc(u_ps[d], 1)
                    for d in range(2):
                        ch = chunk_at(d, s)
                        for h in range(2):
                            pe.wait_ge(u_sb[d][h], i * NCH + s + 1)
                        if s < NCH - 1:
                            for h in range(2):
                                last = mm(CH[d][64 * h:64 * h + 64, 2 * C:3 * C], XT[d][:, ch, 64 * h:64 * h + 64],
                                          VU[d][:, ch, h], start=True, stop=True)
                            last.then_inc(st_ps[d], 1)
                        if s >= 4:
                            if s > 4:
                                pe.wait_ge(y_sb[d], i * 4 + s - 4)
                            for h in range(2):
                                rows = slice(64 * h, 64 * h + 64)
                                mm(Q[2 * d][rows, 0:C], VU[d][:, ch, h], SC[d][h][:, ch, 1], start=True, stop=False)
                            for h in range(2):
                                rows = slice(64 * h, 64 * h + 64)
                                last = mm(Q[2 * d][rows, 0:C], ST[d][s % 2][rows, :], KR[d][rows, ch, 1],
                                          start=False, stop=True)
                            last.then_inc(y_ps[d], 1)
                pe.wait_ge(bon_rdy, i + 1)
                mm(Q[3][:, 0:T], blk[:, :], rc, start=True, stop=True).then_inc(bon_ps, 1)
                pe.wait_ge(ysum_rdy, i + 1)
                mm(Q[0][:, 0:T], blk[:, :], ra, start=True, stop=True).then_inc(mean_ps, 1)
                pe.wait_ge(dev2_rdy, i + 1)
                mm(Q[1][:, 0:T], blk[:, :], rb, start=True, stop=True).then_inc(var_ps, 1)

            with pe.Fori(0, PAIRS) as i:
                pair(i)

            pe.wait_ge(pair_done, PAIRS + 1)
            for h in range(2):
                for r in range(4):
                    region(r, "gv", h, 0, 0)
                    for k in range(4):
                        kt = 4 * r + k
                        for n in range(2):
                            last = mm(Q[2 * h + n][:, :], hT[:, kt, n * P:(n + 1) * P],
                                      ring[:, r, k * 512:(k + 1) * 512], start=(kt == 0), stop=(kt == KT - 1))
                    last.then_inc(used[r], 1)
            pe.wait_ge(late_ld, 48)
            pe.sem_inc(yg_rdy, 2)
            pe.sem_inc(gs_ps, 2)
            with pe.Fori(0, 2) as i:
                for r in range(4):
                    region(r, "gu", 0, i, 1)
                    pe.wait_ge(yg_rdy, i * 4 + r + 1)
                    for kt in range(KT):
                        last = mm(PB[r % 2][:, 0:T], tile(r, kt), hT[:, kt, 0:T], start=(kt == 0), stop=(kt == KT - 1))
                    last.then_inc(used[r], 1)
                    pe.wait_ge(vc_rdy, i * 4 + r + 1)
                    for n in range(2):
                        last = mm(CH[r % 2][:, n * P:(n + 1) * P], vcur[r % 2][:, n],
                                  wsp[:, bass.ds(i * 4 + r, 1), :].rearrange("p a b -> p (a b)"), start=True, stop=True)
                    last.then_inc(gs_ps, 1)
            pe.wait_ge(yg_rdy, GG + 2)
            pe.sem_inc(me_act, 2)
            pe.sem_inc(m_rdy, 1)
            with pe.Fori(0, KT) as i:
                for r in range(4):
                    region(r, "merge", 0, i, 1)
                    if r < 2:
                        pe.wait_ge(me_act, i * 2 + r + 1)
                    else:
                        pe.wait_ge(m_rdy, i + 1)
                    src, n = ((hT, KT), (hT, KT), (yr, KT), (yg, GG))[r]
                    for kt in range(n):
                        last = mm(Q[r][:, 0:T], tile(r, kt), src[:, kt, 0:T], start=(kt == 0), stop=(kt == n - 1))
                    last.then_inc(used[r], 1)
            pe.wait_ge(m_rdy, KT + 1)
            pe.sem_inc(o_sb, 4)
            with pe.Fori(0, 4) as i:
                for r in range(4):
                    region(r, "out", 0, i, 1)
                    pe.wait_ge(o_sb, i * 4 + r + 1)
                    for kt in range(KT):
                        last = mm(four[r][:, 0:T], tile(r, kt), mT[:, kt, :], start=(kt == 0), stop=(kt == KT - 1))
                    last.then_inc(used[r], 1)
            sum_squares(sq, 2, Q[0][:, 0:T])
            sum_squares(sq, 3, Q[1][:, 0:T])
            pe.wait_ge(h_rdy, 2)
            pe.wait_ge(o_sb, KT + 4)
            pe.sem_inc(up_cv, 2)
            pe.sem_inc(ff_rdy, 2)
            with pe.Fori(0, FT // 2) as i:
                for r in range(4):
                    region(r, "up", 0, i, 1)
                    pe.wait_ge(up_cv, i * 2 + 1 + r // 2)
                    for kt in range(KT):
                        last = mm(four[r][:, 0:T], tile(r, kt), h2T[:, kt, :], start=(kt == 0), stop=(kt == KT - 1))
                    last.then_inc(used[r], 1)
            pe.wait_ge(ff_rdy, FT + 2)
            pe.sem_inc(dn_sb, 1)
            with pe.Fori(0, KT) as i:
                pe.wait_ge(dn_sb, i + 1)
                for r in range(4):
                    region(r, "down", 0, i, 1)
                    for k in range(FT // 4):
                        kt = r * (FT // 4) + k
                        last = mm(Q[2][:, 0:T], tile(r, k), ffT[:, kt, :], start=(kt == 0), stop=(kt == FT - 1))
                    last.then_inc(used[r], 1)
            sum_squares(sq, 4, Q[0][:, 0:T])

        @block.scalar
        def _(act):
            A = Steps(act, act_step)
            f = nc.scalar.activation

            def product(r, phase, k, i, per):
                act.wait_ge(used[r], product_count(r, phase, k, i, per))

            def rms(n, out, psum, width):
                act.wait_ge(ssq_ps, n)
                A.need(A.tick(f(out, psum, ACT.Ln, scale=1.0 / D, bias=scal[:, 0:1])))
                f(out, out, ACT.Exp, scale=-0.5).then_inc(rstd_rdy, 1)

            act.preload_act_table_set("natural_log_exp_and_others")
            act.wait_ge(consts_ld, 16 * NCONST)
            f(csil[:], cvec[:], ACT.Exp, scale=-1.0).then_inc(cexp_rdy, 1)
            act.wait_ge(x_ld, 16)
            f(x_sq, hT[:], ACT.Square).then_inc(sq_rdy, 1)
            rms(1, rstd[:, :], Q[1][:, :], TT)
            for n in range(6):
                m = LORA if n < 4 else P
                product(n % 4, "lora", n // 4, 0, 0)
                f(lora_act[0:m, n], PB[n % 2][0:m, :], ACT.Identity, scale=conv_lora[0:m, n, 1:2]).then_inc(lo_mid, 1)
            act.wait_ge(lo_cv, 6)
            for n in range(2):
                f(lora_act[0:LORA, n], lora_act[0:LORA, n], ACT.Tanh).then_inc(lo_act, 1)
            for n in range(4, 6):
                f(lora_act[:, n], lora_act[:, n], ACT.Sigmoid).then_inc(lo_act, 1)
            act.wait_ge(par_rdy, 1)
            act.preload_act_table_set("natural_log_exp_and_others")

            with act.Fori(0, PAIRS) as i:
                A.enter(i, 2)
                act.wait_ge(pair_done, i + 1)
                A.need(A.tick(f(par_a[:, :], paramx[:, bass.ds(i, 1), :].rearrange("p a b -> p (a b)"), ACT.Copy)))
                for n, x, c in ((0, kx, PK), (1, rx, PR), (2, vx, PV)):
                    product(n, "pair", 0, i, 1)
                    f(x, PB[n % 2][:, :], ACT.Identity, scale=par_a[:, c + 1:c + 2]).then_inc(cv_mid, 1)
                act.wait_ge(kk0_rdy, i + 1)
                f(tmp, kkx, ACT.Square).then_inc(kksq_rdy, 1)
                for d in range(2):
                    act.wait_ge(proj_ps, proj_count(i, 3 + 2 * d))
                    f(ew[d], PB[1][:, :], ACT.Exp, scale=-1.0, bias=par_a[:, PNW0 + d:PNW0 + d + 1]).then_inc(pb_free[1], 1)
                    act.wait_ge(proj_ps, proj_count(i, 4 + 2 * d))
                    f(ea[d], PB[0][:, :], ACT.Exp, scale=-1.0, bias=par_a[:, PNA0 + d:PNA0 + d + 1]).then_inc(pb_free[0], 1)
                act.wait_ge(kkm_rdy, i + 1)
                f(tmp2, tmp2, ACT.Ln, scale=float(2 ** LN_SHIFT)).then_inc(pb_free[1], 1)
                act.wait_ge(pb_free[1], item_count(i, 7))
                f(tmp2, tmp2, ACT.Exp, scale=-0.5, bias=scal[:, 3:4]).then_inc(kkr_rdy, 1)
                act.wait_ge(proj_ps, proj_count(i, 8))
                f(gT, PB[0][:, 0:T], ACT.Copy).then_inc(pb_free[0], 1)
                for d in range(2):
                    act.wait_ge(cum_rdy, i * 2 + d + 1)
                    incl, excl = ((cumP[0], -DECAY_C), (cumG[0], -DECAY_C)) if d == 0 else \
                                 ((cumG[1], DECAY_C), (cumP[1], DECAY_C))
                    f(eIn[d], incl[0], ACT.Exp, scale=incl[1])
                    f(eEx[d], excl[0], ACT.Exp, scale=excl[1])
                    f(wc[d], chunks(cumP[d])[:, :, C - 1], ACT.Exp, scale=-DECAY_C)
                    f(eNeg[d], incl[0], ACT.Exp, scale=-incl[1]).then_inc(exp_rdy, 1)
                act.wait_ge(vt_ps, i + 1)
                for h in range(2):
                    hr = slice(64 * h, 64 * h + 64)
                    last = f(VU[0][hr, :, h], chunks(CH[0][hr, :]), ACT.Copy)
                last.then_inc(vt_sb, 1)
                for d in range(2):
                    for s in range(2):
                        act.wait_ge(xt_ps, i * 4 + 2 * d + s + 1)
                        f(XT[d][:, 4 * s:4 * s + 4], Q[2 * s + 1][:, :].rearrange("p (c n) -> p c n", c=4),
                          ACT.Copy).then_inc(xt_sb, 1)
                for s in range(NCH):
                    act.wait_ge(rhs_ps[1], i * NCH + s + 1)
                    f(rhs_sb[1], CH[1][:, 0:C], ACT.Copy).then_inc(rhs_cp[1], 1)
                    for d in range(2):
                        act.wait_ge(u_ps[d], i * NCH + s + 1)
                        f(VU[d][0:64, chunk_at(d, s), 1], CH[d][0:64, C:2 * C], ACT.Copy, scale=-1.0).then_inc(u_sb[d][1], 1)
                    if s >= 4:
                        for d in range(2):
                            ch = chunk_at(d, s)
                            act.wait_ge(y_ps[d], i * 4 + s - 3)
                            f(yd[d][:, ch * C:(ch + 1) * C], Q[2 * d][:, 0:C], ACT.Copy).then_inc(y_sb[d], 1)
                act.wait_ge(dev_rdy, i + 1)
                f(rb, ra, ACT.Square).then_inc(dev2_rdy, 1)
                act.wait_ge(var_ps, i + 1)
                A.need(A.tick(f(rb, Q[1][:, 0:T], ACT.Ln, scale=1.0 / HEAD, bias=scal[:, 2:3])))
                f(rb, rb, ACT.Exp, scale=-0.5).then_inc(rs_rdy, 1)
            A.leave(PAIRS)

            act.wait_ge(pair_done, PAIRS + 1)
            for h in range(2):
                product(3, "gv", h, 0, 0)
                for n in range(2):
                    f(vg[:, n, h * 512:(h + 1) * 512], Q[2 * h + n][:, :], ACT.Gelu).then_inc(gv_act, 1)
            act.wait_ge(gv_st, 2)
            A.need(A.tick(f(vrs, mv[:, :, 1], ACT.Ln, bias=scal[:, 1:2])))
            f(vrs, vrs, ACT.Exp, scale=-0.5).then_inc(gv_rs, 1)
            act.preload_act_table(ACT.Gelu)
            with act.Fori(0, 2) as i:
                for r in range(4):
                    act.wait_ge(yg_rdy, i * 4 + r + 1)
                    product(r, "gu", 0, i, 1)
                    f(ug[r % 2], PB[r % 2][:, 0:T], ACT.Gelu).then_inc(gu_act, 1)
            act.preload_act_table(ACT.Sigmoid)
            with act.Fori(0, KT) as i:
                act.wait_ge(m_rdy, i + 1)
                for r, o in ((0, sga), (1, sgb)):
                    product(r, "merge", 0, i, 1)
                    f(o, Q[r][:, 0:T], ACT.Sigmoid).then_inc(me_act, 1)
            act.wait_ge(m_rdy, KT + 1)
            with act.Fori(0, 4) as i:
                for r in range(4):
                    product(r, "out", 0, i, 1)
                    f(mixT[:, bass.ds(i * 4 + r, 1), :].rearrange("p a b -> p (a b)"), four[r][:, 0:T], ACT.Copy).then_inc(o_sb, 1)
            act.wait_ge(o_sb, KT + 4)
            f(sq, mixT, ACT.Square).then_inc(sq_rdy, 1)
            rms(2, rstd[:, 0:T], Q[0][:, 0:T], T)
            act.wait_ge(x1_rdy, 1)
            f(sq, xT, ACT.Square).then_inc(sq_rdy, 1)
            rms(3, rstd[:, 0:T], Q[1][:, 0:T], T)
            act.preload_act_table(ACT.Silu)
            act.wait_ge(h_rdy, 2)
            with act.Fori(0, FT // 2) as i:
                for r in range(4):
                    product(r, "up", 0, i, 1)
                    if r == 0:
                        act.wait_ge(cw_ld, i * 16 + 16)
                    if r % 2 == 0:
                        act.wait_ge(ff_rdy, i * 2 + r // 2 + 1)
                    f(cv[r], four[r][:, 0:T], ACT.Identity, scale=convw[:, r, 4:5]).then_inc(up_mid, 1)
                for j in range(2):
                    act.wait_ge(up_cv, i * 2 + j + 3)
                    f(sil[j], cv[2 * j], ACT.Silu).then_inc(up_act, 1)
            with act.Fori(0, KT) as i:
                product(3, "down", 0, i, 1)
                f(mixT[:, bass.ds(i, 1), :].rearrange("p a b -> p (a b)"), Q[2][:, 0:T], ACT.Copy).then_inc(dn_sb, 1)
            act.wait_ge(dn_sb, KT + 1)
            f(sq, mixT, ACT.Square).then_inc(sq_rdy, 1)
            rms(4, rstd[:, 0:T], Q[0][:, 0:T], T)

        @block.vector
        def _(dve):
            V = Steps(dve, dve_step)
            tt, ts, stt = nc.vector.tensor_tensor, nc.vector.tensor_scalar, nc.vector.scalar_tensor_tensor

            def product(r, phase, k, i, per):
                dve.wait_ge(used[r], product_count(r, phase, k, i, per))

            def flow(*ins):
                for x in ins:
                    V.need(V.tick(x))

            dve.wait_ge(consts_ld, 16 * NCONST)
            V.tick(nc.vector.tensor_copy(paramx[:, :, 0:NPAR], params[:]))
            V.tick(ts(paramx[:, :, PNW0:PNW0 + 4], params[:, :, PW0:PW0 + 4], -1.0, None, ALU.mult))
            V.tick(ts(paramx[:, :, POKA:POKA + 1], params[:, :, PKA:PKA + 1], -1.0, 1.0, ALU.mult, ALU.add))
            nc.vector.memset(paramx[:, :, POKA + 1:], 0.0).then_inc(par_rdy, 1)
            dve.wait_ge(cexp_rdy, 1)
            flow(ts(csil[:], csil[:], 1.0, None, ALU.add))
            flow(nc.vector.reciprocal(csil[:], csil[:]))
            tt(csil[:], csil[:], cvec[:], ALU.mult).then_inc(csil_rdy, 1)
            dve.wait_ge(rstd_rdy, 1)
            V.tick(tt(hT[:], hT[:], wide(rstd[:, :], KT), ALU.mult))

            def mod_out(psum, at):
                return tt(modT[:, bass.ds(at, 4), :], psum.rearrange("p (a b) -> p a b", a=4),
                          bmod[:, bass.ds(at, 4)][:, :, None].to_broadcast([P, 4, 2]), ALU.add)

            with dve.Fori(0, 8) as i:
                product(3, "mod", 0, i, 1)
                mod_out(Q[0][:, 0:8], i * 4).then_inc(mod_sbd, 1)
            dve.wait_ge(mod_sbd, 9)
            flow(stt(gcol[:], modT[:, KT:2 * KT, :], 1.0, deep(gains[:, 0, :], 2), ALU.add, ALU.mult))
            for s in range(2):
                part = hT[:, :, s * T:(s + 1) * T]
                flow(tt(part, part, gcol[:, :, s:s + 1].to_broadcast([P, KT, T]), ALU.mult))
                last = tt(part, part, modT[:, 0:KT, s:s + 1].to_broadcast([P, KT, T]), ALU.add)
                if s == 0:
                    V.tick(last)
            last.then_inc(h_rdy, 1)

            def side_taps(x, psum, w):
                flow(stt(x[:, :, 1:T], psum[:, :, 0:T - 1], w[0], x[:, :, 1:T], ALU.mult, ALU.add))
                return stt(x[:, :, 0:T - 1], psum[:, :, 1:T], w[2], x[:, :, 0:T - 1], ALU.mult, ALU.add)

            for n in range(6):
                m = LORA if n < 4 else P
                dve.wait_ge(lo_mid, n + 1)
                side_taps(seg(lora_act[0:m, n]), seg(PB[n % 2][0:m, :]),
                          [conv_lora[0:m, n, k:k + 1] for k in range(3)]).then_inc(lo_cv, 1)
            dve.wait_ge(par_rdy, 1)

            def par(c):
                return par_v[:, c:c + 1]

            with dve.Fori(0, PAIRS) as i:
                V.enter(i, PAIR_STEPS)
                flow(nc.vector.tensor_copy(par_v[:, :], paramx[:, bass.ds(i, 1), :].rearrange("p a b -> p (a b)")))
                for n, x, c in ((0, kx, PK), (1, rx, PR), (2, vx, PV)):
                    dve.wait_ge(cv_mid, i * 3 + n + 1)
                    side_taps(seg(x), seg(PB[n % 2][:, :]), [par(c), None, par(c + 2)]).then_inc(pb_free[n % 2], 1)
                    if n == 0:
                        dve.wait_ge(pb_free[0], item_count(i, 0))
                        ts(kkx, kx, par(PKK), None, ALU.mult).then_inc(kk0_rdy, 1)
                dve.wait_ge(pb_free[0], item_count(i, 2))
                for d in range(2):
                    dve.wait_ge(pb_free[1], item_count(i, 3 + 2 * d))
                    flow(ts(ew[d], ew[d], 1.0, None, ALU.add))
                    flow(nc.vector.reciprocal(ew[d], ew[d]))
                    flow(nc.vector.tensor_tensor_scan(cumP[d], scan_mask[:, :], ew[d], 0.0, ALU.mult, ALU.add))
                    tt(cumG[d], cumP[d], ew[d], ALU.subtract).then_inc(cum_rdy, 1)
                    dve.wait_ge(pb_free[0], item_count(i, 4 + 2 * d))
                    flow(ts(ea[d], ea[d], 1.0, None, ALU.add))
                    flow(nc.vector.reciprocal(ea[d], ea[d]))
                    flow(ts(kdir[d], ea[d], par(PKA), par(POKA), ALU.mult, ALU.add))
                    V.tick(tt(kdir[d], kdir[d], kx, ALU.mult))
                dve.wait_ge(proj_ps, proj_count(i, 7))
                ts(tmp2, PB[1][:, :], KK_MIN, None, ALU.max).then_inc(kkm_rdy, 1)
                product(3, "pair", 3, i, 4)
                mod_out(PB[1][:, 0:8], i * 4 + 32).then_inc(pb_free[1], 1)
                dve.wait_ge(kkr_rdy, i + 1)
                flow(tt(kkx, kkx, tmp2, ALU.mult))
                flow(tt(rc, kdir[0][:, 0:T], kdir[1][:, 0:T], ALU.add))
                stt(rc, rc, par(PRK), rx[:, 0:T], ALU.mult, ALU.mult).then_inc(bon_rdy, 1)
                for d in range(2):
                    flow(tt(ea[d], ea[d], kkx, ALU.mult))
                    dve.wait_ge(exp_rdy, i * 2 + d + 1)
                    V.tick(tt(KR[d][:, :, 0], chunks(kkx), chunks(eEx[d]), ALU.mult))
                    V.tick(tt(KR[d][:, :, 1], chunks(rx), chunks(eIn[d]), ALU.mult))
                    if d == 1:
                        dve.wait_ge(nl_ps, i * 2 + 1)
                    for h in range(2):
                        rows = slice(64 * h, 64 * h + 64)
                        V.tick(tt(X[rows, :, h], chunks(kdir[d][rows, :]), chunks(eNeg[d][rows, :]), ALU.mult))
                        last = tt(X[rows, :, 1 - h], chunks(ea[d][rows, :]), chunks(eNeg[d][rows, :]), ALU.mult)
                        if h == 0:
                            V.tick(last)
                    last.then_inc(x_rdy, 1)
                    for s in range(2):
                        dve.wait_ge(sc_ps, i * 4 + 2 * d + s + 1)
                        for h in range(2):
                            last = tt(SC[d][h][:, 4 * s:4 * s + 4].rearrange("p c a t -> p c (a t)"),
                                      Q[2 * s + h][:, :].rearrange("p (c n) -> p c n", c=4),
                                      wide(score_mask[:, d, :], 4), ALU.mult)
                            if h == 0:
                                V.tick(last)
                        last.then_inc(sc_sb, 1)
                    dve.wait_ge(nl_ps, i * 2 + d + 1)
                    tt(NL[d], chunks(Q[0][:, :]), wide(score_mask[:, 1 - d, 0:C], NCH), ALU.mult).then_inc(nl_sb, 1)
                    dve.wait_ge(sc_sb, i * 4 + 2 * d + 2)
                    for h in range(2):
                        hr = slice(64 - 64 * h, 128 - 64 * h)
                        m = V.tick(tt(TU[d][hr], SC[d][h][hr, :, 0],
                                      off_mask[hr, d, 0, :][:, None, :].to_broadcast([64, NCH, C]), ALU.mult))
                    V.need(m)
                    flow(tt(ZU[d], wide(eye2[:, :], NCH), TU[d], ALU.subtract))
                    dve.wait_ge(nl_sb, i * 2 + d + 1)
                    flow(tt(TU[d], NL[d], wide(off_mask[:, 1 - d, 0, :], NCH), ALU.mult))
                    tt(ZL[d], wide(eye2[:, :], NCH), TU[d], ALU.subtract).then_inc(z_rdy[d], 1)
                for lv in range(LEVELS - 1):
                    for d in range(2):
                        dve.wait_ge(tu_ps[d], i * (LEVELS - 1) + lv + 1)
                        tt(TU[d], chunks(Q[2 * d][:, :]), wide(off_mask[:, d, lv + 1, :], NCH), ALU.mult).then_inc(tu_sb[d], 1)
                    for d in range(2):
                        dve.wait_ge(zz_ps[d], i * (LEVELS - 1) + lv + 1)
                        last = tt(ZU[d], ZU[d], chunks(Q[2 * d + 1][:, :]), ALU.subtract)
                        if lv < LEVELS - 2:
                            V.tick(last)
                            last = tt(ZL[d], ZL[d], chunks(Q[2 * d][:, :]), ALU.subtract)
                        last.then_inc(z_rdy[d], 1)
                for s in range(NCH):
                    dve.wait_ge(rhs_ps[0], i * NCH + s + 1)
                    nc.vector.tensor_copy(rhs_sb[0], CH[0][:, 0:C]).then_inc(rhs_cp[0], 1)
                    decay = [wc[0][:, chunk_at(0, s):chunk_at(0, s) + 1],
                             wc[1][:, chunk_at(1, min(s + 1, NCH - 1)):chunk_at(1, min(s + 1, NCH - 1)) + 1]]
                    if 0 < s < NCH - 1:
                        for d in range(2):
                            dve.wait_ge(st_sb[d], i * 7 + s)
                            w = V.tick(ts(STw[d], ST[d][s % 2], decay[d], None, ALU.mult))
                    for d in range(2):
                        dve.wait_ge(u_ps[d], i * NCH + s + 1)
                        ts(VU[d][64:128, chunk_at(d, s), 0], CH[d][64:128, C:2 * C], -1.0, None, ALU.mult).then_inc(u_sb[d][0], 1)
                    if s < NCH - 1:
                        for d in range(2):
                            dve.wait_ge(st_ps[d], i * 7 + s + 1)
                            new, psum = ST[d][(s + 1) % 2], CH[d][:, 2 * C:3 * C]
                            if s == 0:
                                last = ts(new, psum, decay[d], None, ALU.mult)
                            else:
                                V.need(w)
                                last = stt(new, psum, decay[d], STw[d], ALU.mult, ALU.add)
                            last.then_inc(st_sb[d], 1)
                for d in range(2):
                    dve.wait_ge(y_sb[d], i * 4 + 4)
                tt(ra, yd[0], yd[1], ALU.add).then_inc(ysum_rdy, 1)
                dve.wait_ge(bon_ps, i + 1)
                V.tick(tt(rc, Q[3][:, 0:T], vx[:, 0:T], ALU.mult))
                dve.wait_ge(mean_ps, i + 1)
                stt(ra, Q[0][:, 0:T], -1.0 / HEAD, ra, ALU.mult, ALU.add).then_inc(dev_rdy, 1)
                dve.wait_ge(rs_rdy, i + 1)
                flow(tt(ra, ra, rb, ALU.mult))
                flow(ts(ra, ra, par(PLG), par(PLB), ALU.mult, ALU.add))
                flow(tt(ra, ra, rc, ALU.add))
                dve.wait_ge(pb_free[0], item_count(i, 8))
                tt(yr[:, bass.ds(i, 1), :].rearrange("p a b -> p (a b)"), ra, gT, ALU.mult).then_inc(pair_done, 1)
            V.leave(PAIRS)

            dve.wait_ge(pair_done, PAIRS + 1)
            dve.wait_ge(gv_act, 4)
            for n in range(2):
                for h in range(2):
                    m = V.tick(nc.vector.bn_stats(bn[:, n, h, :], vg[:, n, h * 512:(h + 1) * 512]))
            V.need(m)
            for n in range(2):
                nc.vector.bn_aggr(mv[:, n, :], bn[:, n].rearrange("p a b -> p (a b)")).then_inc(gv_st, 1)
            dve.wait_ge(gv_rs, 1)
            for n in range(2):
                flow(ts(vg[:, n], vg[:, n], mv[:, n, 0:1], vrs[:, n:n + 1], ALU.subtract, ALU.mult))
            dve.wait_ge(late_ld, 48)
            with dve.Fori(0, 2) as i:
                V.enter(i, 8)
                for r in range(4):
                    at = (i * 4 + r) * P
                    dve.wait_ge(gs_ps, i * 4 + r + 1)
                    flow(tt(vcur[r % 2], vg[:, :, bass.ds(at, P)],
                            vrow[:, 0, bass.ds(at, P)][:, None, :].to_broadcast([P, 2, P]), ALU.mult))
                    tt(vcur[r % 2], vcur[r % 2], vrow[:, 1, bass.ds(at, P)][:, None, :].to_broadcast([P, 2, P]),
                       ALU.add).then_inc(vc_rdy, 1)
                    dve.wait_ge(gs_ps, i * 4 + r + 3)
                    flow(tt(ssp[r % 2].rearrange("p (a b) -> p a b", a=2),
                            CH[r % 2][:, 0:T].rearrange("p (a b) -> p a b", a=2),
                            bsp[:, bass.ds(i * 4 + r, 1), :].to_broadcast([P, 2, P]), ALU.add))
                    dve.wait_ge(gu_act, i * 4 + r + 1)
                    tt(yg[:, bass.ds(i * 4 + r, 1), :].rearrange("p a b -> p (a b)"), ssp[r % 2], ug[r % 2],
                       ALU.mult).then_inc(yg_rdy, 1)
            V.leave(2)
            with dve.Fori(0, KT) as i:
                V.enter(i, 2)
                for r, o, g in ((2, mta, sga), (3, mtb, sgb)):
                    product(r, "merge", 0, i, 1)
                    dve.wait_ge(me_act, i * 2 + r + 1)
                    m = V.tick(tt(o, g, Q[r][:, 0:T], ALU.mult))
                V.need(m)
                tt(mT[:, bass.ds(i, 1), :].rearrange("p a b -> p (a b)"), mta, mtb, ALU.add).then_inc(m_rdy, 1)
            V.leave(KT)

            def normed_residual(n, gain, at, x):
                flow(tt(gcol[:, :, 0], modT[:, at:at + KT, 0], gains[:, gain, :], ALU.mult))
                dve.wait_ge(rstd_rdy, n)
                flow(tt(mixT, mixT, wide(rstd[:, 0:T], KT), ALU.mult))
                flow(tt(mixT, mixT, gcol[:, :, 0:1].to_broadcast([P, KT, T]), ALU.mult))
                return tt(x, xT, mixT, ALU.add)

            dve.wait_ge(xr_ld, 16)
            normed_residual(2, 1, 2 * KT, xT).then_inc(x1_rdy, 1)
            flow(stt(gcol[:, :, 0], modT[:, 4 * KT:5 * KT, 0], 1.0, gains[:, 2, :], ALU.add, ALU.mult))
            dve.wait_ge(rstd_rdy, 3)
            flow(tt(h2T, xT, wide(rstd[:, 0:T], KT), ALU.mult))
            flow(tt(h2T, h2T, gcol[:, :, 0:1].to_broadcast([P, KT, T]), ALU.mult))
            tt(h2T, h2T, modT[:, 3 * KT:4 * KT, 0:1].to_broadcast([P, KT, T]), ALU.add).then_inc(h_rdy, 1)

            def grid(v):
                return v.rearrange("p (r c) -> p r c", r=ROWS)

            side = [(a, b) for a in (-1, 0, 1) for b in (-1, 0, 1) if (a, b) != (0, 0)]
            with dve.Fori(0, FT // 2) as i:
                V.enter(i, 30)
                for j in range(2):
                    dve.wait_ge(up_mid, i * 4 + 2 * j + 2)
                    prev = [0, 0]
                    for n, (a, b) in enumerate(side):
                        for q in range(2):
                            r = 2 * j + q
                            orow, irow = slice(max(0, -a), ROWS - max(0, a)), slice(max(0, a), ROWS - max(0, -a))
                            ocol, icol = slice(max(0, -b), GRID - max(0, b)), slice(max(0, b), GRID - max(0, -b))
                            if n:
                                V.need(prev[q])
                            w = 3 * (a + 1) + b + 1
                            last = stt(grid(cv[r])[:, orow, ocol], grid(four[r][:, 0:T])[:, irow, icol],
                                       convw[:, r, w:w + 1], grid(cv[r])[:, orow, ocol], ALU.mult, ALU.add)
                            if (n, q) != (7, 1):
                                prev[q] = V.tick(last)
                    last.then_inc(up_cv, 1)
                for j in range(2):
                    dve.wait_ge(up_act, i * 2 + j + 1)
                    tt(ffT[:, bass.ds(i * 2 + j, 1), :].rearrange("p a b -> p (a b)"), sil[j], cv[2 * j + 1],
                       ALU.mult).then_inc(ff_rdy, 1)
            V.leave(FT // 2)
            dve.wait_ge(dn_sb, KT + 1)
            normed_residual(4, 3, 5 * KT, mixT).then_inc(out_rdy, 1)

        @block.gpsimd
        def _(pool):
            with pool.Fori(0, PAIRS) as i:
                pool.wait_ge(vt_sb, i + 1)
                pool.sem_inc(seen, 1)
                nc.gpsimd.tensor_copy(VU[1][0:64, :, 0], VU[0][0:64, :, 0]).then_inc(vt_low, 1)
                nc.gpsimd.tensor_copy(VU[1][64:128, :, 1], VU[0][64:128, :, 1]).then_inc(vt_all, 1)


def tiles(w):
    k, n = w.shape
    return w.reshape(k // P, P, n // P, P).transpose(2, 1, 0, 3).reshape(n // P, P, -1)


def columns(v):
    v = v.reshape(v.shape[:-1] + (-1, P))
    return np.moveaxis(v, -1, 0)


def masks():
    s, t = np.arange(C)[:, None], np.arange(C)[None, :]
    two = lambda m: np.concatenate([m, m], axis=0)
    score = np.stack([np.concatenate([two(s < t), two(s <= t)], 1), np.concatenate([two(s > t), two(s >= t)], 1)], 1)
    off = np.zeros((P, 2, LEVELS, C), bool)
    for lv in range(LEVELS):
        b = 1 << lv
        near = (s // (2 * b) == t // (2 * b)) & (s // b != t // b)
        off[:, 0, lv] = two(near & (s < t))
        off[:, 1, lv] = two(near & (s > t))
    scan = np.ones((P, TT), bool)
    scan[:, ::C] = False
    return {"score_mask": score, "off_mask": off, "eye2": two(s == t), "scan_mask": scan,
            "ident": np.eye(P), "ones": np.ones((P, P)), "blk": np.kron(np.eye(2), np.ones((HEAD, HEAD)))}


def host_layout(a):
    w = a["w_in"][0]
    rw, off = D, 3 * D
    o_ic, o_g = off + 2 * LORA, off + 4 * LORA
    o_u = o_g + 256
    o_ga = o_u + 2 * G
    t = {}
    t["cvec"] = np.stack([columns(a["c"][0]), columns(a["c_ctx"])], -1)
    x = np.concatenate([a["x"][0], a["ctx"][0]], 0)
    t["xT_all"] = x.T.reshape(KT, P, TT).transpose(1, 0, 2)
    t["w_mod"] = tiles(a["w_mod"][0])
    t["bmod"] = columns(a["b_mod"][0])
    t["gains"] = np.stack([columns(a[n][0]) for n in ("g_pre1", "g_post1", "g_pre2", "g_post2")], 1)
    rkv = np.stack([tiles(w[:, rw:2 * rw]), tiles(w[:, 0:rw]), tiles(w[:, 2 * rw:3 * rw])], 1)
    t["w_rkv"] = rkv.reshape(3 * PAIRS, P, REG)
    t["w_lora"] = w[:, off:o_g].reshape(KT, P, 4, LORA).transpose(2, 1, 0, 3).reshape(4, P, -1)
    t["w_gate"] = tiles(w[:, o_g:o_u])
    up = np.zeros((PAIRS, P, 6, P), w.dtype)
    for d in range(2):
        up[:, :LORA, d] = a["w_decay_up"][0, d].reshape(LORA, PAIRS, P).transpose(1, 0, 2)
        up[:, :LORA, 2 + d] = a["w_iclr_up"][0, d].reshape(LORA, PAIRS, P).transpose(1, 0, 2)
        up[:, :, 4 + d] = a["w_gate_up"][0, d * P:(d + 1) * P].reshape(P, PAIRS, P).transpose(1, 0, 2)
    t["w_up_lora"] = up
    cv = a["conv_rwkv"][0]
    cl = np.zeros((P, 6, 3), w.dtype)
    for n in range(4):
        cl[:LORA, n] = cv[:, off + n * LORA:off + (n + 1) * LORA].T
    for n in range(2):
        cl[:, 4 + n] = cv[:, o_g + n * P:o_g + (n + 1) * P].T
    t["conv_lora"] = cl
    par = [columns(cv[k, o:o + rw]) for o in (rw, 0, 2 * rw) for k in range(3)]
    par += [columns(a[n][0, d]) for n in ("w0", "a0") for d in range(2)]
    par += [columns(a[n][0].reshape(-1)) for n in ("k_k", "k_a", "r_k", "lnx_g", "lnx_b")]
    t["params"] = np.stack(par, -1)
    t["w_u"] = tiles(w[:, o_u:o_u + G])
    t["w_v"] = w[:, o_u + G:o_ga].reshape(4, 4, P, 2, 512).transpose(3, 0, 2, 1, 4).reshape(8, P, REG)
    t["w_ga"], t["w_gb"] = tiles(w[:, o_ga:o_ga + D]), tiles(w[:, o_ga + D:])
    t["w_pa"], t["w_pb"], t["w_out"] = (tiles(a[n][0]) for n in ("w_proj_a", "w_proj_b", "w_out"))
    t["lnv"] = np.stack([a["ln_v_g"][0], a["ln_v_b"][0]])
    t["b_spatial"] = a["b_spatial"][0]
    t["w_spatial"] = a["w_spatial"][0].transpose(2, 0, 1)
    u = tiles(a["w_up"][0]).reshape(2, FT, P, REG)
    t["w_up"] = u.transpose(1, 0, 2, 3).reshape(2 * FT, P, REG)
    cf = a["conv_ffn"][0].reshape(9, 2, FT // 2, 2, P)
    t["conv_ffn"] = cf.transpose(2, 4, 3, 1, 0).reshape(FT // 2, P, 4, 9)
    dn = a["w_down"][0].reshape(4, FT // 4, P, KT, P)
    t["w_down"] = dn.transpose(3, 0, 2, 1, 4).reshape(4 * KT, P, -1)
    scal = np.zeros((P, 8))
    scal[:, :4] = [RMS_EPS, LN_EPS, LNX_EPS, 0.5 * LN_SHIFT * np.log(2.0)]
    t["scal"] = scal
    t.update(masks())
    return {k: np.ascontiguousarray(v, dtype=np.float32) for k, v in t.items()}


def kernel(**inputs):
    import concourse.bacc as bacc
    from concourse.bass_utils import run_bass_kernel_spmd

    nc = bacc.Bacc("TRN2", target_bir_lowering=False, num_devices=1)
    arrays = host_layout({k: np.asarray(v) for k, v in inputs.items()})
    io = {k: nc.dram_tensor(k + "_dram", v.shape, F32, kind="ExternalInput").ap() for k, v in arrays.items()}
    io["outT"] = nc.dram_tensor("out_dram", (P, KT, T), F32, kind="ExternalOutput").ap()
    layer_kernel(nc, io)
    r = run_bass_kernel_spmd(nc, [{k + "_dram": v for k, v in arrays.items()}], core_ids=[0])
    out = r.results[0]["out_dram"]
    return out.transpose(1, 0, 2).reshape(D, T).T.reshape(1, T, D)
```

```python
from contextlib import ExitStack

import numpy as np
import concourse.bass as bass
from concourse import mybir

F32 = mybir.dt.float32
ALU = mybir.AluOpType
ACT = mybir.ActivationFunctionType

P = 128
D = 2048
KT = D // P
T = 256
TT = 512
HEAD = 64
C = 64
NCH = TT // C
PAIRS = D // P
LORA = 96
G = 1024
GG = G // P
FF = 5632
FT = FF // P
GRID = 64
ROWS = T // GRID
NMOD = 6 * KT
REG = KT * P
LEVELS = 6
DECAY_C = float(np.exp(-0.5))
NCONST = 14
QUAD = P // 4
BODY_STEPS = 65
ARENA = 32100
RMS_EPS = 1e-6
LNX_EPS = 64e-5
LN_EPS = 1e-5
KK_MIN = 1e-24
LN_SHIFT = 20

PK, PR, PV, PW0, PA0, PKK, PKA, PRK, PLG, PLB, PHW0, PHA0, PHKA, POKA = 0, 3, 6, 9, 11, 13, 14, 15, 16, 17, 18, 20, 22, 23
NPAR = 18
NPARX = 24

PHASES = [("mod", (8, 8, 8, 8)), ("lora", (2, 2, 1, 1)), ("pair", (PAIRS, PAIRS, PAIRS, 4 * PAIRS)),
          ("gv", (2, 2, 2, 2)), ("gu", (2, 2, 2, 2)), ("merge", (KT,) * 4), ("out", (4,) * 4),
          ("up", (FT // 2,) * 4), ("down", (KT,) * 4)]


def loads_before(phase):
    total = [0, 0, 0, 0]
    for name, n in PHASES:
        if name == phase:
            return total
        total = [a + b for a, b in zip(total, n)]
    raise ValueError(phase)


def layer_kernel(nc, io):
    ctx = ExitStack()
    with ctx:
        def sb(name, *shape):
            return ctx.enter_context(nc.sbuf_tensor(name, list(shape), F32))

        def bank(name):
            return ctx.enter_context(nc.psum_tensor(name, [P, 512], F32))

        def sem(name):
            return ctx.enter_context(nc.semaphore(name))

        ring = sb("ring", P, 4, REG)
        hT = sb("hT", P, KT, TT)
        arena = sb("arena", P, ARENA)
        ident = sb("ident", P, P)
        ones = sb("ones", P, P)
        blk = sb("blk", P, P)
        score_mask = sb("score_mask", P, 2, P)
        off_mask = sb("off_mask", P, 2, LEVELS, C)
        eye2 = sb("eye2", P, C)
        scan_mask = sb("scan_mask", P, TT)
        modT = sb("modT", P, NMOD, 2)
        bmod = sb("bmod", P, NMOD)
        gains = sb("gains", P, 4, KT)
        scal = sb("scal", P, 8)
        cvec = sb("cvec", P, KT, 2)
        csil = sb("csil", P, KT, 2)
        csilp = sb("csilp", P, KT, QUAD)
        part_sum = sb("part_sum", P, 2)
        params = sb("params", P, PAIRS, NPAR)
        paramx = sb("paramx", P, PAIRS, NPARX)
        par_a = sb("par_a", P, NPARX)
        par_ak = sb("par_ak", P, NPARX)
        par_v = sb("par_v", P, NPARX)
        par_vk = sb("par_vk", P, NPARX)
        par_vo = sb("par_vo", P, NPARX)
        conv_lora = sb("conv_lora", P, 6, 3)
        rstd = sb("rstd", P, TT)
        gcol = sb("gcol", P, KT, 2)

        used = [0]

        def view(*shape):
            n = int(np.prod(shape))
            v = arena[:, used[0]:used[0] + n]
            used[0] += n
            assert used[0] <= ARENA, used
            if len(shape) == 1:
                return v
            names = "abcd"[:len(shape)]
            return v.rearrange("p (" + " ".join(names) + ") -> p " + " ".join(names),
                               **{k: s for k, s in zip(names, shape)})

        lora_act = view(4, TT)
        gate_act = view(2, TT)
        lora_w = view(6, P)
        kx, rx, vx, kkx = view(TT), view(TT), view(TT), view(TT)
        eN = [view(TT) for _ in range(2)]
        kk2, kkn = eN[0], eN[1]
        ew = [view(TT) for _ in range(2)]
        ea = [view(TT) for _ in range(2)]
        cumP = [view(TT) for _ in range(2)]
        eIn = [cumP[0], ew[1]]
        eEx = [ew[0], cumP[1]]
        wcn = view(2, NCH)
        wc = view(2, NCH)
        kdir = [view(TT) for _ in range(2)]
        X = [view(NCH, 2, C) for _ in range(2)]
        KRn = [view(NCH, 2, C) for _ in range(2)]
        KR = [view(NCH, 2, C) for _ in range(2)]
        SC = [[view(NCH, 2, C) for _ in range(2)] for _ in range(2)]
        NL = [view(NCH, C) for _ in range(2)]
        ZU = [view(NCH, C) for _ in range(2)]
        ZL = [view(NCH, C) for _ in range(2)]
        TU = [view(NCH, C) for _ in range(2)]
        XT = [view(NCH, P) for _ in range(2)]
        VU = [view(NCH, 2, C) for _ in range(2)]
        gT = view(T)
        bon = view(T)
        yd = [view(T) for _ in range(2)]
        mod_sb = arena[:, used[0] - 2 * T:used[0]].rearrange("p (a b) -> p a b", b=P)
        rhs_sb = [view(C) for _ in range(2)]
        ST = [[view(HEAD) for _ in range(2)] for _ in range(2)]
        STw = [view(HEAD) for _ in range(2)]
        ra, rb, rc, yr_out = view(T), view(T), view(T), view(T)
        x_sq = arena[:, 8192:8192 + KT * TT].rearrange("p (a b) -> p a b", a=KT)
        used[0] = 0
        yg = view(GG, T)
        vg = view(2, G)
        vrow = view(2, G)
        bsp = view(GG, P)
        wsp = view(GG, P)
        bn = view(2, 2, 6)
        mv = view(2, 2)
        vrs = view(2)
        ug = [view(T) for _ in range(2)]
        vcur = [view(2, P) for _ in range(2)]
        ssp = [view(T) for _ in range(2)]
        sga, sgb = view(T), view(T)
        mta, mtb = view(T), view(T)
        assert used[0] <= 12288
        yr = arena[:, 12288:12288 + KT * T].rearrange("p (a b) -> p a b", a=KT)
        used[0] = 0
        xT = view(KT, T)
        mixT = view(KT, T)
        sq = view(KT, T)
        used[0] = 2 * KT * T
        ffT = view(FT, T)
        convw_a, convw_v = view(4, 9), view(4, 9)
        cv = [view(T) for _ in range(4)]
        sil = [view(T) for _ in range(2)]
        sqd = [view(T) for _ in range(2)]
        mT = arena[:, 22000:22000 + KT * T].rearrange("p (a b) -> p a b", a=KT)
        conv_all = arena[:, 26200:26200 + FT // 2 * 36].rearrange("p (a b c) -> p a b c", b=4, c=9)
        h2T = hT[:, :, T:TT]

        PB = [bank("PB0"), bank("PB1")]
        CH = [bank("CH0"), bank("CH1")]
        Q = [bank(f"Q{n}") for n in range(4)]

        loaded = [sem(f"region{r}_loaded") for r in range(4)]
        used = [sem(f"region{r}_used") for r in range(4)]
        consts_ld = sem("consts_loaded")
        x_ld = sem("x_loaded")
        seen = sem("waits_seen")
        act_step = sem("scalar_steps")
        dve_step = sem("vector_steps")
        phase_v = sem("vector_phase_done")
        cexp_rdy = sem("exp_c_ready")
        csil_rdy = sem("silu_c_ready")
        par_rdy = sem("parameters_ready")
        mod_cp = sem("mod_partials_copied")
        mod_sum = sem("mod_sums_done")
        mod_rdy = sem("mod_rows_ready")
        sq_rdy = sem("squares_ready")
        ssq_ps = sem("square_sums_done")
        rstd_rdy = sem("rstd_ready")
        gcol_rdy = sem("column_gains_ready")
        hc_rdy = sem("h_context_ready")
        h_rdy = sem("h_latents_ready")
        lo_mid = sem("lora_centre_tap_done")
        lo_cv = sem("lora_conv_done")
        lo_act = sem("lora_act_ready")
        lw_ld = sem("lora_up_loaded")
        pair_done = sem("pair_done")
        proj_ps = sem("projection_done")
        pb_free = [sem("proj_bank0_free"), sem("proj_bank1_free")]
        cv_mid = sem("conv_centre_tap_done")
        kk0_rdy = sem("kk_raw_ready")
        kksq_rdy = sem("kk_squares_ready")
        kkr_rdy = sem("kk_rsqrt_ready")
        cum_rdy = sem("decay_sums_ready")
        x_rdy = sem("khat_beta_ready")
        sc_ps = sem("scores_done")
        sc_sb = sem("scores_masked")
        nl_ps = sem("l_rows_done")
        nl_sb = sem("l_rows_masked")
        xt_ps = sem("token_major_done")
        exp_rdy = sem("decay_exps_ready")
        rc_rdy = sem("bonus_product_ready")
        gb_ps = sem("gate_and_bonus_done")
        g_rdy = sem("gate_ready")
        kk_rdy = sem("kk_ready")
        bonv_rdy = sem("bonus_ready")
        kr_cp = sem("kappa_rho_copied")
        yr_stored = sem("rwkv_out_stored")
        yr_free = sem("rwkv_out_buffer_free")
        yr_ld = sem("rwkv_out_reloaded")
        xt_sb = sem("token_major_copied")
        vt_ps = sem("v_token_major_done")
        vt_sb = sem("v_token_major_copied")
        vt_all = sem("v_token_major_both")
        vt_low = sem("v_token_major_lower")
        z_rdy = [sem(f"inverse_ready{d}") for d in range(2)]
        tu_ps = [sem(f"inverse_t_done{d}") for d in range(2)]
        tu_sb = [sem(f"inverse_t_masked{d}") for d in range(2)]
        zz_ps = [sem(f"inverse_z_done{d}") for d in range(2)]
        rhs_ps = [sem(f"rhs_done{d}") for d in range(2)]
        rhs_cp = [sem(f"rhs_copied{d}") for d in range(2)]
        u_ps = [sem(f"u_done{d}") for d in range(2)]
        u_sb = [[sem(f"u_copied{d}{h}") for h in range(2)] for d in range(2)]
        st_ps = [sem(f"state_done{d}") for d in range(2)]
        st_sb = [sem(f"state_updated{d}") for d in range(2)]
        y_ps = [sem(f"y_done{d}") for d in range(2)]
        y_sb = [sem(f"y_copied{d}") for d in range(2)]
        ysum_rdy = sem("y_sum_ready")
        mean_ps = sem("mean_done")
        dev_rdy = sem("deviation_ready")
        dev2_rdy = sem("deviation_squares_ready")
        var_ps = sem("variance_done")
        rs_rdy = sem("readout_rstd_ready")
        late_ld = sem("late_constants_loaded")
        gv_act = sem("gmlp_v_gelu_done")
        gv_st = sem("gmlp_v_stats")
        gv_rs = sem("gmlp_v_rstd")
        vc_rdy = sem("gmlp_v_normed")
        gs_ps = sem("gmlp_spatial_done")
        gu_act = sem("gmlp_u_gelu_done")
        yg_rdy = sem("gmlp_out_ready")
        me_act = sem("merge_gates_ready")
        m_rdy = sem("merged_ready")
        o_sb = sem("w_out_copied")
        xr_ld = sem("x_reloaded")
        up_mid = sem("up_centre_tap_done")
        up_cv = sem("up_conv_done")
        up_act = sem("silu_done")
        ff_rdy = sem("ff_ready")
        dn_sb = sem("down_copied")
        cw_ld = sem("conv_ffn_loaded")
        x1_rdy = sem("x_after_mixer_tile_ready")
        sqt_rdy = sem("square_tile_ready")
        out_rdy = sem("output_ready")
        stored = sem("output_stored")

        def product_count(r, phase, k, i, per):
            return i * per + (loads_before(phase)[r] + k + 2)

        K_, R_, W0, A0, SSQ, W1, A1, V_ = range(8)
        SLOT = (K_, R_, V_)

        def item_count(i, n):
            return i * 4 + (n // 2 + 2)

        def proj_count(i, n):
            return i * 5 + n

        def seg(v):
            return v.rearrange("p (s t) -> p s t", s=2)

        def chunks(v):
            return v.rearrange("p (c t) -> p c t", t=C)

        class Steps:

            def __init__(self, eng, s):
                self.eng, self.sem, self.base, self.n, self.seen = eng, s, 0, 0, 0
                self.fixed = 0

            def tick(self, ins):
                ins.then_inc(self.sem, 1)
                self.n += 1
                return self.n

            def need(self, n):
                if n > self.seen:
                    self.eng.wait_ge(self.sem, self.base + n)
                    self.seen = n

            def enter(self, i, per):
                self.fixed += self.n
                self.base = i * per + self.fixed
                self.n = self.seen = 0
                self.per = per

            def straight(self):
                self.fixed += self.n
                self.base = self.fixed
                self.n = self.seen = 0

            def leave(self, passes):
                assert self.n == self.per, (self.n, self.per)
                self.fixed += self.per * passes
                self.base = self.fixed
                self.n = self.seen = 0

        def lora_tile(n):
            return lora_act[0:LORA, n] if n < 4 else gate_act[:, n - 4]

        four = [PB[0], PB[1], CH[0], CH[1]]

        def chunk_at(d, s):
            return (s + 4) % NCH if d == 0 else NCH - 1 - s

        def wide(v, n):
            return v[:, None, :].to_broadcast([P, n, v.shape[-1]])

        def deep(v, n):
            return v[:, :, None].to_broadcast([P, v.shape[-1], n])

        block = ctx.enter_context(nc.Block())

        @block.sync
        def _(sp):
            def load(r, phase, k, i, per, src):
                sp.wait_ge(used[r], i * per + (loads_before(phase)[r] + k + 1))
                n = src.shape[-1] if len(src.shape) == 2 else None
                p = src.shape[0]
                sp.dma_start(ring[0:p, r, 0:n], src).then_inc(loaded[r], 16)

            sp.dma_start(cvec[:], io["cvec"]).then_inc(consts_ld, 16)
            for t, name in ((ident, "ident"), (ones, "ones"), (blk, "blk"), (score_mask, "score_mask"),
                            (off_mask, "off_mask"), (eye2, "eye2"), (scan_mask, "scan_mask"), (bmod, "bmod"),
                            (gains, "gains"), (params, "params"), (conv_lora, "conv_lora"), (scal, "scal"), (part_sum, "part_sum")):
                sp.dma_start(t[:], io[name]).then_inc(consts_ld, 16)
            sp.dma_start(hT[:], io["xT_all"]).then_inc(x_ld, 16)
            with sp.Fori(0, 8) as i:
                for r in range(4):
                    load(r, "mod", 0, i, 1, io["w_mod"][bass.ds(i * 4 + r, 1)].rearrange("a p n -> (a p) n"))
            for n in range(6):
                w = io["w_lora"][n] if n < 4 else io["w_gate"][n - 4]
                load(n % 4, "lora", n // 4, 0, 0, w[:, :])

            def load_head(n, p):
                load(n, "pair", 0, p, 1, io["w_rkv"][bass.ds(p * 3 + n, 1)].rearrange("a p n -> (a p) n"))

            def load_lora(p):
                sp.dma_start(lora_w[:], io["w_up_lora"][bass.ds(p, 1)].rearrange("a p m n -> (a p) m n")).then_inc(lw_ld, 16)

            for n in range(3):
                load_head(n, 0)
            load_lora(0)
            for n in range(3):
                load_head(n, 1)

            def body(i, more):
                for k in range(4):
                    load(3, "pair", k, i, 4,
                         io["w_mod"][bass.ds(i * 4 + 32 + k, 1)].rearrange("a p n -> (a p) n"))
                    if k == 0 and more == 2:
                        load_head(0, i + 2)
                    if k == 0 and more >= 1:
                        sp.wait_ge(gb_ps, i + 1)
                        load_lora(i + 1)
                    if k == 0 and more == 2:
                        load_head(1, i + 2)
                if more == 2:
                    load_head(2, i + 2)

            with sp.Fori(0, PAIRS - 2) as i:
                body(i, 2)
            body(PAIRS - 2, 1)
            body(PAIRS - 1, 0)
            for h in range(2):
                for r in range(4):
                    load(r, "gv", h, 0, 0, io["w_v"][h * 4 + r])
            sp.wait_ge(pair_done, PAIRS + 1)
            sp.dma_start(vrow[:], io["lnv"].partition_broadcast(P)).then_inc(late_ld, 16)
            sp.dma_start(bsp[:], io["b_spatial"].partition_broadcast(P)).then_inc(late_ld, 16)
            sp.dma_start(wsp[:], io["w_spatial"]).then_inc(late_ld, 16)
            sp.dma_start(conv_all, io["conv_ffn"]).then_inc(cw_ld, 16)
            sp.wait_ge(yr_stored, 16 * PAIRS)
            sp.dma_start(yr, io["yr"]).then_inc(yr_ld, 16)
            with sp.Fori(0, 2) as i:
                for r in range(4):
                    load(r, "gu", 0, i, 1, io["w_u"][bass.ds(i * 4 + r, 1)].rearrange("a p n -> (a p) n"))
            with sp.Fori(0, KT) as i:
                load(0, "merge", 0, i, 1, io["w_ga"][bass.ds(i, 1)].rearrange("a p n -> (a p) n"))
                load(1, "merge", 0, i, 1, io["w_gb"][bass.ds(i, 1)].rearrange("a p n -> (a p) n"))
                load(2, "merge", 0, i, 1, io["w_pa"][bass.ds(i, 1)].rearrange("a p n -> (a p) n"))
                load(3, "merge", 0, i, 1, io["w_pb"][bass.ds(i, 1)].rearrange("a p n -> (a p) n"))
            with sp.Fori(0, 4) as i:
                for r in range(4):
                    load(r, "out", 0, i, 1, io["w_out"][bass.ds(i * 4 + r, 1)].rearrange("a p n -> (a p) n"))
            sp.wait_ge(m_rdy, KT + 1)
            sp.dma_start(xT[:], io["xT_all"][:, :, 0:T]).then_inc(xr_ld, 16)
            with sp.Fori(0, FT // 2) as i:
                for r in range(4):
                    load(r, "up", 0, i, 1, io["w_up"][bass.ds(i * 4 + r, 1)].rearrange("a p n -> (a p) n"))
            with sp.Fori(0, KT) as i:
                for r in range(4):
                    load(r, "down", 0, i, 1, io["w_down"][bass.ds(i * 4 + r, 1)].rearrange("a p n -> (a p) n"))
            for g in range(4):
                sp.wait_ge(out_rdy, 4 * g + 4)
                sp.dma_start(io["outT"][:, 4 * g:4 * g + 4, :], mixT[:, 4 * g:4 * g + 4, :]).then_inc(stored, 16)
            sp.wait_ge(stored, 64)

        @block.tensor
        def _(pe):
            mm = nc.tensor.matmul

            def region(r, phase, k, i, per):
                pe.wait_ge(loaded[r], i * (16 * per) + 16 * (loads_before(phase)[r] + k + 1))

            def tile(r, kt, m=P):
                return ring[:, r, kt * m:(kt + 1) * m]

            def small():
                pe.sem_inc(seen, 1)

            for r in range(4):
                pe.sem_inc(used[r], 1)
            pe.sem_inc(proj_ps, 1)
            pe.sem_inc(pair_done, 1)
            pe.sem_inc(rs_rdy, 1)
            pe.sem_inc(kr_cp, 2)
            pe.sem_inc(yr_free, 1)

            def mod_tile(r, psum, n):
                for kt in range(KT):
                    q = kt % 4
                    last = mm(psum[QUAD * q:QUAD * (q + 1), n * P:(n + 1) * P], csilp[:, kt, :], tile(r, kt),
                              start=(kt < 4), stop=(kt >= KT - 4))
                last.then_inc(used[r], 1)
                return last

            def mod_sums(psum):
                for n in range(4):
                    last = mm(psum[:, 2 * n:2 * n + 2], mod_sb[:, n], part_sum[:, :], start=True, stop=True)
                last.then_inc(mod_sum, 1)

            def sum_squares(src, n, out):
                pe.wait_ge(sq_rdy, n)
                for kt in range(KT):
                    last = mm(out, ones[:, :], src[:, kt, :], start=(kt == 0), stop=(kt == KT - 1))
                last.then_inc(ssq_ps, 1)

            pe.wait_ge(consts_ld, 16 * NCONST)
            pe.wait_ge(csil_rdy, 1)
            pe.sem_inc(mod_cp, 1)
            pe.sem_inc(mod_rdy, 1)
            pe.sem_inc(mod_sum, 1)

            def mod_four(i):
                pe.wait_ge(mod_cp, i + 1)
                for r in range(4):
                    region(r, "mod", 0, i, 1)
                    mod_tile(r, Q[0], r)
                pe.sem_inc(seen, 1)
                pe.wait_ge(mod_cp, i + 2)
                pe.wait_ge(mod_rdy, i + 1)
                mod_sums(Q[2])

            mod_four(0)
            mod_four(1)
            sum_squares(x_sq, 1, Q[1][:, :])
            with pe.Fori(2, 8) as i:
                mod_four(i)

            for n in range(6):
                r = n % 4
                region(r, "lora", n // 4, 0, 0)
                if n >= 2:
                    pe.wait_ge(lo_cv, n - 1)
                m = LORA if n < 4 else P
                for kt in range(KT):
                    if n == 0:
                        pe.wait_ge(h_rdy, kt + 1)
                        pe.wait_ge(hc_rdy, kt + 1)
                    last = mm(PB[n % 2][0:m, :], tile(r, kt, m), hT[:, kt, :], start=(kt == 0), stop=(kt == KT - 1))
                last.then_inc(used[r], 1)
            pe.wait_ge(lo_cv, 6)
            pe.wait_ge(lo_act, 4)
            pe.sem_inc(pb_free[0], 1)
            pe.sem_inc(pb_free[1], 1)

            def project(p, n, lo=0, hi=KT):
                slot = SLOT[n]
                if lo == 0:
                    pe.wait_ge(pb_free[slot % 2], p * 4 + (slot // 2 + 1))
                    region(n, "pair", 0, p, 1)
                for kt in range(lo, hi):
                    last = mm(PB[slot % 2][:, :], tile(n, kt), hT[:, kt, :], start=(kt == 0), stop=(kt == KT - 1))
                if hi == KT:
                    last.then_inc(used[n], 1)

            def item(p, n):
                if n == W0:
                    pe.wait_ge(lw_ld, p * 16 + 16)
                pe.wait_ge(pb_free[n % 2], p * 4 + (n // 2 + 1))
                if n == SSQ:
                    pe.wait_ge(kksq_rdy, p + 1)
                    mm(PB[SSQ % 2][:, :], blk[:, :], kk2, start=True, stop=True).then_inc(proj_ps, 1)
                else:
                    j = {W0: 0, A0: 2, W1: 1, A1: 3}[n]
                    mm(PB[n % 2][:, :], lora_w[0:LORA, j, :], lora_act[0:LORA, j, :],
                       start=True, stop=True).then_inc(proj_ps, 1)

            def between(p, k):
                if k < 5:
                    item(p, (W0, A0, SSQ, W1, A1)[k])
                else:
                    project(p, 2, k - 5, k - 4)

            def body(i, more):
                pe.wait_ge(pb_free[V_ % 2], item_count(i, V_))
                for ch in range(NCH):
                    for h in range(2):
                        hr = slice(64 * h, 64 * h + 64)
                        last = mm(CH[0][hr, ch * C:(ch + 1) * C], vx[:, ch * C:(ch + 1) * C], ident[:, hr],
                                  start=True, stop=True)
                last.then_inc(vt_ps, 1)
                pe.wait_ge(rc_rdy, i + 1)
                mm(CH[1][:, 0:T], blk[:, :], rc, start=True, stop=True)
                for k in range(2):
                    last = mm(CH[1][:, T:2 * T], lora_w[:, 4 + k, :], gate_act[:, k, 0:T], start=(k == 0), stop=(k == 1))
                last.then_inc(gb_ps, 1)
                pe.wait_ge(rs_rdy, i + 1)
                for d in range(2):
                    pe.wait_ge(x_rdy, i * 2 + d + 1)
                    if d == 1:
                        pe.wait_ge(nl_sb, i * 2 + 1)
                        pe.wait_ge(xt_sb, i * 4 + 2)
                    for s in range(2):
                        for c in range(4):
                            for h in range(2):
                                rows = slice(64 * h, 64 * h + 64)
                                ch = 4 * s + c
                                last = mm(Q[2 * s + h][:, c * P:(c + 1) * P], X[d][rows, ch], KRn[d][rows, ch],
                                          start=True, stop=True)
                        last.then_inc(sc_ps, 1)
                    if more >= 1:
                        project(i + 1, 1, *((6, 10), (12, 14))[d])
                    for s in range(2):
                        pe.wait_ge(sc_sb, i * 4 + 2 * d + s + 1)
                        for c in range(4):
                            ch = 4 * s + c
                            last = nc.tensor.transpose(Q[2 * s + 1][:, c * P:(c + 1) * P], X[d][:, ch], ident[:, :])
                        last.then_inc(xt_ps, 1)
                    for ch in range(NCH):
                        for h in range(2):
                            rows, orow = slice(64 * h, 64 * h + 64), slice(64 - 64 * h, 128 - 64 * h)
                            last = mm(Q[0][orow, ch * C:(ch + 1) * C], KRn[d][rows, ch, 0], X[d][rows, ch, 1 - h],
                                      start=True, stop=True)
                    last.then_inc(nl_ps, 1)
                    if more >= 1:
                        project(i + 1, 1, *((10, 12), (14, KT))[d])
                pe.wait_ge(xt_sb, i * 4 + 4)
                pe.wait_ge(nl_sb, i * 2 + 2)
                pe.wait_ge(bonv_rdy, i + 1)
                pe.wait_ge(g_rdy, i + 1)
                for lv in range(LEVELS - 1):
                    for d in range(2):
                        pe.wait_ge(z_rdy[d], i * LEVELS + lv + 1)
                        small()
                        for ch in range(NCH):
                            for h in range(2):
                                hr = slice(64 - 64 * h, 128 - 64 * h)
                                last = mm(Q[2 * d][hr, ch * C:(ch + 1) * C], NL[d][hr, ch], ZU[d][hr, ch],
                                          start=True, stop=True)
                        last.then_inc(tu_ps[d], 1)
                    if more >= 1:
                        between(i + 1, 3 * lv)
                    for d in range(2):
                        pe.wait_ge(tu_sb[d], i * (LEVELS - 1) + lv + 1)
                        small()
                        for ch in range(NCH):
                            for h in range(2):
                                hr = slice(64 - 64 * h, 128 - 64 * h)
                                last = mm(Q[2 * d + 1][hr, ch * C:(ch + 1) * C], ZL[d][hr, ch], TU[d][hr, ch],
                                          start=True, stop=True)
                        if lv < LEVELS - 2:
                            for ch in range(NCH):
                                for h in range(2):
                                    hr = slice(64 - 64 * h, 128 - 64 * h)
                                    last = mm(Q[2 * d][hr, ch * C:(ch + 1) * C], TU[d][hr, ch], ZL[d][hr, ch],
                                              start=True, stop=True)
                        last.then_inc(zz_ps[d], 1)
                        if lv and d == 1:
                            region(3, "pair", lv - 1, i, 4)
                            mod_tile(3, CH[1], lv - 1)
                        if more >= 1:
                            between(i + 1, 3 * lv + 1 + d)
                pe.wait_ge(vt_all, i + 1)
                pe.wait_ge(kr_cp, i * 2 + 4)
                pe.wait_ge(mod_cp, i + 10)
                for s in range(NCH):
                    if more >= 1 and 1 <= s <= 6:
                        project(i + 1, 2, s + 9, s + 10)
                    for d in range(2):
                        ch = chunk_at(d, s)
                        if s:
                            pe.wait_ge(st_sb[d], i * 7 + s)
                        else:
                            pe.wait_ge(z_rdy[d], i * LEVELS + LEVELS)
                        small()
                        for h in range(2):
                            rows, orow = slice(64 * h, 64 * h + 64), slice(64 - 64 * h, 128 - 64 * h)
                            last = mm(CH[d][orow, 0:C], SC[d][h][rows, ch, 0], VU[d][rows, ch, h],
                                      start=True, stop=(s == 0))
                            if s:
                                last = mm(CH[d][orow, 0:C], KR[d][rows, ch, 0], ST[d][s % 2][rows, :],
                                          start=False, stop=True)
                        last.then_inc(rhs_ps[d], 1)
                    if s == 0:
                        mod_sums(Q[3])
                    if more == 2:
                        project(i + 2, 0, 2 * s, 2 * s + 1)
                    for d in range(2):
                        ch = chunk_at(d, s)
                        pe.wait_ge(rhs_cp[d], i * NCH + s + 1)
                        small()
                        for h in range(2):
                            hr = slice(64 - 64 * h, 128 - 64 * h)
                            last = mm(CH[d][hr, C:2 * C], ZU[d][hr, ch], rhs_sb[d][hr, :], start=True, stop=True)
                        last.then_inc(u_ps[d], 1)
                    if more == 2:
                        project(i + 2, 0, 2 * s + 1, 2 * s + 2)
                    for d in range(2):
                        ch = chunk_at(d, s)
                        for h in range(2):
                            pe.wait_ge(u_sb[d][h], i * NCH + s + 1)
                        if s < NCH - 1:
                            for h in range(2):
                                last = mm(CH[d][64 * h:64 * h + 64, 2 * C:3 * C], XT[d][:, ch, 64 * h:64 * h + 64],
                                          VU[d][:, ch, h], start=True, stop=True)
                            last.then_inc(st_ps[d], 1)
                    for d in range(2):
                        ch = chunk_at(d, s)
                        if s >= 4:
                            if s > 4:
                                pe.wait_ge(y_sb[d], i * 4 + s - 4)
                            for h in range(2):
                                rows = slice(64 * h, 64 * h + 64)
                                mm(Q[2 * d][rows, 0:C], VU[d][:, ch, h], SC[d][h][:, ch, 1], start=True, stop=False)
                            for h in range(2):
                                rows = slice(64 * h, 64 * h + 64)
                                last = mm(Q[2 * d][rows, 0:C], ST[d][s % 2][rows, :], KR[d][rows, ch, 1],
                                          start=False, stop=True)
                            last.then_inc(y_ps[d], 1)
                if more == 2:
                    project(i + 2, 1, 0, 3)
                pe.wait_ge(ysum_rdy, i + 1)
                mm(Q[0][:, 0:T], blk[:, :], ra, start=True, stop=True).then_inc(mean_ps, 1)
                if more == 2:
                    project(i + 2, 1, 3, 6)
                pe.wait_ge(dev2_rdy, i + 1)
                mm(Q[1][:, 0:T], blk[:, :], rb, start=True, stop=True).then_inc(var_ps, 1)

            project(0, 0)
            project(0, 1)
            for n in range(W0, V_):
                item(0, n)
            project(0, 2)
            project(1, 0)
            project(1, 1, 0, 6)
            with pe.Fori(0, PAIRS - 2) as i:
                body(i, 2)
            body(PAIRS - 2, 1)
            body(PAIRS - 1, 0)

            pe.wait_ge(pair_done, PAIRS + 1)
            for h in range(2):
                for r in range(4):
                    region(r, "gv", h, 0, 0)
                    for k in range(4):
                        kt = 4 * r + k
                        for n in range(2):
                            last = mm(Q[2 * h + n][:, :], hT[:, kt, n * P:(n + 1) * P],
                                      ring[:, r, k * 512:(k + 1) * 512], start=(kt == 0), stop=(kt == KT - 1))
                    last.then_inc(used[r], 1)
            pe.wait_ge(late_ld, 48)
            pe.sem_inc(yg_rdy, 2)
            pe.sem_inc(gs_ps, 2)
            with pe.Fori(0, 2) as i:
                for r in range(4):
                    region(r, "gu", 0, i, 1)
                    pe.wait_ge(yg_rdy, i * 4 + r + 1)
                    for kt in range(KT):
                        last = mm(PB[r % 2][:, 0:T], tile(r, kt), hT[:, kt, 0:T], start=(kt == 0), stop=(kt == KT - 1))
                    last.then_inc(used[r], 1)
                    pe.wait_ge(vc_rdy, i * 4 + r + 1)
                    for n in range(2):
                        last = mm(CH[r % 2][:, n * P:(n + 1) * P], vcur[r % 2][:, n],
                                  wsp[:, bass.ds(i * 4 + r, 1), :].rearrange("p a b -> p (a b)"), start=True, stop=True)
                    last.then_inc(gs_ps, 1)
            pe.wait_ge(yg_rdy, GG + 2)
            pe.wait_ge(yr_ld, 16)
            pe.sem_inc(me_act, 2)
            pe.sem_inc(m_rdy, 1)
            with pe.Fori(0, KT) as i:
                for r in range(4):
                    region(r, "merge", 0, i, 1)
                    if r < 2:
                        pe.wait_ge(me_act, i * 2 + r + 1)
                    else:
                        pe.wait_ge(m_rdy, i + 1)
                    src, n = ((hT, KT), (hT, KT), (yr, KT), (yg, GG))[r]
                    for kt in range(n):
                        last = mm(Q[r][:, 0:T], tile(r, kt), src[:, kt, 0:T], start=(kt == 0), stop=(kt == n - 1))
                    last.then_inc(used[r], 1)
            pe.wait_ge(m_rdy, KT + 1)
            pe.sem_inc(o_sb, 4)

            def add_square(src, first=False, last=False):
                m = mm(Q[0][:, 0:T], ones[:, :], src, start=first, stop=last)
                if last:
                    m.then_inc(ssq_ps, 1)

            def out_four(i, first):
                for r in range(4):
                    region(r, "out", 0, i, 1)
                    pe.wait_ge(o_sb, i * 4 + r + 1)
                    for kt in range(KT):
                        last = mm(four[r][:, 0:T], tile(r, kt), mT[:, kt, :], start=(kt == 0), stop=(kt == KT - 1))
                    last.then_inc(used[r], 1)
                    if r or not first:
                        pe.wait_ge(o_sb, i * 4 + r + 4)
                        add_square(sq[:, bass.ds(i * 4 + r - 1, 1), :].rearrange("p a b -> p (a b)"),
                                   first=first and r == 1)

            out_four(0, True)
            with pe.Fori(1, 4) as i:
                out_four(i, False)
            pe.wait_ge(o_sb, KT + 4)
            add_square(sq[:, KT - 1, :], last=True)
            for kt in range(KT):
                pe.wait_ge(sqt_rdy, kt + 1)
                add_square(sq[:, kt, :], first=kt == 0, last=kt == KT - 1)
            pe.sem_inc(up_cv, 2)
            pe.sem_inc(ff_rdy, 2)

            def up_four(i, first):
                for r in range(4):
                    region(r, "up", 0, i, 1)
                    pe.wait_ge(up_cv, i * 2 + 1 + r // 2)
                    for kt in range(KT):
                        if first and r == 0:
                            pe.wait_ge(h_rdy, KT + kt + 1)
                        last = mm(four[r][:, 0:T], tile(r, kt), h2T[:, kt, :], start=(kt == 0), stop=(kt == KT - 1))
                    last.then_inc(used[r], 1)

            up_four(0, True)
            with pe.Fori(1, FT // 2) as i:
                up_four(i, False)
            pe.wait_ge(ff_rdy, FT + 2)
            pe.sem_inc(dn_sb, 2)

            def down_two(i, first):
                for q in range(2):
                    pe.wait_ge(dn_sb, i * 2 + q + 1)
                    for r in range(4):
                        region(r, "down", q, i, 2)
                        for k in range(FT // 4):
                            kt = r * (FT // 4) + k
                            last = mm(Q[2 + q][:, 0:T], tile(r, k), ffT[:, kt, :], start=(kt == 0), stop=(kt == FT - 1))
                        last.then_inc(used[r], 1)
                    if q or not first:
                        pe.wait_ge(dn_sb, i * 2 + q + 2)
                        add_square(sqd[1 - q], first=first)

            down_two(0, True)
            with pe.Fori(1, KT // 2) as i:
                down_two(i, False)
            pe.wait_ge(dn_sb, KT + 2)
            add_square(sqd[1], last=True)

        @block.scalar
        def _(act):
            A = Steps(act, act_step)
            f = nc.scalar.activation

            def product(r, phase, k, i, per):
                act.wait_ge(used[r], product_count(r, phase, k, i, per))

            def rms(n, out, psum, width):
                act.wait_ge(ssq_ps, n)
                A.need(A.tick(f(out, psum, ACT.Ln, scale=1.0 / D, bias=scal[:, 0:1])))
                f(out, out, ACT.Exp, scale=-0.5).then_inc(rstd_rdy, 1)

            act.preload_act_table_set("natural_log_exp_and_others")
            act.wait_ge(consts_ld, 16 * NCONST)
            f(csil[:], cvec[:], ACT.Exp, scale=-1.0).then_inc(cexp_rdy, 1)
            act.wait_ge(x_ld, 16)
            f(x_sq, hT[:], ACT.Square).then_inc(sq_rdy, 1)

            def mod_copy(i):
                product(3, "mod", 0, i, 1)
                act.wait_ge(mod_sum, i + 1)
                f(mod_sb, Q[0][:, :].rearrange("p (a b) -> p a b", b=P), ACT.Copy).then_inc(mod_cp, 1)

            mod_copy(0)
            mod_copy(1)
            rms(1, rstd[:, :], Q[1][:, :], TT)
            with act.Fori(2, 8) as i:
                mod_copy(i)
            act.wait_ge(gcol_rdy, 1)
            for kt in range(KT):
                f(hT[:, kt, T:TT], hT[:, kt, T:TT], ACT.Identity, scale=gcol[:, kt, 1:2],
                  bias=modT[:, kt, 1:2]).then_inc(hc_rdy, 1)
            for n in range(6):
                m = LORA if n < 4 else P
                product(n % 4, "lora", n // 4, 0, 0)
                f(lora_tile(n), PB[n % 2][0:m, :], ACT.Identity, scale=conv_lora[0:m, n, 1:2]).then_inc(lo_mid, 1)
            act.wait_ge(lo_cv, 6)
            for n in range(2):
                f(lora_act[0:LORA, n], lora_act[0:LORA, n], ACT.Tanh).then_inc(lo_act, 1)
            for n in range(4, 6):
                f(gate_act[:, n - 4], gate_act[:, n - 4], ACT.Sigmoid).then_inc(lo_act, 1)
            act.wait_ge(par_rdy, 1)

            def centre(p, n, par):
                product(n, "pair", 0, p, 1)
                c = (PK, PR, PV)[n]
                f((kx, rx, vx)[n], PB[SLOT[n] % 2][:, :], ACT.Identity, scale=par[:, c + 1:c + 2]).then_inc(cv_mid, 1)

            def fetch(par, p):
                A.need(A.tick(f(par[:, :], paramx[:, bass.ds(p, 1), :].rearrange("p a b -> p (a b)"), ACT.Copy)))

            def inputs(p):
                act.wait_ge(kk0_rdy, p + 1)
                f(kk2, kkx, ACT.Square).then_inc(kksq_rdy, 1)
                for n, out, c in ((W0, ew[0], PHW0), (A0, ea[0], PHA0), (W1, ew[1], PHW0 + 1), (A1, ea[1], PHA0 + 1)):
                    act.wait_ge(proj_ps, proj_count(p, n))
                    f(out, PB[n % 2][:, :], ACT.Tanh, scale=0.5, bias=par_a[:, c:c + 1]).then_inc(pb_free[n % 2], 1)
                act.preload_act_table_set("natural_log_exp_and_others")
                act.wait_ge(pb_free[SSQ % 2], item_count(p, SSQ))
                A.need(A.tick(f(kkn, kkn, ACT.Ln, scale=float(2 ** LN_SHIFT))))
                f(kkn, kkn, ACT.Exp, scale=-0.5, bias=scal[:, 3:4]).then_inc(kkr_rdy, 1)
                for d in range(2):
                    sign = -DECAY_C if d == 0 else DECAY_C
                    act.wait_ge(cum_rdy, p * 2 + d + 1)
                    f(wcn[:, d, :], chunks(cumP[d])[:, :, C - 1], ACT.Exp, scale=-DECAY_C)
                    if d == 1:
                        act.wait_ge(kk_rdy, p + 1)
                    A.need(A.tick(f(eN[d], eIn[d], ACT.Exp, scale=-sign)))
                    f(eIn[d], eIn[d], ACT.Exp, scale=sign)
                    f(eEx[d], eEx[d], ACT.Exp, scale=sign).then_inc(exp_rdy, 1)

            fetch(par_a, 0)
            centre(0, 0, par_a)
            centre(0, 1, par_a)
            inputs(0)
            centre(0, 2, par_a)
            act.wait_ge(x_rdy, 2)
            fetch(par_ak, 1)
            centre(1, 0, par_ak)

            def body(i, more):
                act.wait_ge(pair_done, i + 1)
                if more >= 1:
                    fetch(par_a, i + 1)
                act.wait_ge(vt_ps, i + 1)
                for h in range(2):
                    hr = slice(64 * h, 64 * h + 64)
                    last = f(VU[0][hr, :, h], chunks(CH[0][hr, :]), ACT.Copy)
                last.then_inc(vt_sb, 1)
                act.wait_ge(gb_ps, i + 1)
                act.wait_ge(bonv_rdy, i + 1)
                f(gT, CH[1][:, T:2 * T], ACT.Copy).then_inc(g_rdy, 1)
                for d in range(2):
                    for s in range(2):
                        act.wait_ge(xt_ps, i * 4 + 2 * d + s + 1)
                        f(XT[d][:, 4 * s:4 * s + 4], Q[2 * s + 1][:, :].rearrange("p (c n) -> p c n", c=4),
                          ACT.Copy).then_inc(xt_sb, 1)
                if more >= 1:
                    act.wait_ge(x_rdy, i * 2 + 2)
                    centre(i + 1, 1, par_a)
                    inputs(i + 1)
                product(3, "pair", 3, i, 4)
                f(mod_sb, CH[1][:, :].rearrange("p (a b) -> p a b", b=P), ACT.Copy).then_inc(mod_cp, 1)
                for s in range(NCH):
                    act.wait_ge(rhs_ps[1], i * NCH + s + 1)
                    f(rhs_sb[1], CH[1][:, 0:C], ACT.Copy).then_inc(rhs_cp[1], 1)
                    for d in range(2):
                        act.wait_ge(u_ps[d], i * NCH + s + 1)
                        f(VU[d][0:64, chunk_at(d, s), 1], CH[d][0:64, C:2 * C], ACT.Copy, scale=-1.0).then_inc(u_sb[d][1], 1)
                    if s >= 4:
                        for d in range(2):
                            ch = chunk_at(d, s)
                            act.wait_ge(y_ps[d], i * 4 + s - 3)
                            f(yd[d][:, ch * C:(ch + 1) * C], Q[2 * d][:, 0:C], ACT.Copy).then_inc(y_sb[d], 1)
                    if more >= 1 and s == NCH - 2:
                        centre(i + 1, 2, par_a)
                if more == 2:
                    act.wait_ge(x_rdy, i * 2 + 4)
                    fetch(par_ak, i + 2)
                    centre(i + 2, 0, par_ak)
                act.wait_ge(dev_rdy, i + 1)
                f(rb, ra, ACT.Square).then_inc(dev2_rdy, 1)
                act.wait_ge(var_ps, i + 1)
                A.need(A.tick(f(rb, Q[1][:, 0:T], ACT.Ln, scale=1.0 / HEAD, bias=scal[:, 2:3])))
                f(rb, rb, ACT.Exp, scale=-0.5).then_inc(rs_rdy, 1)

            with act.Fori(0, PAIRS - 2) as i:
                A.enter(i, 6)
                body(i, 2)
            A.leave(PAIRS - 2)
            body(PAIRS - 2, 1)
            body(PAIRS - 1, 0)

            act.wait_ge(pair_done, PAIRS + 1)
            for h in range(2):
                product(3, "gv", h, 0, 0)
                for n in range(2):
                    f(vg[:, n, h * 512:(h + 1) * 512], Q[2 * h + n][:, :], ACT.Gelu).then_inc(gv_act, 1)
            act.wait_ge(gv_st, 2)
            A.need(A.tick(f(vrs, mv[:, :, 1], ACT.Ln, bias=scal[:, 1:2])))
            f(vrs, vrs, ACT.Exp, scale=-0.5).then_inc(gv_rs, 1)
            act.preload_act_table(ACT.Gelu)
            with act.Fori(0, 2) as i:
                for r in range(4):
                    act.wait_ge(yg_rdy, i * 4 + r + 1)
                    product(r, "gu", 0, i, 1)
                    f(ug[r % 2], PB[r % 2][:, 0:T], ACT.Gelu).then_inc(gu_act, 1)
            act.preload_act_table(ACT.Sigmoid)
            with act.Fori(0, KT) as i:
                act.wait_ge(m_rdy, i + 1)
                for r, o in ((0, sga), (1, sgb)):
                    product(r, "merge", 0, i, 1)
                    f(o, Q[r][:, 0:T], ACT.Sigmoid).then_inc(me_act, 1)
            act.wait_ge(m_rdy, KT + 1)
            with act.Fori(0, 4) as i:
                for r in range(4):
                    product(r, "out", 0, i, 1)
                    at = bass.ds(i * 4 + r, 1)
                    f(mixT[:, at, :].rearrange("p a b -> p (a b)"), four[r][:, 0:T], ACT.Copy)
                    f(sq[:, at, :].rearrange("p a b -> p (a b)"), four[r][:, 0:T], ACT.Square).then_inc(o_sb, 1)
            rms(2, rstd[:, 0:T], Q[0][:, 0:T], T)
            for kt in range(KT):
                act.wait_ge(x1_rdy, kt + 1)
                f(sq[:, kt, :], xT[:, kt, :], ACT.Square).then_inc(sqt_rdy, 1)
            rms(3, rstd[:, 0:T], Q[0][:, 0:T], T)
            act.preload_act_table(ACT.Silu)
            act.wait_ge(cw_ld, 16)
            A.straight()
            with act.Fori(0, FT // 2) as i:
                A.enter(i, 1)
                A.need(A.tick(f(convw_a, conv_all[:, bass.ds(i, 1)].rearrange("p a m n -> p (a m) n"), ACT.Copy)))
                for r in range(4):
                    product(r, "up", 0, i, 1)
                    if r % 2 == 0:
                        act.wait_ge(ff_rdy, i * 2 + r // 2 + 1)
                    f(cv[r], four[r][:, 0:T], ACT.Identity, scale=convw_a[:, r, 4:5]).then_inc(up_mid, 1)
                for j in range(2):
                    act.wait_ge(up_cv, i * 2 + j + 3)
                    f(sil[j], cv[2 * j], ACT.Silu).then_inc(up_act, 1)
            A.leave(FT // 2)
            with act.Fori(0, KT // 2) as i:
                for q in range(2):
                    product(3, "down", q, i, 2)
                    f(mixT[:, bass.ds(i * 2 + q, 1), :].rearrange("p a b -> p (a b)"), Q[2 + q][:, 0:T], ACT.Copy)
                    f(sqd[q], Q[2 + q][:, 0:T], ACT.Square).then_inc(dn_sb, 1)
            rms(4, rstd[:, 0:T], Q[0][:, 0:T], T)

        @block.vector
        def _(dve):
            V = Steps(dve, dve_step)
            tt, ts, stt = nc.vector.tensor_tensor, nc.vector.tensor_scalar, nc.vector.scalar_tensor_tensor

            def product(r, phase, k, i, per):
                dve.wait_ge(used[r], product_count(r, phase, k, i, per))

            def flow(*ins):
                for x in ins:
                    V.need(V.tick(x))

            dve.wait_ge(consts_ld, 16 * NCONST)
            V.tick(nc.vector.tensor_copy(paramx[:, :, 0:NPAR], params[:]))
            V.tick(ts(paramx[:, :, PHW0:PHW0 + 4], params[:, :, PW0:PW0 + 4], 0.5, None, ALU.mult))
            V.tick(ts(paramx[:, :, PHKA:PHKA + 1], params[:, :, PKA:PKA + 1], 0.5, None, ALU.mult))
            ts(paramx[:, :, POKA:POKA + 1], params[:, :, PKA:PKA + 1], -0.5, 1.0, ALU.mult, ALU.add).then_inc(par_rdy, 1)
            dve.wait_ge(cexp_rdy, 1)
            flow(ts(csil[:], csil[:], 1.0, None, ALU.add))
            flow(nc.vector.reciprocal(csil[:], csil[:]))
            z = V.tick(nc.vector.memset(csilp[:], 0.0))
            V.need(z)
            tt(csilp[:, :, 0:2], csil[:], cvec[:], ALU.mult).then_inc(csil_rdy, 1)

            def mod_out(psum, at):
                return tt(modT[:, bass.ds(at, 4), :], psum.rearrange("p (a b) -> p a b", a=4),
                          bmod[:, bass.ds(at, 4)][:, :, None].to_broadcast([P, 4, 2]), ALU.add)

            def mod_add(i):
                dve.wait_ge(mod_sum, i + 2)
                mod_out(Q[2][:, 0:8], i * 4).then_inc(mod_rdy, 1)

            mod_add(0)
            mod_add(1)
            dve.wait_ge(rstd_rdy, 1)
            V.tick(tt(hT[:], hT[:], wide(rstd[:, :], KT), ALU.mult))
            with dve.Fori(2, 8) as i:
                mod_add(i)
            dve.wait_ge(mod_rdy, 9)
            V.need(V.n)
            stt(gcol[:], modT[:, KT:2 * KT, :], 1.0, deep(gains[:, 0, :], 2), ALU.add, ALU.mult).then_inc(gcol_rdy, 1)
            dve.wait_ge(gcol_rdy, 1)
            for kt in range(KT):
                ts(hT[:, kt, 0:T], hT[:, kt, 0:T], gcol[:, kt, 0:1], modT[:, kt, 0:1], ALU.mult, ALU.add).then_inc(h_rdy, 1)

            def side_taps(x, psum, w):
                flow(stt(x[:, :, 1:T], psum[:, :, 0:T - 1], w[0], x[:, :, 1:T], ALU.mult, ALU.add))
                return stt(x[:, :, 0:T - 1], psum[:, :, 1:T], w[2], x[:, :, 0:T - 1], ALU.mult, ALU.add)

            for n in range(6):
                m = LORA if n < 4 else P
                dve.wait_ge(lo_mid, n + 1)
                side_taps(seg(lora_tile(n)), seg(PB[n % 2][0:m, :]),
                          [conv_lora[0:m, n, k:k + 1] for k in range(3)]).then_inc(lo_cv, 1)
            dve.wait_ge(par_rdy, 1)

            def par(c):
                return par_v[:, c:c + 1]

            def fetch(par_t, p):
                V.need(V.tick(nc.vector.tensor_copy(par_t[:, :], paramx[:, bass.ds(p, 1), :].rearrange("p a b -> p (a b)"))))

            def outer(p, n, par_t):
                c = (PK, PR, PV)[n]
                dve.wait_ge(cv_mid, cv_count(p, n))
                side_taps(seg((kx, rx, vx)[n]), seg(PB[SLOT[n] % 2][:, :]),
                          [par_t[:, c:c + 1], None, par_t[:, c + 2:c + 3]]).then_inc(pb_free[SLOT[n] % 2], 1)

            def cv_count(p, n):
                if n == 0:
                    return 1 if isinstance(p, int) and p == 0 else p * 3 + 1
                return p * 3 + n + 1

            def times(out, x, y):
                return tt(out, chunks(x), chunks(y), ALU.mult)

            def inputs(p, n):
                if n == 0:
                    ts(kkx, kx, par(PKK), None, ALU.mult).then_inc(kk0_rdy, 1)
                if n in (1, 3):
                    d = n // 2
                    dve.wait_ge(pb_free[d], item_count(p, (W0, W1)[d]))
                    flow(ts(ew[d], ew[d], 0.5, 0.5, ALU.mult, ALU.add))
                    flow(nc.vector.tensor_tensor_scan(cumP[d], scan_mask[:, :], ew[d], 0.0, ALU.mult, ALU.add))
                if n == 2:
                    dve.wait_ge(proj_ps, proj_count(p, SSQ))
                    ts(kkn, PB[SSQ % 2][:, :], KK_MIN, None, ALU.max).then_inc(pb_free[SSQ % 2], 1)
                if n in (2, 4):
                    d = n // 2 - 1
                    tt(ew[d], cumP[d], ew[d], ALU.subtract).then_inc(cum_rdy, 1)
                    dve.wait_ge(pb_free[1 - d], item_count(p, (A0, A1)[d]))
                    m = V.tick(ts(kdir[d], ea[d], par(PHKA), par(POKA), ALU.mult, ALU.add))
                    V.tick(ts(ea[d], ea[d], 0.5, 0.5, ALU.mult, ALU.add))
                    V.need(m)
                    V.tick(tt(kdir[d], kdir[d], kx, ALU.mult))
                if n == 5:
                    V.need(V.n)
                    flow(tt(rc, kdir[0][:, 0:T], kdir[1][:, 0:T], ALU.add))
                    stt(rc, rc, par(PRK), rx[:, 0:T], ALU.mult, ALU.mult).then_inc(rc_rdy, 1)
                    dve.wait_ge(kkr_rdy, p + 1)
                    tt(kkx, kkx, kkn, ALU.mult).then_inc(kk_rdy, 1)
                if n == 6:
                    dve.wait_ge(kk_rdy, p + 1)
                    V.tick(tt(ea[0], ea[0], kkx, ALU.mult))
                    V.tick(tt(ea[1], ea[1], kkx, ALU.mult))
                    dve.wait_ge(kr_cp, p * 2 + 2)
                if n in (7, 9):
                    d = n // 2 - 3
                    dve.wait_ge(exp_rdy, p * 2 + d + 1)
                    V.tick(times(KRn[d][:, :, 0], kkx, eEx[d]))
                    V.tick(times(KRn[d][:, :, 1], rx, eIn[d]))
                if n in (8, 9):
                    d = n - 8
                    V.need(V.n)
                    for h in range(2):
                        rows = slice(64 * h, 64 * h + 64)
                        V.tick(times(X[d][rows, :, h], kdir[d][rows, :], eN[d][rows, :]))
                        last = times(X[d][rows, :, 1 - h], ea[d][rows, :], eN[d][rows, :])
                        if h == 0:
                            V.tick(last)
                    last.then_inc(x_rdy, 1)

            def body(i, more):
                fetch(par_vo, i)
                if more >= 1:
                    fetch(par_v, i + 1)
                dve.wait_ge(exp_rdy, i * 2 + 2)
                V.tick(nc.vector.tensor_copy(wc[:], wcn[:]))
                dve.wait_ge(gb_ps, i + 1)
                tt(bon, CH[1][:, 0:T], vx[:, 0:T], ALU.mult).then_inc(bonv_rdy, 1)
                for d in range(2):
                    for s in range(2):
                        dve.wait_ge(sc_ps, i * 4 + 2 * d + s + 1)
                        for h in range(2):
                            last = tt(SC[d][h][:, 4 * s:4 * s + 4].rearrange("p c a t -> p c (a t)"),
                                      Q[2 * s + h][:, :].rearrange("p (c n) -> p c n", c=4),
                                      wide(score_mask[:, d, :], 4), ALU.mult)
                            if h == 0:
                                V.tick(last)
                        last.then_inc(sc_sb, 1)
                    dve.wait_ge(sc_sb, i * 4 + 2 * d + 2)
                    for h in range(2):
                        hr = slice(64 - 64 * h, 128 - 64 * h)
                        m = V.tick(tt(TU[d][hr], SC[d][h][hr, :, 0],
                                      off_mask[hr, d, 0, :][:, None, :].to_broadcast([64, NCH, C]), ALU.mult))
                    V.need(m)
                    flow(tt(ZU[d], wide(eye2[:, :], NCH), TU[d], ALU.subtract))
                    dve.wait_ge(nl_ps, i * 2 + d + 1)
                    tt(NL[d], chunks(Q[0][:, :]), wide(score_mask[:, 1 - d, 0:C], NCH), ALU.mult).then_inc(nl_sb, 1)
                    dve.wait_ge(nl_sb, i * 2 + d + 1)
                    flow(tt(TU[d], NL[d], wide(off_mask[:, 1 - d, 0, :], NCH), ALU.mult))
                    tt(ZL[d], wide(eye2[:, :], NCH), TU[d], ALU.subtract).then_inc(z_rdy[d], 1)
                if more >= 1:
                    outer(i + 1, 1, par_v)
                for lv in range(LEVELS - 1):
                    for d in range(2):
                        dve.wait_ge(tu_ps[d], i * (LEVELS - 1) + lv + 1)
                        tt(TU[d], chunks(Q[2 * d][:, :]), wide(off_mask[:, d, lv + 1, :], NCH), ALU.mult).then_inc(tu_sb[d], 1)
                    if more >= 1:
                        inputs(i + 1, 2 * lv)
                    for d in range(2):
                        dve.wait_ge(zz_ps[d], i * (LEVELS - 1) + lv + 1)
                        last = tt(ZU[d], ZU[d], chunks(Q[2 * d + 1][:, :]), ALU.subtract)
                        if lv < LEVELS - 2:
                            V.tick(last)
                            last = tt(ZL[d], ZL[d], chunks(Q[2 * d][:, :]), ALU.subtract)
                        last.then_inc(z_rdy[d], 1)
                    if more >= 1:
                        inputs(i + 1, 2 * lv + 1)
                for s in range(NCH):
                    dve.wait_ge(rhs_ps[0], i * NCH + s + 1)
                    nc.vector.tensor_copy(rhs_sb[0], CH[0][:, 0:C]).then_inc(rhs_cp[0], 1)
                    if s == 1:
                        dve.wait_ge(mod_sum, i + 10)
                        mod_out(Q[3][:, 0:8], i * 4 + 32).then_inc(mod_rdy, 1)
                    nxt = chunk_at(1, min(s + 1, NCH - 1))
                    decay = [wc[:, 0, chunk_at(0, s):chunk_at(0, s) + 1], wc[:, 1, nxt:nxt + 1]]
                    if 0 < s < NCH - 1:
                        for d in range(2):
                            dve.wait_ge(st_sb[d], i * 7 + s)
                            w = V.tick(ts(STw[d], ST[d][s % 2], decay[d], None, ALU.mult))
                    for d in range(2):
                        dve.wait_ge(u_ps[d], i * NCH + s + 1)
                        ts(VU[d][64:128, chunk_at(d, s), 0], CH[d][64:128, C:2 * C], -1.0, None, ALU.mult).then_inc(u_sb[d][0], 1)
                    if s < NCH - 1:
                        for d in range(2):
                            dve.wait_ge(st_ps[d], i * 7 + s + 1)
                            new, psum = ST[d][(s + 1) % 2], CH[d][:, 2 * C:3 * C]
                            if s == 0:
                                last = ts(new, psum, decay[d], None, ALU.mult)
                            else:
                                V.need(w)
                                last = stt(new, psum, decay[d], STw[d], ALU.mult, ALU.add)
                            last.then_inc(st_sb[d], 1)
                    if more >= 1 and s == NCH - 2:
                        outer(i + 1, 2, par_v)
                for d in range(2):
                    dve.wait_ge(y_sb[d], i * 4 + 4)
                tt(ra, yd[0], yd[1], ALU.add).then_inc(ysum_rdy, 1)
                if more == 2:
                    fetch(par_vk, i + 2)
                    outer(i + 2, 0, par_vk)
                dve.wait_ge(mean_ps, i + 1)
                stt(ra, Q[0][:, 0:T], -1.0 / HEAD, ra, ALU.mult, ALU.add).then_inc(dev_rdy, 1)
                dve.wait_ge(rs_rdy, i + 2)
                flow(tt(ra, ra, rb, ALU.mult))
                flow(ts(ra, ra, par_vo[:, PLG:PLG + 1], par_vo[:, PLB:PLB + 1], ALU.mult, ALU.add))
                dve.wait_ge(bonv_rdy, i + 1)
                flow(tt(ra, ra, bon, ALU.add))
                dve.wait_ge(g_rdy, i + 1)
                dve.wait_ge(yr_free, i + 1)
                tt(yr_out, ra, gT, ALU.mult).then_inc(pair_done, 1)

            fetch(par_v, 0)
            outer(0, 0, par_v)
            outer(0, 1, par_v)
            dve.wait_ge(pb_free[0], item_count(0, K_))
            dve.wait_ge(pb_free[1], item_count(0, R_))
            for n in range(10):
                inputs(0, n)
            outer(0, 2, par_v)
            fetch(par_vk, 1)
            outer(1, 0, par_vk)
            V.straight()
            with dve.Fori(0, PAIRS - 2) as i:
                V.enter(i, BODY_STEPS)
                body(i, 2)
            V.leave(PAIRS - 2)
            body(PAIRS - 2, 1)
            body(PAIRS - 1, 0)

            dve.wait_ge(pair_done, PAIRS + 1)
            dve.wait_ge(gv_act, 4)
            for n in range(2):
                for h in range(2):
                    m = V.tick(nc.vector.bn_stats(bn[:, n, h, :], vg[:, n, h * 512:(h + 1) * 512]))
            V.need(m)
            for n in range(2):
                nc.vector.bn_aggr(mv[:, n, :], bn[:, n].rearrange("p a b -> p (a b)")).then_inc(gv_st, 1)
            dve.wait_ge(gv_rs, 1)
            for n in range(2):
                flow(ts(vg[:, n], vg[:, n], mv[:, n, 0:1], vrs[:, n:n + 1], ALU.subtract, ALU.mult))
            dve.wait_ge(late_ld, 48)
            with dve.Fori(0, 2) as i:
                V.enter(i, 8)
                for r in range(4):
                    at = (i * 4 + r) * P
                    dve.wait_ge(gs_ps, i * 4 + r + 1)
                    flow(tt(vcur[r % 2], vg[:, :, bass.ds(at, P)],
                            vrow[:, 0, bass.ds(at, P)][:, None, :].to_broadcast([P, 2, P]), ALU.mult))
                    tt(vcur[r % 2], vcur[r % 2], vrow[:, 1, bass.ds(at, P)][:, None, :].to_broadcast([P, 2, P]),
                       ALU.add).then_inc(vc_rdy, 1)
                    dve.wait_ge(gs_ps, i * 4 + r + 3)
                    flow(tt(ssp[r % 2].rearrange("p (a b) -> p a b", a=2),
                            CH[r % 2][:, 0:T].rearrange("p (a b) -> p a b", a=2),
                            bsp[:, bass.ds(i * 4 + r, 1), :].to_broadcast([P, 2, P]), ALU.add))
                    dve.wait_ge(gu_act, i * 4 + r + 1)
                    tt(yg[:, bass.ds(i * 4 + r, 1), :].rearrange("p a b -> p (a b)"), ssp[r % 2], ug[r % 2],
                       ALU.mult).then_inc(yg_rdy, 1)
            V.leave(2)
            with dve.Fori(0, KT) as i:
                V.enter(i, 2)
                for r, o, g in ((2, mta, sga), (3, mtb, sgb)):
                    product(r, "merge", 0, i, 1)
                    dve.wait_ge(me_act, i * 2 + r + 1)
                    m = V.tick(tt(o, g, Q[r][:, 0:T], ALU.mult))
                V.need(m)
                tt(mT[:, bass.ds(i, 1), :].rearrange("p a b -> p (a b)"), mta, mtb, ALU.add).then_inc(m_rdy, 1)
            V.leave(KT)

            def normed_residual(n, gain, at, out, done):
                flow(tt(gcol[:, :, 0], modT[:, at:at + KT, 0], gains[:, gain, :], ALU.mult))
                dve.wait_ge(rstd_rdy, n)
                m = [0] * KT
                for kt in range(KT + 1):
                    if kt < KT:
                        m[kt] = V.tick(stt(mixT[:, kt, :], mixT[:, kt, :], gcol[:, kt, 0:1], rstd[:, 0:T], ALU.mult, ALU.mult))
                    if kt:
                        V.need(m[kt - 1])
                        tt(out[:, kt - 1, :], xT[:, kt - 1, :], mixT[:, kt - 1, :], ALU.add).then_inc(done, 1)

            dve.wait_ge(xr_ld, 16)
            stt(gcol[:, :, 1], modT[:, 4 * KT:5 * KT, 0], 1.0, gains[:, 2, :], ALU.add, ALU.mult)
            normed_residual(2, 1, 2 * KT, xT, x1_rdy)
            dve.wait_ge(rstd_rdy, 3)
            for kt in range(KT + 1):
                if kt < KT:
                    m1 = V.tick(stt(h2T[:, kt, :], xT[:, kt, :], gcol[:, kt, 1:2], rstd[:, 0:T], ALU.mult, ALU.mult))
                if kt:
                    V.need(m0)
                    ts(h2T[:, kt - 1, :], h2T[:, kt - 1, :], modT[:, 3 * KT + kt - 1, 0:1], None, ALU.add).then_inc(h_rdy, 1)
                m0 = m1

            def grid(v):
                return v.rearrange("p (r c) -> p r c", r=ROWS)

            side = [(a, b) for a in (-1, 0, 1) for b in (-1, 0, 1) if (a, b) != (0, 0)]
            dve.wait_ge(cw_ld, 16)
            with dve.Fori(0, FT // 2) as i:
                V.enter(i, 31)
                V.need(V.tick(nc.vector.tensor_copy(convw_v, conv_all[:, bass.ds(i, 1)].rearrange("p a m n -> p (a m) n"))))
                for j in range(2):
                    dve.wait_ge(up_mid, i * 4 + 2 * j + 2)
                    prev = [0, 0]
                    for n, (a, b) in enumerate(side):
                        for q in range(2):
                            r = 2 * j + q
                            orow, irow = slice(max(0, -a), ROWS - max(0, a)), slice(max(0, a), ROWS - max(0, -a))
                            ocol, icol = slice(max(0, -b), GRID - max(0, b)), slice(max(0, b), GRID - max(0, -b))
                            if n:
                                V.need(prev[q])
                            w = 3 * (a + 1) + b + 1
                            last = stt(grid(cv[r])[:, orow, ocol], grid(four[r][:, 0:T])[:, irow, icol],
                                       convw_v[:, r, w:w + 1], grid(cv[r])[:, orow, ocol], ALU.mult, ALU.add)
                            if (n, q) != (7, 1):
                                prev[q] = V.tick(last)
                    last.then_inc(up_cv, 1)
                for j in range(2):
                    dve.wait_ge(up_act, i * 2 + j + 1)
                    tt(ffT[:, bass.ds(i * 2 + j, 1), :].rearrange("p a b -> p (a b)"), sil[j], cv[2 * j + 1],
                       ALU.mult).then_inc(ff_rdy, 1)
            V.leave(FT // 2)
            normed_residual(4, 3, 5 * KT, mixT, out_rdy)

        @block.gpsimd
        def _(pool):
            with pool.Fori(0, PAIRS) as i:
                pool.wait_ge(pair_done, i + 1)
                pool.wait_ge(x_rdy, i * 2 + 2)
                pool.sem_inc(seen, 1)
                for d in range(2):
                    nc.gpsimd.tensor_copy(KR[d], KRn[d]).then_inc(kr_cp, 1)
                pool.wait_ge(vt_sb, i + 1)
                pool.wait_ge(kr_cp, i * 2 + 4)
                pool.sem_inc(seen, 1)
                nc.gpsimd.tensor_copy(VU[1][0:64, :, 0], VU[0][0:64, :, 0]).then_inc(vt_low, 1)
                nc.gpsimd.tensor_copy(VU[1][64:128, :, 1], VU[0][64:128, :, 1]).then_inc(vt_all, 1)
                pool.wait_ge(pair_done, i + 2)
                pool.sem_inc(seen, 1)
                pool.dma_start(io["yr"][:, bass.ds(i, 1), :].rearrange("p a b -> p (a b)"), yr_out).then_inc(yr_stored, 16)
                pool.wait_ge(yr_stored, i * 16 + 16)
                pool.sem_inc(yr_free, 1)


def tiles(w):
    k, n = w.shape
    return w.reshape(k // P, P, n // P, P).transpose(2, 1, 0, 3).reshape(n // P, P, -1)


def columns(v):
    v = v.reshape(v.shape[:-1] + (-1, P))
    return np.moveaxis(v, -1, 0)


def masks():
    s, t = np.arange(C)[:, None], np.arange(C)[None, :]
    two = lambda m: np.concatenate([m, m], axis=0)
    score = np.stack([np.concatenate([two(s < t), two(s <= t)], 1), np.concatenate([two(s > t), two(s >= t)], 1)], 1)
    off = np.zeros((P, 2, LEVELS, C), bool)
    for lv in range(LEVELS):
        b = 1 << lv
        near = (s // (2 * b) == t // (2 * b)) & (s // b != t // b)
        off[:, 0, lv] = two(near & (s < t))
        off[:, 1, lv] = two(near & (s > t))
    scan = np.ones((P, TT), bool)
    scan[:, ::C] = False
    return {"score_mask": score, "off_mask": off, "eye2": two(s == t), "scan_mask": scan,
            "part_sum": np.eye(QUAD)[np.arange(P) % QUAD][:, :2], "ident": np.eye(P), "ones": np.ones((P, P)), "blk": np.kron(np.eye(2), np.ones((HEAD, HEAD)))}


def host_layout(a):
    w = a["w_in"][0]
    rw, off = D, 3 * D
    o_ic, o_g = off + 2 * LORA, off + 4 * LORA
    o_u = o_g + 256
    o_ga = o_u + 2 * G
    t = {}
    t["cvec"] = np.stack([columns(a["c"][0]), columns(a["c_ctx"])], -1)
    x = np.concatenate([a["x"][0], a["ctx"][0]], 0)
    t["xT_all"] = x.T.reshape(KT, P, TT).transpose(1, 0, 2)
    t["w_mod"] = tiles(a["w_mod"][0])
    t["bmod"] = columns(a["b_mod"][0])
    t["gains"] = np.stack([columns(a[n][0]) for n in ("g_pre1", "g_post1", "g_pre2", "g_post2")], 1)
    rkv = np.stack([tiles(w[:, rw:2 * rw]), tiles(w[:, 0:rw]), tiles(w[:, 2 * rw:3 * rw])], 1)
    t["w_rkv"] = rkv.reshape(3 * PAIRS, P, REG)
    t["w_lora"] = w[:, off:o_g].reshape(KT, P, 4, LORA).transpose(2, 1, 0, 3).reshape(4, P, -1)
    t["w_gate"] = tiles(w[:, o_g:o_u])
    up = np.zeros((PAIRS, P, 6, P), w.dtype)
    for d in range(2):
        up[:, :LORA, d] = a["w_decay_up"][0, d].reshape(LORA, PAIRS, P).transpose(1, 0, 2)
        up[:, :LORA, 2 + d] = a["w_iclr_up"][0, d].reshape(LORA, PAIRS, P).transpose(1, 0, 2)
        up[:, :, 4 + d] = a["w_gate_up"][0, d * P:(d + 1) * P].reshape(P, PAIRS, P).transpose(1, 0, 2)
    t["w_up_lora"] = up
    cv = a["conv_rwkv"][0]
    cl = np.zeros((P, 6, 3), w.dtype)
    for n in range(4):
        cl[:LORA, n] = cv[:, off + n * LORA:off + (n + 1) * LORA].T
    for n in range(2):
        cl[:, 4 + n] = cv[:, o_g + n * P:o_g + (n + 1) * P].T
    t["conv_lora"] = cl
    par = [columns(cv[k, o:o + rw]) for o in (rw, 0, 2 * rw) for k in range(3)]
    par += [columns(a[n][0, d]) for n in ("w0", "a0") for d in range(2)]
    par += [columns(a[n][0].reshape(-1)) for n in ("k_k", "k_a", "r_k", "lnx_g", "lnx_b")]
    t["params"] = np.stack(par, -1)
    t["w_u"] = tiles(w[:, o_u:o_u + G])
    t["w_v"] = w[:, o_u + G:o_ga].reshape(4, 4, P, 2, 512).transpose(3, 0, 2, 1, 4).reshape(8, P, REG)
    t["w_ga"], t["w_gb"] = tiles(w[:, o_ga:o_ga + D]), tiles(w[:, o_ga + D:])
    t["w_pa"], t["w_pb"], t["w_out"] = (tiles(a[n][0]) for n in ("w_proj_a", "w_proj_b", "w_out"))
    t["lnv"] = np.stack([a["ln_v_g"][0], a["ln_v_b"][0]])
    t["b_spatial"] = a["b_spatial"][0]
    t["w_spatial"] = a["w_spatial"][0].transpose(2, 0, 1)
    u = tiles(a["w_up"][0]).reshape(2, FT, P, REG)
    t["w_up"] = u.transpose(1, 0, 2, 3).reshape(2 * FT, P, REG)
    cf = a["conv_ffn"][0].reshape(9, 2, FT // 2, 2, P)
    t["conv_ffn"] = cf.transpose(4, 2, 3, 1, 0).reshape(P, FT // 2, 4, 9)
    dn = a["w_down"][0].reshape(4, FT // 4, P, KT, P)
    t["w_down"] = dn.transpose(3, 0, 2, 1, 4).reshape(4 * KT, P, -1)
    scal = np.zeros((P, 8))
    scal[:, :4] = [RMS_EPS, LN_EPS, LNX_EPS, 0.5 * LN_SHIFT * np.log(2.0)]
    t["scal"] = scal
    t.update(masks())
    return {k: np.ascontiguousarray(v, dtype=np.float32) for k, v in t.items()}


def kernel(**inputs):
    import concourse.bacc as bacc
    from concourse.bass_utils import run_bass_kernel_spmd

    nc = bacc.Bacc("TRN2", target_bir_lowering=False, num_devices=1)
    arrays = host_layout({k: np.asarray(v) for k, v in inputs.items()})
    io = {k: nc.dram_tensor(k + "_dram", v.shape, F32, kind="ExternalInput").ap() for k, v in arrays.items()}
    io["outT"] = nc.dram_tensor("out_dram", (P, KT, T), F32, kind="ExternalOutput").ap()
    io["yr"] = nc.dram_tensor("yr_scratch", (P, KT, T), F32).ap()
    layer_kernel(nc, io)
    r = run_bass_kernel_spmd(nc, [{k + "_dram": v for k, v in arrays.items()}], core_ids=[0])
    out = r.results[0]["out_dram"]
    return out.transpose(1, 0, 2).reshape(D, T).T.reshape(1, T, D)
```

```python
from contextlib import ExitStack

import numpy as np
import concourse.bass as bass
from concourse import mybir

F32 = mybir.dt.float32
F32R = mybir.dt.float32r
ALU = mybir.AluOpType
ACT = mybir.ActivationFunctionType

P = 128
D = 2048
KT = D // P
T = 256
TT = 512
HEAD = 64
C = 64
NCH = TT // C
PAIRS = D // P
LORA = 96
G = 1024
GG = G // P
FF = 5632
FT = FF // P
GRID = 64
ROWS = T // GRID
NMOD = 6 * KT
REG = KT * P
LEVELS = 6
DECAY_C = float(np.exp(-0.5))
NCONST = 14
QUAD = P // 4
BODY_STEPS = 65
ARENA = 32100
RMS_EPS = 1e-6
LNX_EPS = 64e-5
LN_EPS = 1e-5
KK_MIN = 1e-24
LN_SHIFT = 20

PK, PR, PV, PW0, PA0, PKK, PKA, PRK, PLG, PLB, PHW0, PHA0, PHKA, POKA = 0, 3, 6, 9, 11, 13, 14, 15, 16, 17, 18, 20, 22, 23
NPAR = 18
NPARX = 24

PHASES = [("mod", (8, 8, 8, 8)), ("lora", (2, 2, 1, 1)), ("pair", (PAIRS, PAIRS, PAIRS, 4 * PAIRS)),
          ("gv", (2, 2, 2, 2)), ("gu", (2, 2, 2, 2)), ("merge", (KT,) * 4), ("out", (4,) * 4),
          ("up", (FT // 2,) * 4), ("down", (KT,) * 4)]

SPLIT = {"gu": 0, "merge": GG, "out": GG + 4 * KT, "up": GG + 5 * KT, "down": GG + 5 * KT + 2 * FT}
POOL_COLS = 4 * P


def width(phase, r):
    if phase == "down":
        return FT // 4 * P
    return G if (phase, r) == ("merge", 3) else REG


def loads_before(phase):
    total = [0, 0, 0, 0]
    for name, n in PHASES:
        if name == phase:
            return total
        total = [a + b for a, b in zip(total, n)]
    raise ValueError(phase)


def layer_kernel(nc, io):
    ctx = ExitStack()
    with ctx:
        def sb(name, *shape):
            return ctx.enter_context(nc.sbuf_tensor(name, list(shape), F32))

        def bank(name):
            return ctx.enter_context(nc.psum_tensor(name, [P, 512], F32))

        def sem(name):
            return ctx.enter_context(nc.semaphore(name))

        at_ring = (nc.sbuf_base + 31) // 32 * 32
        ring = sb("ring", P, 4, REG)
        at_hT = nc.sbuf_base
        hT = sb("hT", P, KT, TT)
        at_arena = nc.sbuf_base
        arena = sb("arena", P, ARENA)

        def rounded(name, base, offset, *shape):
            return nc.alloc_sbuf_tensor_at(name, [P, *shape], F32R, offset=base + 4 * offset)

        ident = sb("ident", P, P)
        ones = sb("ones", P, P)
        blk = sb("blk", P, P)
        score_mask = sb("score_mask", P, 2, P)
        off_mask = sb("off_mask", P, 2, LEVELS, C)
        eye2 = sb("eye2", P, C)
        scan_mask = sb("scan_mask", P, TT)
        modT = sb("modT", P, NMOD, 2)
        bmod = sb("bmod", P, NMOD)
        gains = sb("gains", P, 4, KT)
        scal = sb("scal", P, 8)
        cvec = sb("cvec", P, KT, 2)
        csil = sb("csil", P, KT, 2)
        csilp = sb("csilp", P, KT, QUAD)
        part_sum = sb("part_sum", P, 2)
        params = sb("params", P, PAIRS, NPAR)
        paramx = sb("paramx", P, PAIRS, NPARX)
        par_a = sb("par_a", P, NPARX)
        par_ak = sb("par_ak", P, NPARX)
        par_v = sb("par_v", P, NPARX)
        par_vk = sb("par_vk", P, NPARX)
        par_vo = sb("par_vo", P, NPARX)
        conv_lora = sb("conv_lora", P, 6, 3)
        rstd = sb("rstd", P, TT)
        gcol = sb("gcol", P, KT, 2)

        top = [0]

        def view(*shape):
            n = int(np.prod(shape))
            v = arena[:, top[0]:top[0] + n]
            top[0] += n
            assert top[0] <= ARENA, top
            if len(shape) == 1:
                return v
            names = "abcd"[:len(shape)]
            return v.rearrange("p (" + " ".join(names) + ") -> p " + " ".join(names),
                               **{k: s for k, s in zip(names, shape)})

        lora_act = view(4, TT)
        gate_act = view(2, TT)
        lora_w = view(6, P)
        kx, rx, vx, kkx = view(TT), view(TT), view(TT), view(TT)
        eN = [view(TT) for _ in range(2)]
        kk2, kkn = eN[0], eN[1]
        ew = [view(TT) for _ in range(2)]
        ea = [view(TT) for _ in range(2)]
        cumP = [view(TT) for _ in range(2)]
        eIn = [cumP[0], ew[1]]
        eEx = [ew[0], cumP[1]]
        wcn = view(2, NCH)
        wc = view(2, NCH)
        kdir = [view(TT) for _ in range(2)]
        X = [view(NCH, 2, C) for _ in range(2)]
        KRn = [view(NCH, 2, C) for _ in range(2)]
        KR = [view(NCH, 2, C) for _ in range(2)]
        SC = [[view(NCH, 2, C) for _ in range(2)] for _ in range(2)]
        NL = [view(NCH, C) for _ in range(2)]
        ZU = [view(NCH, C) for _ in range(2)]
        ZL = [view(NCH, C) for _ in range(2)]
        TU = [view(NCH, C) for _ in range(2)]
        XT = [view(NCH, P) for _ in range(2)]
        VU = [view(NCH, 2, C) for _ in range(2)]
        gT = view(T)
        bon = view(T)
        yd = [view(T) for _ in range(2)]
        mod_sb = arena[:, top[0] - 2 * T:top[0]].rearrange("p (a b) -> p a b", b=P)
        rhs_sb = [view(C) for _ in range(2)]
        ST = [[view(HEAD) for _ in range(2)] for _ in range(2)]
        STw = [view(HEAD) for _ in range(2)]
        ra, rb, rc, yr_out = view(T), view(T), view(T), view(T)
        x_sq = arena[:, 8192:8192 + KT * TT].rearrange("p (a b) -> p a b", a=KT)
        def at(offset, *shape):
            top[0] = offset
            return view(*shape)

        xT = at(0, KT, T)
        yg_lo = at(GG * T, GG, T)
        w_hi = at(KT * T, 2, REG)
        FFA = KT * T + 2 * REG
        vg = at(FFA, 2, G)
        vrow = view(2, G)
        bsp = view(GG, P)
        wsp = view(GG, P)
        bn = view(2, 2, 6)
        mv = view(2, 2)
        vrs = view(2)
        ug = [view(T) for _ in range(2)]
        vcur = [view(2, P) for _ in range(2)]
        ssp = [view(T) for _ in range(2)]
        assert top[0] <= FFA + 2 * KT * T
        m_lo = at(FFA + KT * T, KT, T)
        sq = view(KT, T)
        yr = at(FFA + 3 * KT * T, KT, T)
        top[0] += KT * T
        sga, sgb = view(T), view(T)
        mta, mtb = view(T), view(T)
        assert top[0] <= FFA + 2 * FT * T
        ff_lo = at(FFA + FT * T, FT, T)
        conv_all = view(FT // 2, 4, 9)
        convw_a, convw_v = view(4, 9), view(4, 9)
        sqd = [view(T) for _ in range(2)]
        off_flat = off_mask[:].rearrange("p a b c -> p (a b c)")
        cv = [off_flat[:, n * T:(n + 1) * T] for n in range(3)] + [scan_mask[:, 0:T]]
        sil = [scan_mask[:, T:2 * T], score_mask[:].rearrange("p a b -> p (a b)")]
        mixT = hT[:, :, 0:T]
        x_out = w_hi.rearrange("p a b -> p (a b)").rearrange("p (a b) -> p a b", a=KT)
        h2_lo = hT[:, :, 0:T]
        w_hi_r = rounded("w_hi_r", at_arena, KT * T, 2, REG)
        w_lo_r = rounded("w_lo_r", at_ring, 0, 4, REG)
        yg_hi_r = rounded("yg_hi_r", at_arena, 0, GG, T)
        yg_lo_r = rounded("yg_lo_r", at_arena, GG * T, GG, T)
        m_hi_r = rounded("m_hi_r", at_arena, FFA, KT, T)
        m_lo_r = rounded("m_lo_r", at_arena, FFA + KT * T, KT, T)
        h_hi_r = rounded("h_hi_r", at_arena, FFA + 2 * KT * T, KT, T)
        yr_lo_r = rounded("yr_lo_r", at_arena, FFA + 3 * KT * T, KT, T)
        yr_hi_r = rounded("yr_hi_r", at_arena, FFA + 4 * KT * T, KT, T)
        ff_hi_r = rounded("ff_hi_r", at_arena, FFA, FT, T)
        ff_lo_r = rounded("ff_lo_r", at_arena, FFA + FT * T, FT, T)
        hT_r = rounded("hT_r", at_hT, 0, KT, TT)
        h_lo_r = hT_r[:, :, T:TT]
        h2_lo_r, h2_hi_r = hT_r[:, :, 0:T], hT_r[:, :, T:TT]

        def as_f32(v):
            return v.bitcast(F32)

        PB = [bank("PB0"), bank("PB1")]
        CH = [bank("CH0"), bank("CH1")]
        Q = [bank(f"Q{n}") for n in range(4)]

        loaded = [sem(f"region{r}_loaded") for r in range(4)]
        used = [sem(f"region{r}_used") for r in range(4)]
        consts_ld = sem("consts_loaded")
        x_ld = sem("x_loaded")
        seen = sem("waits_seen")
        act_step = sem("scalar_steps")
        dve_step = sem("vector_steps")
        cexp_rdy = sem("exp_c_ready")
        csil_rdy = sem("silu_c_ready")
        par_rdy = sem("parameters_ready")
        mod_cp = sem("mod_partials_copied")
        mod_sum = sem("mod_sums_done")
        mod_rdy = sem("mod_rows_ready")
        sq_rdy = sem("squares_ready")
        ssq_ps = sem("square_sums_done")
        rstd_rdy = sem("rstd_ready")
        gcol_rdy = sem("column_gains_ready")
        hc_rdy = sem("h_context_ready")
        h_rdy = sem("h_latents_ready")
        lo_mid = sem("lora_centre_tap_done")
        lo_cv = sem("lora_conv_done")
        lo_act = sem("lora_act_ready")
        lw_ld = sem("lora_up_loaded")
        pair_done = sem("pair_done")
        proj_ps = sem("projection_done")
        pb_free = [sem("proj_bank0_free"), sem("proj_bank1_free")]
        cv_mid = sem("conv_centre_tap_done")
        kk0_rdy = sem("kk_raw_ready")
        kksq_rdy = sem("kk_squares_ready")
        kkr_rdy = sem("kk_rsqrt_ready")
        cum_rdy = sem("decay_sums_ready")
        x_rdy = sem("khat_beta_ready")
        sc_ps = sem("scores_done")
        sc_sb = sem("scores_masked")
        nl_ps = sem("l_rows_done")
        nl_sb = sem("l_rows_masked")
        xt_ps = sem("token_major_done")
        exp_rdy = sem("decay_exps_ready")
        rc_rdy = sem("bonus_product_ready")
        gb_ps = sem("gate_and_bonus_done")
        g_rdy = sem("gate_ready")
        kk_rdy = sem("kk_ready")
        bonv_rdy = sem("bonus_ready")
        kr_cp = sem("kappa_rho_copied")
        yr_stored = sem("rwkv_out_stored")
        yr_free = sem("rwkv_out_buffer_free")
        yr_ld = sem("rwkv_out_reloaded")
        xt_sb = sem("token_major_copied")
        vt_ps = sem("v_token_major_done")
        vt_sb = sem("v_token_major_copied")
        vt_all = sem("v_token_major_both")
        z_rdy = [sem(f"inverse_ready{d}") for d in range(2)]
        tu_ps = [sem(f"inverse_t_done{d}") for d in range(2)]
        tu_sb = [sem(f"inverse_t_masked{d}") for d in range(2)]
        zz_ps = [sem(f"inverse_z_done{d}") for d in range(2)]
        rhs_ps = [sem(f"rhs_done{d}") for d in range(2)]
        rhs_cp = [sem(f"rhs_copied{d}") for d in range(2)]
        u_ps = [sem(f"u_done{d}") for d in range(2)]
        u_sb = [[sem(f"u_copied{d}{h}") for h in range(2)] for d in range(2)]
        st_ps = [sem(f"state_done{d}") for d in range(2)]
        st_sb = [sem(f"state_updated{d}") for d in range(2)]
        y_ps = [sem(f"y_done{d}") for d in range(2)]
        y_sb = [sem(f"y_copied{d}") for d in range(2)]
        ysum_rdy = sem("y_sum_ready")
        mean_ps = sem("mean_done")
        dev_rdy = sem("deviation_ready")
        dev2_rdy = sem("deviation_squares_ready")
        var_ps = sem("variance_done")
        rs_rdy = sem("readout_rstd_ready")
        late_ld = sem("late_constants_loaded")
        hi_rdy = sem("weight_high_ready")
        lo_rdy = sem("weight_low_ready")
        hh_rdy = sem("h_high_ready")
        hl_rdy = sem("h_low_ready")
        yrh_rdy = sem("rwkv_high_ready")
        yrl_rdy = sem("rwkv_low_ready")
        pool_hi = sem("activation_high_ready")
        pool_lo = sem("activation_low_ready")
        up_lo = sem("up_weight_low_ready")
        h2_raw = sem("h2_ready")
        h2h_rdy = sem("h2_high_ready")
        gv_act = sem("gmlp_v_gelu_done")
        gv_st = sem("gmlp_v_stats")
        gv_rs = sem("gmlp_v_rstd")
        vc_rdy = sem("gmlp_v_normed")
        gs_ps = sem("gmlp_spatial_done")
        gu_act = sem("gmlp_u_gelu_done")
        yg_rdy = sem("gmlp_out_ready")
        me_act = sem("merge_gates_ready")
        m_rdy = sem("merged_ready")
        o_sb = sem("w_out_copied")
        xr_ld = sem("x_reloaded")
        up_mid = sem("up_centre_tap_done")
        up_cv = sem("up_conv_done")
        up_act = sem("silu_done")
        ff_rdy = sem("ff_ready")
        dn_sb = sem("down_copied")
        cw_ld = sem("conv_ffn_loaded")
        x1_rdy = sem("x_after_mixer_tile_ready")
        sqt_rdy = sem("square_tile_ready")
        out_rdy = sem("output_ready")
        stored = sem("output_stored")

        def product_count(r, phase, k, i, per):
            return i * per + (loads_before(phase)[r] + k + 2)

        K_, R_, W0, A0, SSQ, W1, A1, V_ = range(8)
        SLOT = (K_, R_, V_)

        def item_count(i, n):
            return i * 4 + (n // 2 + 2)

        def proj_count(i, n):
            return i * 5 + n

        def split_count(phase, i, r):
            return i * 4 + (SPLIT[phase] + r + 1)

        def seg(v):
            return v.rearrange("p (s t) -> p s t", s=2)

        def chunks(v):
            return v.rearrange("p (c t) -> p c t", t=C)

        class Steps:

            def __init__(self, eng, s):
                self.eng, self.sem, self.base, self.n, self.seen = eng, s, 0, 0, 0
                self.fixed = 0

            def tick(self, ins):
                ins.then_inc(self.sem, 1)
                self.n += 1
                return self.n

            def need(self, n):
                if n > self.seen:
                    self.eng.wait_ge(self.sem, self.base + n)
                    self.seen = n

            def enter(self, i, per):
                self.fixed += self.n
                self.base = i * per + self.fixed
                self.n = self.seen = 0
                self.per = per

            def straight(self):
                self.fixed += self.n
                self.base = self.fixed
                self.n = self.seen = 0

            def leave(self, passes):
                assert self.n == self.per, (self.n, self.per)
                self.fixed += self.per * passes
                self.base = self.fixed
                self.n = self.seen = 0

        def lora_tile(n):
            return lora_act[0:LORA, n] if n < 4 else gate_act[:, n - 4]

        four = [PB[0], PB[1], CH[0], CH[1]]

        def chunk_at(d, s):
            return (s + 4) % NCH if d == 0 else NCH - 1 - s

        def wide(v, n):
            return v[:, None, :].to_broadcast([P, n, v.shape[-1]])

        def deep(v, n):
            return v[:, :, None].to_broadcast([P, v.shape[-1], n])

        block = ctx.enter_context(nc.Block())

        @block.sync
        def _(sp):
            def load(r, phase, k, i, per, src):
                sp.wait_ge(used[r], i * per + (loads_before(phase)[r] + k + 1))
                n = src.shape[-1] if len(src.shape) == 2 else None
                p = src.shape[0]
                sp.dma_start(ring[0:p, r, 0:n], src).then_inc(loaded[r], 16)

            sp.dma_start(cvec[:], io["cvec"]).then_inc(consts_ld, 16)
            for t, name in ((ident, "ident"), (ones, "ones"), (blk, "blk"), (score_mask, "score_mask"),
                            (off_mask, "off_mask"), (eye2, "eye2"), (scan_mask, "scan_mask"), (bmod, "bmod"),
                            (gains, "gains"), (params, "params"), (conv_lora, "conv_lora"), (scal, "scal"),
                            (part_sum, "part_sum")):
                sp.dma_start(t[:], io[name]).then_inc(consts_ld, 16)
            sp.dma_start(hT[:], io["xT_all"]).then_inc(x_ld, 16)
            with sp.Fori(0, 8) as i:
                for r in range(4):
                    load(r, "mod", 0, i, 1, io["w_mod"][bass.ds(i * 4 + r, 1)].rearrange("a p n -> (a p) n"))
            for n in range(6):
                w = io["w_lora"][n] if n < 4 else io["w_gate"][n - 4]
                load(n % 4, "lora", n // 4, 0, 0, w[:, :])

            def load_head(n, p):
                load(n, "pair", 0, p, 1, io["w_rkv"][bass.ds(p * 3 + n, 1)].rearrange("a p n -> (a p) n"))

            def load_lora(p):
                sp.dma_start(lora_w[:], io["w_up_lora"][bass.ds(p, 1)].rearrange("a p m n -> (a p) m n")).then_inc(lw_ld, 16)

            for n in range(3):
                load_head(n, 0)
            load_lora(0)
            for n in range(3):
                load_head(n, 1)

            def body(i, more):
                for k in range(4):
                    load(3, "pair", k, i, 4,
                         io["w_mod"][bass.ds(i * 4 + 32 + k, 1)].rearrange("a p n -> (a p) n"))
                    if k == 0 and more == 2:
                        load_head(0, i + 2)
                    if k == 0 and more == 0:
                        for r in range(3):
                            load(r, "gv", 0, 0, 0, io["w_v"][r])
                    if k == 0 and more >= 1:
                        sp.wait_ge(gb_ps, i + 1)
                        load_lora(i + 1)
                    if k == 0 and more == 2:
                        load_head(1, i + 2)
                if more == 2:
                    load_head(2, i + 2)

            with sp.Fori(0, PAIRS - 2) as i:
                body(i, 2)
            body(PAIRS - 2, 1)
            body(PAIRS - 1, 0)
            load(3, "gv", 0, 0, 0, io["w_v"][3])
            for r in range(4):
                load(r, "gv", 1, 0, 0, io["w_v"][4 + r])
            sp.wait_ge(pair_done, PAIRS + 1)
            sp.dma_start(vrow[:], io["lnv"].partition_broadcast(P)).then_inc(late_ld, 16)
            sp.dma_start(bsp[:], io["b_spatial"].partition_broadcast(P)).then_inc(late_ld, 16)
            sp.dma_start(wsp[:], io["w_spatial"]).then_inc(late_ld, 16)
            sp.dma_start(conv_all, io["conv_ffn"]).then_inc(cw_ld, 16)
            sp.wait_ge(yr_stored, 16 * PAIRS)
            sp.dma_start(yr, io["yr"]).then_inc(yr_ld, 16)
            with sp.Fori(0, 2) as i:
                for r in range(4):
                    load(r, "gu", 0, i, 1, io["w_u"][bass.ds(i * 4 + r, 1)].rearrange("a p n -> (a p) n"))
            with sp.Fori(0, KT) as i:
                load(0, "merge", 0, i, 1, io["w_ga"][bass.ds(i, 1)].rearrange("a p n -> (a p) n"))
                load(1, "merge", 0, i, 1, io["w_gb"][bass.ds(i, 1)].rearrange("a p n -> (a p) n"))
                load(2, "merge", 0, i, 1, io["w_pa"][bass.ds(i, 1)].rearrange("a p n -> (a p) n"))
                load(3, "merge", 0, i, 1, io["w_pb"][bass.ds(i, 1)].rearrange("a p n -> (a p) n"))
            with sp.Fori(0, 4) as i:
                for r in range(4):
                    load(r, "out", 0, i, 1, io["w_out"][bass.ds(i * 4 + r, 1)].rearrange("a p n -> (a p) n"))
            sp.wait_ge(m_rdy, KT + 1)
            sp.dma_start(xT[:], io["xT_all"][:, :, 0:T]).then_inc(xr_ld, 16)
            with sp.Fori(0, FT // 2) as i:
                for r in range(4):
                    load(r, "up", 0, i, 1, io["w_up"][bass.ds(i * 4 + r, 1)].rearrange("a p n -> (a p) n"))
            with sp.Fori(0, KT) as i:
                for r in range(4):
                    load(r, "down", 0, i, 1, io["w_down"][bass.ds(i * 4 + r, 1)].rearrange("a p n -> (a p) n"))
            for g in range(4):
                sp.wait_ge(out_rdy, 4 * g + 4)
                sp.dma_start(io["outT"][:, 4 * g:4 * g + 4, :], x_out[:, 4 * g:4 * g + 4, :]).then_inc(stored, 16)
            sp.wait_ge(stored, 64)

        @block.tensor
        def _(pe):
            mm = nc.tensor.matmul

            def region(r, phase, k, i, per):
                pe.wait_ge(loaded[r], i * (16 * per) + 16 * (loads_before(phase)[r] + k + 1))

            def tile(r, kt, m=P):
                return ring[:, r, kt * m:(kt + 1) * m]

            def small():
                pe.sem_inc(seen, 1)

            for r in range(4):
                pe.sem_inc(used[r], 1)
            pe.sem_inc(proj_ps, 1)
            pe.sem_inc(pair_done, 1)
            pe.sem_inc(rs_rdy, 1)
            pe.sem_inc(kr_cp, 2)
            pe.sem_inc(yr_free, 1)

            def mod_tile(r, psum, n):
                for q in range(4):
                    last = mm(psum[QUAD * q:QUAD * (q + 1), :], csilp[:, 4 * n + q, :],
                              ring[:, r, q * 4 * P:(q + 1) * 4 * P], start=(n == 0), stop=(n == 3))
                last.then_inc(used[r], 1)
                return last

            def mod_sums(psum):
                for n in range(4):
                    last = mm(psum[:, 2 * n:2 * n + 2], mod_sb[:, n], part_sum[:, :], start=True, stop=True)
                last.then_inc(mod_sum, 1)

            def sum_squares(src, n, out):
                pe.wait_ge(sq_rdy, n)
                for kt in range(KT):
                    last = mm(out, ones[:, :], src[:, kt, :], start=(kt == 0), stop=(kt == KT - 1))
                last.then_inc(ssq_ps, 1)

            pe.wait_ge(consts_ld, 16 * NCONST)
            pe.wait_ge(csil_rdy, 1)
            pe.sem_inc(mod_cp, 1)
            pe.sem_inc(mod_rdy, 1)
            pe.sem_inc(mod_sum, 1)

            def mod_four(i):
                pe.wait_ge(mod_cp, i + 1)
                for r in range(4):
                    region(r, "mod", 0, i, 1)
                    mod_tile(r, Q[0], r)
                pe.sem_inc(seen, 1)
                pe.wait_ge(mod_cp, i + 2)
                pe.wait_ge(mod_rdy, i + 1)
                mod_sums(Q[2])

            mod_four(0)
            mod_four(1)
            sum_squares(x_sq, 1, Q[1][:, :])
            with pe.Fori(2, 8) as i:
                mod_four(i)

            for n in range(6):
                r = n % 4
                region(r, "lora", n // 4, 0, 0)
                if n >= 2:
                    pe.wait_ge(lo_cv, n - 1)
                m = LORA if n < 4 else P
                for kt in range(KT):
                    if n == 0:
                        pe.wait_ge(h_rdy, kt + 1)
                        pe.wait_ge(hc_rdy, kt + 1)
                    last = mm(PB[n % 2][0:m, :], tile(r, kt, m), hT[:, kt, :], start=(kt == 0), stop=(kt == KT - 1))
                last.then_inc(used[r], 1)
            pe.wait_ge(lo_cv, 6)
            pe.wait_ge(lo_act, 4)
            pe.sem_inc(pb_free[0], 1)
            pe.sem_inc(pb_free[1], 1)

            def project(p, n, lo=0, hi=KT):
                slot = SLOT[n]
                if lo == 0:
                    pe.wait_ge(pb_free[slot % 2], p * 4 + (slot // 2 + 1))
                    region(n, "pair", 0, p, 1)
                for kt in range(lo, hi):
                    last = mm(PB[slot % 2][:, :], tile(n, kt), hT[:, kt, :], start=(kt == 0), stop=(kt == KT - 1))
                if hi == KT:
                    last.then_inc(used[n], 1)

            def item(p, n):
                if n == W0:
                    pe.wait_ge(lw_ld, p * 16 + 16)
                pe.wait_ge(pb_free[n % 2], p * 4 + (n // 2 + 1))
                if n == SSQ:
                    pe.wait_ge(kksq_rdy, p + 1)
                    mm(PB[SSQ % 2][:, :], blk[:, :], kk2, start=True, stop=True).then_inc(proj_ps, 1)
                else:
                    j = {W0: 0, A0: 2, W1: 1, A1: 3}[n]
                    mm(PB[n % 2][:, :], lora_w[0:LORA, j, :], lora_act[0:LORA, j, :],
                       start=True, stop=True).then_inc(proj_ps, 1)

            def gv_part(h, bank, lo, hi):
                for x in range(lo, hi):
                    kt, n = x // 2, x % 2
                    r = kt // 4
                    if x % 8 == 0:
                        region(r, "gv", h, 0, 0)
                    last = mm(bank[n][:, :], hT[:, kt, n * P:(n + 1) * P], ring[:, r, (kt % 4) * 512:(kt % 4 + 1) * 512],
                              start=(kt == 0), stop=(kt == KT - 1))
                    if x % 8 == 7:
                        last.then_inc(used[r], 1)

            def behind_last(k):
                gv_part(0, PB, min(k + 10, 24), min(k + 11, 24))

            def between(p, k):
                if k < 5:
                    item(p, (W0, A0, SSQ, W1, A1)[k])
                else:
                    project(p, 2, k - 5, k - 4)

            def body(i, more):
                if more == 0:
                    pe.wait_ge(pb_free[0], item_count(i, A1))
                pe.wait_ge(pb_free[V_ % 2], item_count(i, V_))
                for ch in range(NCH):
                    for h in range(2):
                        hr = slice(64 * h, 64 * h + 64)
                        last = mm(CH[0][hr, ch * C:(ch + 1) * C], vx[:, ch * C:(ch + 1) * C], ident[:, hr],
                                  start=True, stop=True)
                last.then_inc(vt_ps, 1)
                pe.wait_ge(rc_rdy, i + 1)
                mm(CH[1][:, 0:T], blk[:, :], rc, start=True, stop=True)
                for k in range(2):
                    last = mm(CH[1][:, T:2 * T], lora_w[:, 4 + k, :], gate_act[:, k, 0:T], start=(k == 0), stop=(k == 1))
                last.then_inc(gb_ps, 1)
                pe.wait_ge(rs_rdy, i + 1)
                for d in range(2):
                    pe.wait_ge(x_rdy, i * 2 + d + 1)
                    if d == 1:
                        pe.wait_ge(nl_sb, i * 2 + 1)
                        pe.wait_ge(xt_sb, i * 4 + 2)
                    for s in range(2):
                        for c in range(4):
                            for h in range(2):
                                rows = slice(64 * h, 64 * h + 64)
                                ch = 4 * s + c
                                last = mm(Q[2 * s + h][:, c * P:(c + 1) * P], X[d][rows, ch], KRn[d][rows, ch],
                                          start=True, stop=True)
                        last.then_inc(sc_ps, 1)
                    if more >= 1:
                        project(i + 1, 1, *((6, 10), (12, 14))[d])
                    else:
                        gv_part(0, PB, *((0, 4), (6, 8))[d])
                    for s in range(2):
                        pe.wait_ge(sc_sb, i * 4 + 2 * d + s + 1)
                        for c in range(4):
                            ch = 4 * s + c
                            last = nc.tensor.transpose(Q[2 * s + 1][:, c * P:(c + 1) * P], X[d][:, ch], ident[:, :])
                        last.then_inc(xt_ps, 1)
                    for ch in range(NCH):
                        for h in range(2):
                            rows, orow = slice(64 * h, 64 * h + 64), slice(64 - 64 * h, 128 - 64 * h)
                            last = mm(Q[0][orow, ch * C:(ch + 1) * C], KRn[d][rows, ch, 0], X[d][rows, ch, 1 - h],
                                      start=True, stop=True)
                    last.then_inc(nl_ps, 1)
                    if more >= 1:
                        project(i + 1, 1, *((10, 12), (14, KT))[d])
                    else:
                        gv_part(0, PB, *((4, 6), (8, 10))[d])
                pe.wait_ge(xt_sb, i * 4 + 4)
                pe.wait_ge(nl_sb, i * 2 + 2)
                pe.wait_ge(bonv_rdy, i + 1)
                pe.wait_ge(g_rdy, i + 1)
                for lv in range(LEVELS - 1):
                    for d in range(2):
                        pe.wait_ge(z_rdy[d], i * LEVELS + lv + 1)
                        small()
                        for ch in range(NCH):
                            for h in range(2):
                                hr = slice(64 - 64 * h, 128 - 64 * h)
                                last = mm(Q[2 * d][hr, ch * C:(ch + 1) * C], NL[d][hr, ch], ZU[d][hr, ch],
                                          start=True, stop=True)
                        last.then_inc(tu_ps[d], 1)
                    if more >= 1:
                        between(i + 1, 3 * lv)
                    else:
                        behind_last(3 * lv)
                    for d in range(2):
                        pe.wait_ge(tu_sb[d], i * (LEVELS - 1) + lv + 1)
                        small()
                        for ch in range(NCH):
                            for h in range(2):
                                hr = slice(64 - 64 * h, 128 - 64 * h)
                                last = mm(Q[2 * d + 1][hr, ch * C:(ch + 1) * C], ZL[d][hr, ch], TU[d][hr, ch],
                                          start=True, stop=True)
                        if lv < LEVELS - 2:
                            for ch in range(NCH):
                                for h in range(2):
                                    hr = slice(64 - 64 * h, 128 - 64 * h)
                                    last = mm(Q[2 * d][hr, ch * C:(ch + 1) * C], TU[d][hr, ch], ZL[d][hr, ch],
                                              start=True, stop=True)
                        last.then_inc(zz_ps[d], 1)
                        if lv and d == 1:
                            region(3, "pair", lv - 1, i, 4)
                            mod_tile(3, CH[1], lv - 1)
                        if more >= 1:
                            between(i + 1, 3 * lv + 1 + d)
                        else:
                            behind_last(3 * lv + 1 + d)
                pe.wait_ge(vt_all, i * 2 + 2)
                pe.wait_ge(kr_cp, i * 2 + 4)
                pe.wait_ge(mod_cp, i + 10)
                for s in range(NCH):
                    if more >= 1 and 1 <= s <= 6:
                        project(i + 1, 2, s + 9, s + 10)
                    for d in range(2):
                        ch = chunk_at(d, s)
                        if s:
                            pe.wait_ge(st_sb[d], i * 7 + s)
                        else:
                            pe.wait_ge(z_rdy[d], i * LEVELS + LEVELS)
                        small()
                        for h in range(2):
                            rows, orow = slice(64 * h, 64 * h + 64), slice(64 - 64 * h, 128 - 64 * h)
                            last = mm(CH[d][orow, 0:C], SC[d][h][rows, ch, 0], VU[d][rows, ch, h],
                                      start=True, stop=(s == 0))
                            if s:
                                last = mm(CH[d][orow, 0:C], KR[d][rows, ch, 0], ST[d][s % 2][rows, :],
                                          start=False, stop=True)
                        last.then_inc(rhs_ps[d], 1)
                    if s == 0:
                        mod_sums(Q[3])
                    if more == 2:
                        project(i + 2, 0, 2 * s, 2 * s + 1)
                    if more == 0:
                        gv_part(0, PB, 24 + s, 25 + s)
                    for d in range(2):
                        ch = chunk_at(d, s)
                        pe.wait_ge(rhs_cp[d], i * NCH + s + 1)
                        small()
                        for h in range(2):
                            hr = slice(64 - 64 * h, 128 - 64 * h)
                            last = mm(CH[d][hr, C:2 * C], ZU[d][hr, ch], rhs_sb[d][hr, :], start=True, stop=True)
                        last.then_inc(u_ps[d], 1)
                    if more == 2:
                        project(i + 2, 0, 2 * s + 1, 2 * s + 2)
                    for d in range(2):
                        ch = chunk_at(d, s)
                        for h in range(2):
                            pe.wait_ge(u_sb[d][h], i * NCH + s + 1)
                        if s < NCH - 1:
                            for h in range(2):
                                last = mm(CH[d][64 * h:64 * h + 64, 2 * C:3 * C], XT[d][:, ch, 64 * h:64 * h + 64],
                                          VU[d][:, ch, h], start=True, stop=True)
                            last.then_inc(st_ps[d], 1)
                    for d in range(2):
                        ch = chunk_at(d, s)
                        if s >= 4:
                            if s > 4:
                                pe.wait_ge(y_sb[d], i * 4 + s - 4)
                            for h in range(2):
                                rows = slice(64 * h, 64 * h + 64)
                                mm(Q[2 * d][rows, 0:C], VU[d][:, ch, h], SC[d][h][:, ch, 1], start=True, stop=False)
                            for h in range(2):
                                rows = slice(64 * h, 64 * h + 64)
                                last = mm(Q[2 * d][rows, 0:C], ST[d][s % 2][rows, :], KR[d][rows, ch, 1],
                                          start=False, stop=True)
                            last.then_inc(y_ps[d], 1)
                if more == 2:
                    project(i + 2, 1, 0, 3)
                pe.wait_ge(ysum_rdy, i + 1)
                mm(Q[0][:, 0:T], blk[:, :], ra, start=True, stop=True).then_inc(mean_ps, 1)
                if more == 2:
                    project(i + 2, 1, 3, 6)
                pe.wait_ge(dev2_rdy, i + 1)
                mm(Q[1][:, 0:T], blk[:, :], rb, start=True, stop=True).then_inc(var_ps, 1)

            project(0, 0)
            project(0, 1)
            for n in range(W0, V_):
                item(0, n)
            project(0, 2)
            project(1, 0)
            project(1, 1, 0, 6)
            with pe.Fori(0, PAIRS - 2) as i:
                body(i, 2)
            body(PAIRS - 2, 1)
            body(PAIRS - 1, 0)

            pe.wait_ge(pair_done, PAIRS + 1)
            gv_part(1, Q[2:4], 0, 2 * KT)

            def split_tile(phase, i, r):
                pe.wait_ge(lo_rdy, split_count(phase, i, r))

            def exact(out, r, k, hi, lo, start, stop):
                cols = slice(k * P, (k + 1) * P)
                mm(out, w_hi_r[:, r % 2, cols], hi, start=start, stop=False)
                mm(out, w_hi_r[:, r % 2, cols], lo, start=False, stop=False)
                return mm(out, w_lo_r[:, r, cols], hi, start=False, stop=stop)

            pe.wait_ge(late_ld, 48)
            pe.wait_ge(hh_rdy, 1)
            pe.wait_ge(hl_rdy, 1)
            pe.sem_inc(yg_rdy, 2)
            pe.sem_inc(gs_ps, 2)
            for t in range(GG + 1):
                i, r = t // 4, t % 4
                if t < GG:
                    split_tile("gu", i, r)
                    if t >= 2:
                        pe.wait_ge(gu_act, t - 1)
                    for kt in range(KT):
                        last = exact(PB[r % 2][:, 0:T], r, kt, h_hi_r[:, kt], h_lo_r[:, kt], kt == 0, kt == KT - 1)
                    last.then_inc(used[r], 1)
                if t:
                    r = (t - 1) % 4
                    pe.wait_ge(vc_rdy, t)
                    pe.wait_ge(yg_rdy, t)
                    for n in range(2):
                        last = mm(CH[r % 2][:, n * P:(n + 1) * P], vcur[r % 2][:, n], wsp[:, t - 1, :], start=True, stop=True)
                    last.then_inc(gs_ps, 1)
            pe.wait_ge(yg_rdy, GG + 2)
            pe.sem_inc(me_act, 2)
            pe.sem_inc(m_rdy, 1)
            with pe.Fori(0, KT) as i:
                for r in range(4):
                    split_tile("merge", i, r)
                    if r == 2:
                        pe.wait_ge(yrl_rdy, 1)
                    if r == 3:
                        pe.wait_ge(pool_lo, GG)
                    if r < 2:
                        pe.wait_ge(me_act, i * 2 + r + 1)
                    else:
                        pe.wait_ge(m_rdy, i + 1)
                    hi, lo, n = ((h_hi_r, h_lo_r, KT), (h_hi_r, h_lo_r, KT), (yr_hi_r, yr_lo_r, KT), (yg_hi_r, yg_lo_r, GG))[r]
                    for kt in range(n):
                        last = exact(Q[r][:, 0:T], r, kt, hi[:, kt], lo[:, kt], kt == 0, kt == n - 1)
                    last.then_inc(used[r], 1)
            pe.wait_ge(m_rdy, KT + 1)
            pe.sem_inc(o_sb, 4)

            def add_square(src, first=False, last=False):
                m = mm(Q[0][:, 0:T], ones[:, :], src, start=first, stop=last)
                if last:
                    m.then_inc(ssq_ps, 1)

            def out_four(i, first):
                for r in range(4):
                    split_tile("out", i, r)
                    pe.wait_ge(o_sb, i * 4 + r + 1)
                    for kt in range(KT):
                        if first and r == 0:
                            pe.wait_ge(pool_lo, GG + kt + 1)
                        last = exact(four[r][:, 0:T], r, kt, m_hi_r[:, kt], m_lo_r[:, kt], kt == 0, kt == KT - 1)
                    last.then_inc(used[r], 1)
                    if r or not first:
                        pe.wait_ge(o_sb, i * 4 + r + 4)
                        add_square(sq[:, bass.ds(i * 4 + r - 1, 1), :].rearrange("p a b -> p (a b)"),
                                   first=first and r == 1)

            out_four(0, True)
            with pe.Fori(1, 4) as i:
                out_four(i, False)
            pe.wait_ge(o_sb, KT + 4)
            add_square(sq[:, KT - 1, :], last=True)
            for kt in range(KT):
                pe.wait_ge(sqt_rdy, kt + 1)
                add_square(sq[:, kt, :], first=kt == 0, last=kt == KT - 1)
            pe.sem_inc(up_cv, 2)
            pe.sem_inc(ff_rdy, 2)

            def up_four(i, first):
                for r in range(4):
                    split_tile("up", i, r)
                    pe.wait_ge(up_lo, i * 4 + r + 1)
                    pe.wait_ge(up_cv, i * 2 + 1 + r // 2)
                    for kt in range(KT):
                        if first and r == 0:
                            pe.wait_ge(h_rdy, KT + kt + 1)
                        last = exact(four[r][:, 0:T], r, kt, h2_hi_r[:, kt], h2_lo_r[:, kt], kt == 0, kt == KT - 1)
                    last.then_inc(used[r], 1)

            up_four(0, True)
            with pe.Fori(1, FT // 2) as i:
                up_four(i, False)
            pe.sem_inc(dn_sb, 2)

            def down_two(i, first):
                for q in range(2):
                    pe.wait_ge(dn_sb, i * 2 + q + 1)
                    for r in range(4):
                        split_tile("down", i * 2 + q, r)
                        if first and q == 0:
                            pe.wait_ge(pool_lo, GG + KT + (r + 1) * (FT // 4))
                        for k in range(FT // 4):
                            kt = r * (FT // 4) + k
                            last = exact(Q[2 + q][:, 0:T], r, k, ff_hi_r[:, kt], ff_lo_r[:, kt], kt == 0, kt == FT - 1)
                        last.then_inc(used[r], 1)
                    if q or not first:
                        pe.wait_ge(dn_sb, i * 2 + q + 2)
                        add_square(sqd[1 - q], first=first)

            down_two(0, True)
            with pe.Fori(1, KT // 2) as i:
                down_two(i, False)
            pe.wait_ge(dn_sb, KT + 2)
            add_square(sqd[1], last=True)

        @block.scalar
        def _(act):
            A = Steps(act, act_step)
            f = nc.scalar.activation

            def product(r, phase, k, i, per):
                act.wait_ge(used[r], product_count(r, phase, k, i, per))

            def rms(n, out, psum, width):
                act.wait_ge(ssq_ps, n)
                A.need(A.tick(f(out, psum, ACT.Ln, scale=1.0 / D, bias=scal[:, 0:1])))
                f(out, out, ACT.Exp, scale=-0.5).then_inc(rstd_rdy, 1)

            act.preload_act_table_set("natural_log_exp_and_others")
            act.wait_ge(consts_ld, 16 * NCONST)
            f(csil[:], cvec[:], ACT.Exp, scale=-1.0).then_inc(cexp_rdy, 1)
            act.wait_ge(x_ld, 16)
            f(x_sq, hT[:], ACT.Square).then_inc(sq_rdy, 1)

            def mod_copy(i):
                product(3, "mod", 0, i, 1)
                act.wait_ge(mod_sum, i + 1)
                f(mod_sb, Q[0][:, :].rearrange("p (a b) -> p a b", b=P), ACT.Copy).then_inc(mod_cp, 1)

            mod_copy(0)
            mod_copy(1)
            rms(1, rstd[:, :], Q[1][:, :], TT)
            with act.Fori(2, 8) as i:
                mod_copy(i)
            act.wait_ge(gcol_rdy, 1)
            for kt in range(KT):
                f(hT[:, kt, T:TT], hT[:, kt, T:TT], ACT.Identity, scale=gcol[:, kt, 1:2],
                  bias=modT[:, kt, 1:2]).then_inc(hc_rdy, 1)
            for n in range(6):
                m = LORA if n < 4 else P
                product(n % 4, "lora", n // 4, 0, 0)
                f(lora_tile(n), PB[n % 2][0:m, :], ACT.Identity, scale=conv_lora[0:m, n, 1:2]).then_inc(lo_mid, 1)
            act.wait_ge(lo_cv, 6)
            for n in range(2):
                f(lora_act[0:LORA, n], lora_act[0:LORA, n], ACT.Tanh).then_inc(lo_act, 1)
            for n in range(4, 6):
                f(gate_act[:, n - 4], gate_act[:, n - 4], ACT.Sigmoid).then_inc(lo_act, 1)
            act.wait_ge(par_rdy, 1)

            def centre(p, n, par):
                product(n, "pair", 0, p, 1)
                c = (PK, PR, PV)[n]
                f((kx, rx, vx)[n], PB[SLOT[n] % 2][:, :], ACT.Identity, scale=par[:, c + 1:c + 2]).then_inc(cv_mid, 1)

            def fetch(par, p):
                A.need(A.tick(f(par[:, :], paramx[:, bass.ds(p, 1), :].rearrange("p a b -> p (a b)"), ACT.Copy)))

            def inputs(p):
                act.wait_ge(kk0_rdy, p + 1)
                f(kk2, kkx, ACT.Square).then_inc(kksq_rdy, 1)
                for n, out, c in ((W0, ew[0], PHW0), (A0, ea[0], PHA0), (W1, ew[1], PHW0 + 1), (A1, ea[1], PHA0 + 1)):
                    act.wait_ge(proj_ps, proj_count(p, n))
                    f(out, PB[n % 2][:, :], ACT.Tanh, scale=0.5, bias=par_a[:, c:c + 1]).then_inc(pb_free[n % 2], 1)
                act.preload_act_table_set("natural_log_exp_and_others")
                act.wait_ge(pb_free[SSQ % 2], item_count(p, SSQ))
                A.need(A.tick(f(kkn, kkn, ACT.Ln, scale=float(2 ** LN_SHIFT))))
                f(kkn, kkn, ACT.Exp, scale=-0.5, bias=scal[:, 3:4]).then_inc(kkr_rdy, 1)
                for d in range(2):
                    sign = -DECAY_C if d == 0 else DECAY_C
                    act.wait_ge(cum_rdy, p * 2 + d + 1)
                    f(wcn[:, d, :], chunks(cumP[d])[:, :, C - 1], ACT.Exp, scale=-DECAY_C)
                    if d == 1:
                        act.wait_ge(kk_rdy, p + 1)
                    A.need(A.tick(f(eN[d], eIn[d], ACT.Exp, scale=-sign)))
                    f(eIn[d], eIn[d], ACT.Exp, scale=sign)
                    f(eEx[d], eEx[d], ACT.Exp, scale=sign).then_inc(exp_rdy, 1)

            fetch(par_a, 0)
            centre(0, 0, par_a)
            centre(0, 1, par_a)
            inputs(0)
            centre(0, 2, par_a)
            act.wait_ge(x_rdy, 2)
            fetch(par_ak, 1)
            centre(1, 0, par_ak)

            def body(i, more):
                act.wait_ge(pair_done, i + 1)
                if more >= 1:
                    fetch(par_a, i + 1)
                act.wait_ge(vt_ps, i + 1)
                for h in range(2):
                    hr = slice(64 * h, 64 * h + 64)
                    last = f(VU[0][hr, :, h], chunks(CH[0][hr, :]), ACT.Copy)
                last.then_inc(vt_sb, 1)
                act.wait_ge(gb_ps, i + 1)
                act.wait_ge(bonv_rdy, i + 1)
                f(gT, CH[1][:, T:2 * T], ACT.Copy).then_inc(g_rdy, 1)
                for d in range(2):
                    for s in range(2):
                        act.wait_ge(xt_ps, i * 4 + 2 * d + s + 1)
                        f(XT[d][:, 4 * s:4 * s + 4], Q[2 * s + 1][:, :].rearrange("p (c n) -> p c n", c=4),
                          ACT.Copy).then_inc(xt_sb, 1)
                if more >= 1:
                    act.wait_ge(x_rdy, i * 2 + 2)
                    centre(i + 1, 1, par_a)
                    inputs(i + 1)
                product(3, "pair", 3, i, 4)
                f(mod_sb, CH[1][:, :].rearrange("p (a b) -> p a b", b=P), ACT.Copy).then_inc(mod_cp, 1)
                for s in range(NCH):
                    act.wait_ge(rhs_ps[1], i * NCH + s + 1)
                    f(rhs_sb[1], CH[1][:, 0:C], ACT.Copy).then_inc(rhs_cp[1], 1)
                    for d in range(2):
                        act.wait_ge(u_ps[d], i * NCH + s + 1)
                        f(VU[d][0:64, chunk_at(d, s), 1], CH[d][0:64, C:2 * C], ACT.Copy, scale=-1.0).then_inc(u_sb[d][1], 1)
                    if s >= 4:
                        for d in range(2):
                            ch = chunk_at(d, s)
                            act.wait_ge(y_ps[d], i * 4 + s - 3)
                            f(yd[d][:, ch * C:(ch + 1) * C], Q[2 * d][:, 0:C], ACT.Copy).then_inc(y_sb[d], 1)
                    if more >= 1 and s == NCH - 2:
                        centre(i + 1, 2, par_a)
                if more == 2:
                    act.wait_ge(x_rdy, i * 2 + 4)
                    fetch(par_ak, i + 2)
                    centre(i + 2, 0, par_ak)
                act.wait_ge(dev_rdy, i + 1)
                f(rb, ra, ACT.Square).then_inc(dev2_rdy, 1)
                act.wait_ge(var_ps, i + 1)
                A.need(A.tick(f(rb, Q[1][:, 0:T], ACT.Ln, scale=1.0 / HEAD, bias=scal[:, 2:3])))
                f(rb, rb, ACT.Exp, scale=-0.5).then_inc(rs_rdy, 1)

            with act.Fori(0, PAIRS - 2) as i:
                A.enter(i, 6)
                body(i, 2)
            A.leave(PAIRS - 2)
            body(PAIRS - 2, 1)
            body(PAIRS - 1, 0)

            act.wait_ge(pair_done, PAIRS + 1)
            f(h_hi_r[:, :, :], hT[:, :, 0:T], ACT.Copy).then_inc(hh_rdy, 1)

            def high(phase, i, r, first=False):
                i, r = (i, r) if r < 4 else (i + 1, r - 4)
                act.wait_ge(loaded[r], i * 16 + 16 * (loads_before(phase)[r] + 1))
                if r < 2 and not (phase == "gu" and first):
                    act.wait_ge(used[r + 2], i + (loads_before(phase)[r + 2] + 1))
                elif r >= 2:
                    act.wait_ge(used[r - 2], i + (loads_before(phase)[r - 2] + 2))
                n = width(phase, r) // (2 if (phase, r) == ("merge", 0) else 1)
                f(w_hi_r[:, r % 2, 0:n], ring[:, r, 0:n], ACT.Copy).then_inc(hi_rdy, 1)

            def highs(phase, i, r, n, then):
                if isinstance(i, int) and i == n - 1 and r >= 2:
                    if then:
                        high(then, 0, r - 2)
                else:
                    high(phase, i, r + 2)

            def fours(n, body, first=0):
                for i in range(first):
                    body(i)
                with act.Fori(first, n - 1) as i:
                    body(i)
                body(n - 1)

            for h in range(2):
                if h:
                    high("gu", 0, 0, first=True)
                    high("gu", 0, 1, first=True)
                product(3, "gv", h, 0, 0)
                for n in range(2):
                    f(vg[:, n, h * 512:(h + 1) * 512], (PB, Q[2:4])[h][n][:, :], ACT.Gelu).then_inc(gv_act, 1)
            act.wait_ge(gv_st, 2)
            A.need(A.tick(f(vrs, mv[:, :, 1], ACT.Ln, bias=scal[:, 1:2])))
            f(vrs, vrs, ACT.Exp, scale=-0.5).then_inc(gv_rs, 1)
            act.preload_act_table(ACT.Gelu)

            def gu_four(i):
                for r in range(4):
                    highs("gu", i, r, 2, "merge")
                    act.wait_ge(yg_rdy, i * 4 + r + 1)
                    product(r, "gu", 0, i, 1)
                    f(ug[r % 2], PB[r % 2][:, 0:T], ACT.Gelu).then_inc(gu_act, 1)
                    if isinstance(i, int) and (i, r) == (0, 0):
                        act.wait_ge(yr_ld, 16)
                        f(yr_hi_r[:, :, :], yr, ACT.Copy).then_inc(yrh_rdy, 1)

            gu_four(0)
            gu_four(1)
            act.preload_act_table(ACT.Sigmoid)

            def merge_four(i):
                act.wait_ge(m_rdy, i + 1)
                for r in range(4):
                    highs("merge", i, r, KT, "out")
                    if r < 2:
                        product(r, "merge", 0, i, 1)
                        f((sga, sgb)[r], Q[r][:, 0:T], ACT.Sigmoid).then_inc(me_act, 1)

            fours(KT, merge_four)

            def out_four(i):
                for r in range(4):
                    highs("out", i, r, 4, "up")
                    product(r, "out", 0, i, 1)
                    to = bass.ds(i * 4 + r, 1)
                    f(mixT[:, to, :].rearrange("p a b -> p (a b)"), four[r][:, 0:T], ACT.Copy)
                    f(sq[:, to, :].rearrange("p a b -> p (a b)"), four[r][:, 0:T], ACT.Square).then_inc(o_sb, 1)

            fours(4, out_four)
            rms(2, rstd[:, 0:T], Q[0][:, 0:T], T)
            for kt in range(KT):
                act.wait_ge(x1_rdy, kt + 1)
                f(sq[:, kt, :], xT[:, kt, :], ACT.Square).then_inc(sqt_rdy, 1)
            rms(3, rstd[:, 0:T], Q[0][:, 0:T], T)
            for kt in range(KT):
                act.wait_ge(h2_raw, kt + 1)
                f(h2_hi_r[:, kt], h2_lo[:, kt], ACT.Identity, bias=modT[:, 3 * KT + kt, 0:1]).then_inc(h2h_rdy, 1)
            act.preload_act_table(ACT.Silu)
            act.wait_ge(cw_ld, 16)
            A.straight()

            def silu(i, j):
                act.wait_ge(up_cv, i * 2 + j + 3)
                f(sil[j], cv[2 * j], ACT.Silu).then_inc(up_act, 1)

            def up_four(i, first=False):
                if not first:
                    act.wait_ge(up_mid, i * 4)
                A.need(A.tick(f(convw_a, conv_all[:, bass.ds(i, 1)].rearrange("p a m n -> p (a m) n"), ACT.Copy)))
                for r in range(4):
                    if r % 2 == 0:
                        highs("up", i, r, FT // 2, "down")
                    product(r, "up", 0, i, 1)
                    if r % 2 == 0:
                        act.wait_ge(ff_rdy, i * 2 + r // 2 + 1)
                    f(cv[r], four[r][:, 0:T], ACT.Identity, scale=convw_a[:, r, 4:5]).then_inc(up_mid, 1)
                    if r % 2:
                        highs("up", i, r, FT // 2, "down")
                    if r == 1 and not first:
                        silu(i - 1, 1)
                    if r == 3:
                        silu(i, 0)

            up_four(0, True)
            A.straight()
            with act.Fori(1, FT // 2 - 1) as i:
                A.enter(i - 1, 1)
                up_four(i)
            A.leave(FT // 2 - 2)
            up_four(FT // 2 - 1)
            silu(FT // 2 - 1, 1)

            def down_one(i, q, last=False):
                for r in range(4):
                    if r < 2 or not last:
                        k, to = (q, r + 2) if r < 2 else (q + 1, r - 2)
                        act.wait_ge(loaded[to], i * 32 + 16 * (loads_before("down")[to] + k + 1))
                        act.wait_ge(used[r], i * 2 + (loads_before("down")[r] + q + 2))
                        f(w_hi_r[:, r % 2, 0:FT // 4 * P], ring[:, to, 0:FT // 4 * P], ACT.Copy).then_inc(hi_rdy, 1)
                product(3, "down", q, i, 2)
                f(mixT[:, bass.ds(i * 2 + q, 1), :].rearrange("p a b -> p (a b)"), Q[2 + q][:, 0:T], ACT.Copy)
                f(sqd[q], Q[2 + q][:, 0:T], ACT.Square).then_inc(dn_sb, 1)

            with act.Fori(0, KT // 2 - 1) as i:
                down_one(i, 0)
                down_one(i, 1)
            down_one(KT // 2 - 1, 0)
            down_one(KT // 2 - 1, 1, True)
            rms(4, rstd[:, 0:T], Q[0][:, 0:T], T)

        @block.vector
        def _(dve):
            V = Steps(dve, dve_step)
            tt, ts, stt = nc.vector.tensor_tensor, nc.vector.tensor_scalar, nc.vector.scalar_tensor_tensor

            def product(r, phase, k, i, per):
                dve.wait_ge(used[r], product_count(r, phase, k, i, per))

            def flow(*ins):
                for x in ins:
                    V.need(V.tick(x))

            dve.wait_ge(consts_ld, 16 * NCONST)
            V.tick(nc.vector.tensor_copy(paramx[:, :, 0:NPAR], params[:]))
            V.tick(ts(paramx[:, :, PHW0:PHW0 + 4], params[:, :, PW0:PW0 + 4], 0.5, None, ALU.mult))
            V.tick(ts(paramx[:, :, PHKA:PHKA + 1], params[:, :, PKA:PKA + 1], 0.5, None, ALU.mult))
            ts(paramx[:, :, POKA:POKA + 1], params[:, :, PKA:PKA + 1], -0.5, 1.0, ALU.mult, ALU.add).then_inc(par_rdy, 1)
            dve.wait_ge(cexp_rdy, 1)
            flow(ts(csil[:], csil[:], 1.0, None, ALU.add))
            flow(nc.vector.reciprocal(csil[:], csil[:]))
            z = V.tick(nc.vector.memset(csilp[:], 0.0))
            V.need(z)
            tt(csilp[:, :, 0:2], csil[:], cvec[:], ALU.mult).then_inc(csil_rdy, 1)

            def mod_out(psum, at):
                return tt(modT[:, bass.ds(at, 4), :], psum.rearrange("p (a b) -> p a b", a=4),
                          bmod[:, bass.ds(at, 4)][:, :, None].to_broadcast([P, 4, 2]), ALU.add)

            def mod_add(i):
                dve.wait_ge(mod_sum, i + 2)
                mod_out(Q[2][:, 0:8], i * 4).then_inc(mod_rdy, 1)

            mod_add(0)
            mod_add(1)
            dve.wait_ge(rstd_rdy, 1)
            V.tick(tt(hT[:], hT[:], wide(rstd[:, :], KT), ALU.mult))
            with dve.Fori(2, 8) as i:
                mod_add(i)
            dve.wait_ge(mod_rdy, 9)
            V.need(V.n)
            stt(gcol[:], modT[:, KT:2 * KT, :], 1.0, deep(gains[:, 0, :], 2), ALU.add, ALU.mult).then_inc(gcol_rdy, 1)
            dve.wait_ge(gcol_rdy, 1)
            for kt in range(KT):
                ts(hT[:, kt, 0:T], hT[:, kt, 0:T], gcol[:, kt, 0:1], modT[:, kt, 0:1], ALU.mult, ALU.add).then_inc(h_rdy, 1)

            def side_taps(x, psum, w):
                flow(stt(x[:, :, 1:T], psum[:, :, 0:T - 1], w[0], x[:, :, 1:T], ALU.mult, ALU.add))
                return stt(x[:, :, 0:T - 1], psum[:, :, 1:T], w[2], x[:, :, 0:T - 1], ALU.mult, ALU.add)

            for n in range(6):
                m = LORA if n < 4 else P
                dve.wait_ge(lo_mid, n + 1)
                side_taps(seg(lora_tile(n)), seg(PB[n % 2][0:m, :]),
                          [conv_lora[0:m, n, k:k + 1] for k in range(3)]).then_inc(lo_cv, 1)
            dve.wait_ge(par_rdy, 1)

            def par(c):
                return par_v[:, c:c + 1]

            def fetch(par_t, p):
                V.need(V.tick(nc.vector.tensor_copy(par_t[:, :], paramx[:, bass.ds(p, 1), :].rearrange("p a b -> p (a b)"))))

            def outer(p, n, par_t):
                c = (PK, PR, PV)[n]
                dve.wait_ge(cv_mid, cv_count(p, n))
                side_taps(seg((kx, rx, vx)[n]), seg(PB[SLOT[n] % 2][:, :]),
                          [par_t[:, c:c + 1], None, par_t[:, c + 2:c + 3]]).then_inc(pb_free[SLOT[n] % 2], 1)

            def cv_count(p, n):
                if n == 0:
                    return 1 if isinstance(p, int) and p == 0 else p * 3 + 1
                return p * 3 + n + 1

            def times(out, x, y):
                return tt(out, chunks(x), chunks(y), ALU.mult)

            def inputs(p, n):
                if n == 0:
                    ts(kkx, kx, par(PKK), None, ALU.mult).then_inc(kk0_rdy, 1)
                if n in (1, 3):
                    d = n // 2
                    dve.wait_ge(pb_free[d], item_count(p, (W0, W1)[d]))
                    flow(ts(ew[d], ew[d], 0.5, 0.5, ALU.mult, ALU.add))
                    flow(nc.vector.tensor_tensor_scan(cumP[d], scan_mask[:, :], ew[d], 0.0, ALU.mult, ALU.add))
                if n == 2:
                    dve.wait_ge(proj_ps, proj_count(p, SSQ))
                    ts(kkn, PB[SSQ % 2][:, :], KK_MIN, None, ALU.max).then_inc(pb_free[SSQ % 2], 1)
                if n in (2, 4):
                    d = n // 2 - 1
                    tt(ew[d], cumP[d], ew[d], ALU.subtract).then_inc(cum_rdy, 1)
                    dve.wait_ge(pb_free[1 - d], item_count(p, (A0, A1)[d]))
                    m = V.tick(ts(kdir[d], ea[d], par(PHKA), par(POKA), ALU.mult, ALU.add))
                    V.tick(ts(ea[d], ea[d], 0.5, 0.5, ALU.mult, ALU.add))
                    V.need(m)
                    V.tick(tt(kdir[d], kdir[d], kx, ALU.mult))
                if n == 5:
                    V.need(V.n)
                    flow(tt(rc, kdir[0][:, 0:T], kdir[1][:, 0:T], ALU.add))
                    stt(rc, rc, par(PRK), rx[:, 0:T], ALU.mult, ALU.mult).then_inc(rc_rdy, 1)
                    dve.wait_ge(kkr_rdy, p + 1)
                    tt(kkx, kkx, kkn, ALU.mult).then_inc(kk_rdy, 1)
                if n == 6:
                    dve.wait_ge(kk_rdy, p + 1)
                    V.tick(tt(ea[0], ea[0], kkx, ALU.mult))
                    V.tick(tt(ea[1], ea[1], kkx, ALU.mult))
                    dve.wait_ge(kr_cp, p * 2 + 2)
                if n in (7, 9):
                    d = n // 2 - 3
                    dve.wait_ge(exp_rdy, p * 2 + d + 1)
                    V.tick(times(KRn[d][:, :, 0], kkx, eEx[d]))
                    V.tick(times(KRn[d][:, :, 1], rx, eIn[d]))
                if n in (8, 9):
                    d = n - 8
                    V.need(V.n)
                    for h in range(2):
                        rows = slice(64 * h, 64 * h + 64)
                        V.tick(times(X[d][rows, :, h], kdir[d][rows, :], eN[d][rows, :]))
                        last = times(X[d][rows, :, 1 - h], ea[d][rows, :], eN[d][rows, :])
                        if h == 0:
                            V.tick(last)
                    last.then_inc(x_rdy, 1)

            def body(i, more):
                fetch(par_vo, i)
                if more >= 1:
                    fetch(par_v, i + 1)
                dve.wait_ge(exp_rdy, i * 2 + 2)
                V.tick(nc.vector.tensor_copy(wc[:], wcn[:]))
                dve.wait_ge(gb_ps, i + 1)
                tt(bon, CH[1][:, 0:T], vx[:, 0:T], ALU.mult).then_inc(bonv_rdy, 1)
                for d in range(2):
                    for s in range(2):
                        dve.wait_ge(sc_ps, i * 4 + 2 * d + s + 1)
                        for h in range(2):
                            last = tt(SC[d][h][:, 4 * s:4 * s + 4].rearrange("p c a t -> p c (a t)"),
                                      Q[2 * s + h][:, :].rearrange("p (c n) -> p c n", c=4),
                                      wide(score_mask[:, d, :], 4), ALU.mult)
                            if h == 0:
                                V.tick(last)
                        last.then_inc(sc_sb, 1)
                    dve.wait_ge(sc_sb, i * 4 + 2 * d + 2)
                    for h in range(2):
                        hr = slice(64 - 64 * h, 128 - 64 * h)
                        m = V.tick(tt(TU[d][hr], SC[d][h][hr, :, 0],
                                      off_mask[hr, d, 0, :][:, None, :].to_broadcast([64, NCH, C]), ALU.mult))
                    V.need(m)
                    flow(tt(ZU[d], wide(eye2[:, :], NCH), TU[d], ALU.subtract))
                    dve.wait_ge(nl_ps, i * 2 + d + 1)
                    tt(NL[d], chunks(Q[0][:, :]), wide(score_mask[:, 1 - d, 0:C], NCH), ALU.mult).then_inc(nl_sb, 1)
                    dve.wait_ge(nl_sb, i * 2 + d + 1)
                    flow(tt(TU[d], NL[d], wide(off_mask[:, 1 - d, 0, :], NCH), ALU.mult))
                    tt(ZL[d], wide(eye2[:, :], NCH), TU[d], ALU.subtract).then_inc(z_rdy[d], 1)
                if more >= 1:
                    outer(i + 1, 1, par_v)
                for lv in range(LEVELS - 1):
                    for d in range(2):
                        dve.wait_ge(tu_ps[d], i * (LEVELS - 1) + lv + 1)
                        tt(TU[d], chunks(Q[2 * d][:, :]), wide(off_mask[:, d, lv + 1, :], NCH), ALU.mult).then_inc(tu_sb[d], 1)
                    if more >= 1:
                        inputs(i + 1, 2 * lv)
                    for d in range(2):
                        dve.wait_ge(zz_ps[d], i * (LEVELS - 1) + lv + 1)
                        last = tt(ZU[d], ZU[d], chunks(Q[2 * d + 1][:, :]), ALU.subtract)
                        if lv < LEVELS - 2:
                            V.tick(last)
                            last = tt(ZL[d], ZL[d], chunks(Q[2 * d][:, :]), ALU.subtract)
                        last.then_inc(z_rdy[d], 1)
                    if more >= 1:
                        inputs(i + 1, 2 * lv + 1)
                for s in range(NCH):
                    dve.wait_ge(rhs_ps[0], i * NCH + s + 1)
                    nc.vector.tensor_copy(rhs_sb[0], CH[0][:, 0:C]).then_inc(rhs_cp[0], 1)
                    if s == 1:
                        dve.wait_ge(mod_sum, i + 10)
                        mod_out(Q[3][:, 0:8], i * 4 + 32).then_inc(mod_rdy, 1)
                    nxt = chunk_at(1, min(s + 1, NCH - 1))
                    decay = [wc[:, 0, chunk_at(0, s):chunk_at(0, s) + 1], wc[:, 1, nxt:nxt + 1]]
                    if 0 < s < NCH - 1:
                        for d in range(2):
                            dve.wait_ge(st_sb[d], i * 7 + s)
                            w = V.tick(ts(STw[d], ST[d][s % 2], decay[d], None, ALU.mult))
                    for d in range(2):
                        dve.wait_ge(u_ps[d], i * NCH + s + 1)
                        ts(VU[d][64:128, chunk_at(d, s), 0], CH[d][64:128, C:2 * C], -1.0, None, ALU.mult).then_inc(u_sb[d][0], 1)
                    if s < NCH - 1:
                        for d in range(2):
                            dve.wait_ge(st_ps[d], i * 7 + s + 1)
                            new, psum = ST[d][(s + 1) % 2], CH[d][:, 2 * C:3 * C]
                            if s == 0:
                                last = ts(new, psum, decay[d], None, ALU.mult)
                            else:
                                V.need(w)
                                last = stt(new, psum, decay[d], STw[d], ALU.mult, ALU.add)
                            last.then_inc(st_sb[d], 1)
                    if more >= 1 and s == NCH - 2:
                        outer(i + 1, 2, par_v)
                for d in range(2):
                    dve.wait_ge(y_sb[d], i * 4 + 4)
                tt(ra, yd[0], yd[1], ALU.add).then_inc(ysum_rdy, 1)
                if more == 2:
                    fetch(par_vk, i + 2)
                    outer(i + 2, 0, par_vk)
                dve.wait_ge(mean_ps, i + 1)
                stt(ra, Q[0][:, 0:T], -1.0 / HEAD, ra, ALU.mult, ALU.add).then_inc(dev_rdy, 1)
                dve.wait_ge(rs_rdy, i + 2)
                flow(tt(ra, ra, rb, ALU.mult))
                flow(ts(ra, ra, par_vo[:, PLG:PLG + 1], par_vo[:, PLB:PLB + 1], ALU.mult, ALU.add))
                dve.wait_ge(bonv_rdy, i + 1)
                flow(tt(ra, ra, bon, ALU.add))
                dve.wait_ge(g_rdy, i + 1)
                dve.wait_ge(yr_free, i + 1)
                tt(yr_out, ra, gT, ALU.mult).then_inc(pair_done, 1)

            fetch(par_v, 0)
            outer(0, 0, par_v)
            outer(0, 1, par_v)
            dve.wait_ge(pb_free[0], item_count(0, K_))
            dve.wait_ge(pb_free[1], item_count(0, R_))
            for n in range(10):
                inputs(0, n)
            outer(0, 2, par_v)
            fetch(par_vk, 1)
            outer(1, 0, par_vk)
            V.straight()
            with dve.Fori(0, PAIRS - 2) as i:
                V.enter(i, BODY_STEPS)
                body(i, 2)
            V.leave(PAIRS - 2)
            body(PAIRS - 2, 1)
            body(PAIRS - 1, 0)

            dve.wait_ge(pair_done, PAIRS + 1)
            dve.wait_ge(hh_rdy, 1)
            tt(h_lo_r, hT[:, :, 0:T], as_f32(h_hi_r[:, :, :]), ALU.subtract).then_inc(hl_rdy, 1)

            def low(phase, i, r):
                if phase == "merge" and r % 4 == 0:
                    n = i + r // 4
                    dve.wait_ge(loaded[0], n * 16 + 16 * (loads_before(phase)[0] + 1))
                    dve.wait_ge(used[2], n + (loads_before(phase)[2] + 1))
                    flow(nc.vector.tensor_copy(w_hi_r[:, 0, REG // 2:], ring[:, 0, REG // 2:]))
                dve.wait_ge(hi_rdy, split_count(phase, i, r))
                r, n = r % 4, width(phase, r % 4) - (POOL_COLS if phase == "up" else 0)
                tt(w_lo_r[:, r, 0:n], ring[:, r, 0:n], as_f32(w_hi_r[:, r % 2, 0:n]), ALU.subtract).then_inc(lo_rdy, 1)

            def lows(phase, i, r, n, then):
                if isinstance(i, int) and i == n - 1 and r >= 2:
                    if then:
                        low(then, 0, r - 2)
                else:
                    low(phase, i, r + 2)

            low("gu", 0, 0)
            low("gu", 0, 1)
            dve.wait_ge(gv_act, 4)
            for n in range(2):
                for h in range(2):
                    m = V.tick(nc.vector.bn_stats(bn[:, n, h, :], vg[:, n, h * 512:(h + 1) * 512]))
            V.need(m)
            for n in range(2):
                nc.vector.bn_aggr(mv[:, n, :], bn[:, n].rearrange("p a b -> p (a b)")).then_inc(gv_st, 1)
            dve.wait_ge(gv_rs, 1)
            for n in range(2):
                flow(ts(vg[:, n], vg[:, n], mv[:, n, 0:1], vrs[:, n:n + 1], ALU.subtract, ALU.mult))
            dve.wait_ge(late_ld, 48)
            for i in range(2):
                for r in range(4):
                    to = slice((i * 4 + r) * P, (i * 4 + r + 1) * P)
                    dve.wait_ge(gs_ps, i * 4 + r + 1)
                    flow(tt(vcur[r % 2], vg[:, :, to], vrow[:, 0, to][:, None, :].to_broadcast([P, 2, P]), ALU.mult))
                    tt(vcur[r % 2], vcur[r % 2], vrow[:, 1, to][:, None, :].to_broadcast([P, 2, P]),
                       ALU.add).then_inc(vc_rdy, 1)
                    lows("gu", i, r, 2, "merge")
                    dve.wait_ge(gs_ps, i * 4 + r + 3)
                    flow(tt(ssp[r % 2].rearrange("p (a b) -> p a b", a=2),
                            CH[r % 2][:, 0:T].rearrange("p (a b) -> p a b", a=2),
                            bsp[:, i * 4 + r:i * 4 + r + 1, :].to_broadcast([P, 2, P]), ALU.add))
                    dve.wait_ge(gu_act, i * 4 + r + 1)
                    tt(yg_lo[:, i * 4 + r, :], ssp[r % 2], ug[r % 2], ALU.mult).then_inc(yg_rdy, 1)
                    if (i, r) == (0, 1):
                        dve.wait_ge(yrh_rdy, 1)
                        tt(yr_lo_r[:, :, :], yr, as_f32(yr_hi_r[:, :, :]), ALU.subtract).then_inc(yrl_rdy, 1)

            def merge_four(i):
                for r in range(4):
                    lows("merge", i, r, KT, "out")
                    if r >= 2:
                        o, g = ((mta, sga), (mtb, sgb))[r - 2]
                        product(r, "merge", 0, i, 1)
                        dve.wait_ge(me_act, i * 2 + r + 1)
                        m = V.tick(tt(o, g, Q[r][:, 0:T], ALU.mult))
                V.need(m)
                tt(m_lo[:, bass.ds(i, 1), :].rearrange("p a b -> p (a b)"), mta, mtb, ALU.add).then_inc(m_rdy, 1)

            V.straight()
            with dve.Fori(0, KT - 1) as i:
                V.enter(i, 3)
                merge_four(i)
            V.leave(KT - 1)
            merge_four(KT - 1)
            with dve.Fori(0, 3) as i:
                for r in range(4):
                    low("out", i, r + 2)
            for r in range(4):
                lows("out", 3, r, 4, "up")

            def normed_residual(n, gain, at, out, done):
                flow(tt(gcol[:, :, 0], modT[:, at:at + KT, 0], gains[:, gain, :], ALU.mult))
                dve.wait_ge(rstd_rdy, n)
                m = [0] * KT
                for kt in range(KT + 1):
                    if kt < KT:
                        m[kt] = V.tick(stt(mixT[:, kt, :], mixT[:, kt, :], gcol[:, kt, 0:1], rstd[:, 0:T], ALU.mult, ALU.mult))
                    if kt:
                        V.need(m[kt - 1])
                        tt(out[:, kt - 1, :], xT[:, kt - 1, :], mixT[:, kt - 1, :], ALU.add).then_inc(done, 1)

            dve.wait_ge(xr_ld, 16)
            stt(gcol[:, :, 1], modT[:, 4 * KT:5 * KT, 0], 1.0, gains[:, 2, :], ALU.add, ALU.mult)
            normed_residual(2, 1, 2 * KT, xT, x1_rdy)
            dve.wait_ge(rstd_rdy, 3)
            for kt in range(KT + 2):
                if kt < KT:
                    stt(h2_lo[:, kt, :], xT[:, kt, :], gcol[:, kt, 1:2], rstd[:, 0:T], ALU.mult, ALU.mult).then_inc(h2_raw, 1)
                if kt >= 2:
                    dve.wait_ge(h2h_rdy, kt - 1)
                    stt(h2_lo_r[:, kt - 2], h2_lo[:, kt - 2], modT[:, 3 * KT + kt - 2, 0:1], as_f32(h2_hi_r[:, kt - 2]),
                        ALU.add, ALU.subtract).then_inc(h_rdy, 1)

            def grid(v):
                return v.rearrange("p (r c) -> p r c", r=ROWS)

            side = [(a, b) for a in (-1, 0, 1) for b in (-1, 0, 1) if (a, b) != (0, 0)]

            def taps(i, j, half, prev):
                if half == 0:
                    dve.wait_ge(up_mid, i * 4 + 2 * j + 2)
                for n in range(4 * half, 4 * half + 4):
                    a, b = side[n]
                    for q in range(2):
                        r = 2 * j + q
                        orow, irow = slice(max(0, -a), ROWS - max(0, a)), slice(max(0, a), ROWS - max(0, -a))
                        ocol, icol = slice(max(0, -b), GRID - max(0, b)), slice(max(0, b), GRID - max(0, -b))
                        if n:
                            V.need(prev[q])
                        w = 3 * (a + 1) + b + 1
                        last = stt(grid(cv[r])[:, orow, ocol], grid(four[r][:, 0:T])[:, irow, icol],
                                   convw_v[:, r, w:w + 1], grid(cv[r])[:, orow, ocol], ALU.mult, ALU.add)
                        if (n, q) != (7, 1):
                            prev[q] = V.tick(last)
                if half:
                    last.then_inc(up_cv, 1)
                return prev

            def gated(i, j):
                dve.wait_ge(up_act, i * 2 + j + 1)
                tt(ff_lo[:, bass.ds(i * 2 + j, 1), :].rearrange("p a b -> p (a b)"), sil[j], cv[2 * j + 1],
                   ALU.mult).then_inc(ff_rdy, 1)

            def up_four(i, carry):
                if carry is not None:
                    dve.wait_ge(dve_step, V.base)
                    taps(i - 1, 1, 1, carry)
                lows("up", i, 0, FT // 2, "down")
                if carry is not None:
                    dve.wait_ge(up_cv, i * 2 + 2)
                V.need(V.tick(nc.vector.tensor_copy(convw_v, conv_all[:, bass.ds(i, 1)].rearrange("p a m n -> p (a m) n"))))
                prev = taps(i, 0, 0, [0, 0])
                lows("up", i, 1, FT // 2, "down")
                if carry is not None:
                    gated(i - 1, 1)
                taps(i, 0, 1, prev)
                lows("up", i, 2, FT // 2, "down")
                prev = taps(i, 1, 0, [0, 0])
                lows("up", i, 3, FT // 2, "down")
                gated(i, 0)
                return prev

            dve.wait_ge(cw_ld, 16)
            V.straight()
            up_four(0, None)
            V.straight()
            with dve.Fori(1, FT // 2 - 1) as i:
                V.enter(i - 1, 31)
                up_four(i, [0, 0])
            V.leave(FT // 2 - 2)
            prev = up_four(FT // 2 - 1, [0, 0])
            taps(FT // 2 - 1, 1, 1, prev)
            gated(FT // 2 - 1, 1)

            def low_down(i, k):
                dve.wait_ge(hi_rdy, i * 8 + (SPLIT["down"] + k + 3))
                r, n = (k + 2) % 4, FT // 4 * P
                tt(w_lo_r[:, r, 0:n], ring[:, r, 0:n], as_f32(w_hi_r[:, r % 2, 0:n]), ALU.subtract).then_inc(lo_rdy, 1)

            with dve.Fori(0, KT // 2 - 1) as i:
                for k in range(8):
                    low_down(i, k)
            for k in range(6):
                low_down(KT // 2 - 1, k)
            normed_residual(4, 3, 5 * KT, x_out, out_rdy)

        @block.gpsimd
        def _(pool):
            with pool.Fori(0, PAIRS) as i:
                pool.wait_ge(pair_done, i + 1)
                pool.wait_ge(x_rdy, i * 2 + 2)
                pool.sem_inc(seen, 1)
                for d in range(2):
                    nc.gpsimd.tensor_copy(KR[d], KRn[d]).then_inc(kr_cp, 1)
                pool.wait_ge(vt_sb, i + 1)
                pool.wait_ge(kr_cp, i * 2 + 4)
                pool.sem_inc(seen, 1)
                nc.gpsimd.tensor_copy(VU[1][0:64, :, 0], VU[0][0:64, :, 0]).then_inc(vt_all, 1)
                nc.gpsimd.tensor_copy(VU[1][64:128, :, 1], VU[0][64:128, :, 1]).then_inc(vt_all, 1)
                pool.wait_ge(pair_done, i + 2)
                pool.sem_inc(seen, 1)
                pool.dma_start(io["yr"][:, bass.ds(i, 1), :].rearrange("p a b -> p (a b)"), yr_out).then_inc(yr_stored, 16)
                pool.wait_ge(yr_stored, i * 16 + 16)
                pool.sem_inc(yr_free, 1)

            def split(ready, count, lo, hi_r, lo_r, i, n):
                lo, hi_r, lo_r = (one(v, i) for v in (lo, hi_r, lo_r))
                pool.wait_ge(ready, count)
                pool.sem_inc(seen, 1)
                nc.gpsimd.tensor_copy(hi_r, lo).then_inc(pool_hi, 1)
                pool.wait_ge(pool_hi, n)
                pool.sem_inc(seen, 1)
                nc.gpsimd.tensor_tensor(lo_r, lo, as_f32(hi_r), ALU.subtract).then_inc(pool_lo, 1)

            def one(v, i):
                return v[:, bass.ds(i, 1), :].rearrange("p a b -> p (a b)")

            with pool.Fori(0, GG) as i:
                split(yg_rdy, i + 3, yg_lo, yg_hi_r, yg_lo_r, i, i + 1)
            with pool.Fori(0, KT) as i:
                split(m_rdy, i + 2, m_lo, m_hi_r, m_lo_r, i, i + (GG + 1))

            def up_four(i, first):
                for r in range(4):
                    pool.wait_ge(hi_rdy, split_count("up", i, r))
                    pool.sem_inc(seen, 1)
                    nc.gpsimd.tensor_tensor(w_lo_r[:, r, REG - POOL_COLS:], ring[:, r, REG - POOL_COLS:],
                                            as_f32(w_hi_r[:, r % 2, REG - POOL_COLS:]), ALU.subtract).then_inc(up_lo, 1)
                    if r % 2 and not first:
                        ff_split(i * 2 - 2 + r // 2)

            def ff_split(n):
                split(ff_rdy, n + 3, ff_lo, ff_hi_r, ff_lo_r, n, n + (GG + KT + 1))

            up_four(0, True)
            with pool.Fori(1, FT // 2) as i:
                up_four(i, False)
            ff_split(FT - 2)
            ff_split(FT - 1)


def tiles(w):
    k, n = w.shape
    return w.reshape(k // P, P, n // P, P).transpose(2, 1, 0, 3).reshape(n // P, P, -1)


def columns(v):
    v = v.reshape(v.shape[:-1] + (-1, P))
    return np.moveaxis(v, -1, 0)


def masks():
    s, t = np.arange(C)[:, None], np.arange(C)[None, :]
    two = lambda m: np.concatenate([m, m], axis=0)
    score = np.stack([np.concatenate([two(s < t), two(s <= t)], 1), np.concatenate([two(s > t), two(s >= t)], 1)], 1)
    off = np.zeros((P, 2, LEVELS, C), bool)
    for lv in range(LEVELS):
        b = 1 << lv
        near = (s // (2 * b) == t // (2 * b)) & (s // b != t // b)
        off[:, 0, lv] = two(near & (s < t))
        off[:, 1, lv] = two(near & (s > t))
    scan = np.ones((P, TT), bool)
    scan[:, ::C] = False
    return {"score_mask": score, "off_mask": off, "eye2": two(s == t), "scan_mask": scan,
            "part_sum": np.eye(QUAD)[np.arange(P) % QUAD][:, :2], "ident": np.eye(P), "ones": np.ones((P, P)),
            "blk": np.kron(np.eye(2), np.ones((HEAD, HEAD)))}


def host_layout(a):
    w = a["w_in"][0]
    rw, off = D, 3 * D
    o_g = off + 4 * LORA
    o_u = o_g + 256
    o_ga = o_u + 2 * G
    t = {}
    t["cvec"] = np.stack([columns(a["c"][0]), columns(a["c_ctx"])], -1)
    x = np.concatenate([a["x"][0], a["ctx"][0]], 0)
    t["xT_all"] = x.T.reshape(KT, P, TT).transpose(1, 0, 2)
    t["w_mod"] = a["w_mod"][0].reshape(4, 4, P, NMOD // 4, 4 * P).transpose(3, 0, 2, 1, 4).reshape(NMOD, P, REG)
    t["bmod"] = columns(a["b_mod"][0])
    t["gains"] = np.stack([columns(a[n][0]) for n in ("g_pre1", "g_post1", "g_pre2", "g_post2")], 1)
    rkv = np.stack([tiles(w[:, rw:2 * rw]), tiles(w[:, 0:rw]), tiles(w[:, 2 * rw:3 * rw])], 1)
    t["w_rkv"] = rkv.reshape(3 * PAIRS, P, REG)
    t["w_lora"] = w[:, off:o_g].reshape(KT, P, 4, LORA).transpose(2, 1, 0, 3).reshape(4, P, -1)
    t["w_gate"] = tiles(w[:, o_g:o_u])
    up = np.zeros((PAIRS, P, 6, P), w.dtype)
    for d in range(2):
        up[:, :LORA, d] = a["w_decay_up"][0, d].reshape(LORA, PAIRS, P).transpose(1, 0, 2)
        up[:, :LORA, 2 + d] = a["w_iclr_up"][0, d].reshape(LORA, PAIRS, P).transpose(1, 0, 2)
        up[:, :, 4 + d] = a["w_gate_up"][0, d * P:(d + 1) * P].reshape(P, PAIRS, P).transpose(1, 0, 2)
    t["w_up_lora"] = up
    cv = a["conv_rwkv"][0]
    cl = np.zeros((P, 6, 3), w.dtype)
    for n in range(4):
        cl[:LORA, n] = cv[:, off + n * LORA:off + (n + 1) * LORA].T
    for n in range(2):
        cl[:, 4 + n] = cv[:, o_g + n * P:o_g + (n + 1) * P].T
    t["conv_lora"] = cl
    par = [columns(cv[k, o:o + rw]) for o in (rw, 0, 2 * rw) for k in range(3)]
    par += [columns(a[n][0, d]) for n in ("w0", "a0") for d in range(2)]
    par += [columns(a[n][0].reshape(-1)) for n in ("k_k", "k_a", "r_k", "lnx_g", "lnx_b")]
    t["params"] = np.stack(par, -1)
    t["w_u"] = tiles(w[:, o_u:o_u + G])
    t["w_v"] = w[:, o_u + G:o_ga].reshape(4, 4, P, 2, 512).transpose(3, 0, 2, 1, 4).reshape(8, P, REG)
    t["w_ga"], t["w_gb"] = tiles(w[:, o_ga:o_ga + D]), tiles(w[:, o_ga + D:])
    t["w_pa"], t["w_pb"], t["w_out"] = (tiles(a[n][0]) for n in ("w_proj_a", "w_proj_b", "w_out"))
    t["lnv"] = np.stack([a["ln_v_g"][0], a["ln_v_b"][0]])
    t["b_spatial"] = a["b_spatial"][0]
    t["w_spatial"] = a["w_spatial"][0].transpose(2, 0, 1)
    u = tiles(a["w_up"][0]).reshape(2, FT, P, REG)
    t["w_up"] = u.transpose(1, 0, 2, 3).reshape(2 * FT, P, REG)
    cf = a["conv_ffn"][0].reshape(9, 2, FT // 2, 2, P)
    t["conv_ffn"] = cf.transpose(4, 2, 3, 1, 0).reshape(P, FT // 2, 4, 9)
    dn = a["w_down"][0].reshape(4, FT // 4, P, KT, P)
    t["w_down"] = dn.transpose(3, 0, 2, 1, 4).reshape(4 * KT, P, -1)
    scal = np.zeros((P, 8))
    scal[:, :4] = [RMS_EPS, LN_EPS, LNX_EPS, 0.5 * LN_SHIFT * np.log(2.0)]
    t["scal"] = scal
    t.update(masks())
    return {k: np.ascontiguousarray(v, dtype=np.float32) for k, v in t.items()}


def kernel(**inputs):
    import concourse.bacc as bacc
    from concourse.bass_utils import run_bass_kernel_spmd

    nc = bacc.Bacc("TRN2", target_bir_lowering=False, num_devices=1)
    arrays = host_layout({k: np.asarray(v) for k, v in inputs.items()})
    io = {k: nc.dram_tensor(k + "_dram", v.shape, F32, kind="ExternalInput").ap() for k, v in arrays.items()}
    io["outT"] = nc.dram_tensor("out_dram", (P, KT, T), F32, kind="ExternalOutput").ap()
    io["yr"] = nc.dram_tensor("yr_scratch", (P, KT, T), F32).ap()
    layer_kernel(nc, io)
    r = run_bass_kernel_spmd(nc, [{k + "_dram": v for k, v in arrays.items()}], core_ids=[0])
    out = r.results[0]["out_dram"]
    return out.transpose(1, 0, 2).reshape(D, T).T.reshape(1, T, D)
```
